# Optimizing a Trainium2 kernel written in Bass

```python
import jax, jax.numpy as jnp
from jax import lax
import numpy as np

D_MODEL = 1024
BATCH = 1
SEQ = 256
DEPTH = 2

CHUNK = 64
EPS = 1e-6
HG_HEADS = 4
HG_DK = 128
HG_DV = 128
HG_WIDTH = HG_HEADS * HG_DV
SW_HEADS = 8
KV_HEADS = 2
GROUP = SW_HEADS // KV_HEADS
HEAD_DIM = 64
SW_WIDTH = SW_HEADS * HEAD_DIM
KV_WIDTH = KV_HEADS * HEAD_DIM
WINDOW = 128
W_CHUNKS = WINDOW // CHUNK
IN_WIDTH = 4 * HG_WIDTH + SW_WIDTH + 2 * KV_WIDTH + 2 * D_MODEL
D_FF = 3584
N_EXPERTS = 8
TOP_K = 2
N_DENSE = (DEPTH + 1) // 2
N_MOE = DEPTH // 2
PLE_DIM = 256

kernel_name = "hybrid_hgrn2_swa_moe_trunk"

def rms_norm(x, gain):
    xf = x.astype(jnp.float32)
    y = xf * lax.rsqrt(jnp.mean(xf * xf, axis=-1, keepdims=True) + EPS)
    return (y * gain.astype(jnp.float32)).astype(x.dtype)

def swiglu(h, wg, wu, wd):
    return (jax.nn.silu(h @ wg) * (h @ wu)) @ wd

def hgrn2_mixer(q, f_logit, inp, g, lb, norm_gain):
    B, S, _ = q.shape
    nc = S // CHUNK
    f = lb + (1.0 - lb) * jax.nn.sigmoid(f_logit.astype(jnp.float32))
    logf = jnp.log(f)
    k = 1.0 - f
    qf = jax.nn.silu(q.astype(jnp.float32))

    def to_chunks(t, d):
        return t.reshape(B, nc, CHUNK, HG_HEADS, d).transpose(1, 0, 3, 2, 4)

    tri = jnp.tril(jnp.ones((CHUNK, CHUNK), dtype=bool))

    def step(state, xs):
        qc, kc, ic, lfc = xs
        b = jnp.cumsum(lfc, axis=2)
        b_last = b[:, :, -1:, :]
        o_inter = jnp.einsum('bhtk,bhkv->bhtv', qc * jnp.exp(b), state)
        diff = b[:, :, :, None, :] - b[:, :, None, :, :]
        decay = jnp.exp(jnp.where(tri[:, :, None], diff, -jnp.inf))
        scores = jnp.einsum('bhtk,bhsk,bhtsk->bhts', qc, kc, decay)
        o_intra = jnp.einsum('bhts,bhsv->bhtv', scores, ic)
        new_state = (jnp.exp(b_last[:, :, 0, :])[..., None] * state
                     + jnp.einsum('bhsk,bhsv->bhkv', kc * jnp.exp(b_last - b), ic))
        return new_state, o_inter + o_intra

    init = jnp.zeros((B, HG_HEADS, HG_DK, HG_DV), jnp.float32)
    _, o = lax.scan(step, init, (to_chunks(qf, HG_DK), to_chunks(k, HG_DK),
                                 to_chunks(inp.astype(jnp.float32), HG_DV),
                                 to_chunks(logf, HG_DK)))
    o = o.transpose(1, 0, 3, 2, 4).reshape(B, S, HG_HEADS, HG_DV)
    o = rms_norm(o, norm_gain.reshape(HG_HEADS, HG_DV)).reshape(B, S, HG_WIDTH)
    return (o * jax.nn.silu(g.astype(jnp.float32))).astype(q.dtype)

def swa_mixer(q, k, v, q_gain, k_gain, sinks):
    B, S, _ = q.shape
    nc = S // CHUNK
    scale = HEAD_DIM ** -0.5
    q = rms_norm(q.reshape(B, S, SW_HEADS, HEAD_DIM), q_gain).astype(jnp.float32) * scale
    k = rms_norm(k.reshape(B, S, KV_HEADS, HEAD_DIM), k_gain).astype(jnp.float32)
    v = v.reshape(B, S, KV_HEADS, HEAD_DIM).astype(jnp.float32)
    pad = (W_CHUNKS - 1) * CHUNK

    def band(t):
        tp = jnp.pad(t, ((0, 0), (pad, 0), (0, 0), (0, 0)))
        tp = tp.reshape(B, nc + W_CHUNKS - 1, CHUNK, KV_HEADS, HEAD_DIM)
        return jnp.concatenate([tp[:, j:j + nc] for j in range(W_CHUNKS)], axis=2)

    qb = q.reshape(B, nc, CHUNK, KV_HEADS, GROUP, HEAD_DIM)
    kb, vb = band(k), band(v)
    s = jnp.einsum('bnqhgd,bnkhd->bnhgqk', qb, kb)
    key_chunk = (jnp.arange(nc)[:, None]
                 + (jnp.arange(W_CHUNKS * CHUNK) // CHUNK)[None, :] - (W_CHUNKS - 1))
    valid = key_chunk >= 0
    s = jnp.where(valid[None, :, None, None, None, :], s, -jnp.inf)
    sink = jnp.broadcast_to(
        sinks.astype(jnp.float32).reshape(KV_HEADS, GROUP)[None, None, :, :, None, None],
        s.shape[:-1] + (1,))
    probs = jax.nn.softmax(jnp.concatenate([s, sink], axis=-1), axis=-1)[..., :-1]
    o = jnp.einsum('bnhgqk,bnkhd->bnqhgd', probs, vb)
    return o.reshape(B, S, SW_WIDTH).astype(q.dtype)

def moe_swiglu(h, w_router, wg, wu, wd):
    B, S, D = h.shape
    t = h.reshape(B * S, D)
    logits = (t @ w_router).astype(jnp.float32)
    top_vals, top_idx = lax.top_k(logits, TOP_K)
    w = jax.nn.softmax(top_vals, axis=-1)
    gates = jnp.sum(jax.nn.one_hot(top_idx, N_EXPERTS, dtype=jnp.float32) * w[..., None], axis=1)

    def expert(acc, xs):
        g_e, wg_e, wu_e, wd_e = xs
        return acc + g_e[:, None].astype(t.dtype) * swiglu(t, wg_e, wu_e, wd_e), None

    acc, _ = lax.scan(expert, jnp.zeros_like(t), (gates.T, wg, wu, wd))
    return acc.reshape(B, S, D)

def setup_inputs(seed: int = 0) -> dict:
    key = jax.random.key(seed)
    ks = jax.random.split(key, 24)
    f32 = jnp.float32

    def nrm(k, shape, fan_in):
        return jax.random.normal(k, shape, f32) * fan_in ** -0.5

    def gain(k, shape):
        return 1.0 + 0.02 * jax.random.normal(k, shape, f32)

    return {
        "x": jax.random.normal(ks[0], (BATCH, SEQ, D_MODEL), f32),
        "p": jax.random.normal(ks[1], (DEPTH, BATCH, SEQ, PLE_DIM), f32),
        "lb_logits": jax.random.normal(ks[2], (DEPTH, HG_WIDTH), f32),
        "g_mix": gain(ks[3], (DEPTH, D_MODEL)),
        "w_in": nrm(ks[4], (DEPTH, D_MODEL, IN_WIDTH), D_MODEL),
        "q_norm": gain(ks[5], (DEPTH, HEAD_DIM)),
        "k_norm": gain(ks[6], (DEPTH, HEAD_DIM)),
        "sinks": 0.5 * jax.random.normal(ks[7], (DEPTH, SW_HEADS), f32),
        "hgrn_norm": gain(ks[8], (DEPTH, HG_WIDTH)),
        "w_pa": nrm(ks[9], (DEPTH, HG_WIDTH, D_MODEL), HG_WIDTH),
        "w_pb": nrm(ks[10], (DEPTH, SW_WIDTH, D_MODEL), SW_WIDTH),
        "w_o": nrm(ks[11], (DEPTH, D_MODEL, D_MODEL), D_MODEL),
        "g_ffn": gain(ks[12], (DEPTH, D_MODEL)),
        "w_dense_gate": nrm(ks[13], (N_DENSE, D_MODEL, D_FF), D_MODEL),
        "w_dense_up": nrm(ks[14], (N_DENSE, D_MODEL, D_FF), D_MODEL),
        "w_dense_down": nrm(ks[15], (N_DENSE, D_FF, D_MODEL), D_FF),
        "w_router": nrm(ks[16], (N_MOE, D_MODEL, N_EXPERTS), D_MODEL),
        "w_moe_gate": nrm(ks[17], (N_MOE, N_EXPERTS, D_MODEL, D_FF), D_MODEL),
        "w_moe_up": nrm(ks[18], (N_MOE, N_EXPERTS, D_MODEL, D_FF), D_MODEL),
        "w_moe_down": nrm(ks[19], (N_MOE, N_EXPERTS, D_FF, D_MODEL), D_FF),
        "g_ple": gain(ks[20], (DEPTH, D_MODEL)),
        "w_ple_gate": nrm(ks[21], (DEPTH, D_MODEL, D_MODEL), D_MODEL),
        "w_ple_up": nrm(ks[22], (DEPTH, PLE_DIM, D_MODEL), PLE_DIM),
    }

def reference(x, p, lb_logits, g_mix, w_in, q_norm, k_norm, sinks, hgrn_norm,
              w_pa, w_pb, w_o, g_ffn, w_dense_gate, w_dense_up, w_dense_down,
              w_router, w_moe_gate, w_moe_up, w_moe_down, g_ple, w_ple_gate, w_ple_up):
    lb_soft = jax.nn.softmax(lb_logits.astype(jnp.float32), axis=0)
    lb_all = jnp.cumsum(lb_soft, axis=0) - lb_soft[0]
    sizes = [HG_WIDTH] * 4 + [SW_WIDTH, KV_WIDTH, KV_WIDTH, D_MODEL, D_MODEL]
    split_points = np.cumsum(sizes)[:-1].tolist()

    for i in range(DEPTH):
        h = rms_norm(x, g_mix[i])
        proj = h @ w_in[i]
        qa, fa, ia, ga, qb, kb, vb, gate_a, gate_b = jnp.split(proj, split_points, axis=-1)
        ya = hgrn2_mixer(qa, fa, ia, ga, lb_all[i], hgrn_norm[i])
        yb = swa_mixer(qb, kb, vb, q_norm[i], k_norm[i], sinks[i])
        merged = (jax.nn.sigmoid(gate_a) * (ya @ w_pa[i])
                  + jax.nn.sigmoid(gate_b) * (yb @ w_pb[i]))
        x = x + merged @ w_o[i]

        h2 = rms_norm(x, g_ffn[i])
        if i % 2 == 0:
            j = i // 2
            x = x + swiglu(h2, w_dense_gate[j], w_dense_up[j], w_dense_down[j])
        else:
            j = i // 2
            x = x + moe_swiglu(h2, w_router[j], w_moe_gate[j], w_moe_up[j], w_moe_down[j])

        gate_p = jax.nn.sigmoid(rms_norm(x, g_ple[i]) @ w_ple_gate[i])
        x = x + gate_p * (p[i].astype(x.dtype) @ w_ple_up[i])
    return x


_drawn_inputs = setup_inputs


def setup_inputs(seed=0):
    import zlib

    import numpy as np

    out = dict(_drawn_inputs(seed))
    spreads = {}
    factors = {'q_norm': 6.389, 'k_norm': 3.697, 'sinks': 8.0, 'g_ple': 8.0}
    for name, (base, spread) in spreads.items():
        noise = np.random.default_rng([zlib.crc32(name.encode()), seed]).standard_normal(out[name].shape)
        drawn = base * np.exp(spread * noise) if base else spread * noise
        out[name] = __import__('jax').numpy.asarray(drawn.astype(out[name].dtype))
    for name, factor in factors.items():
        out[name] = (out[name] * factor).astype(out[name].dtype)
    return out
```

```python
from contextlib import ExitStack

import concourse.bass as bass
from concourse import mybir

ALU = mybir.AluOpType
ACT = mybir.ActivationFunctionType
F32 = mybir.dt.float32
I32 = mybir.dt.int32
U8 = mybir.dt.uint8
AX_X = mybir.AxisListType.X

P = 128
BANK = 512
EPS = 1e-6
CHUNK = 64
HEADS = 4
SW_HEADS = 8
KV_HEADS = 2
HEAD_DIM = 64
TOP_K = 2
SLOTS = 14
UNIT = 2048
MASKED = -1e30
F_LEAST = 1e-19


def build_trunk(nc, x_in, p_in, lb_logits, g_mix, w_in, q_norm, k_norm, sinks, hgrn_norm, w_pa, w_pb, w_o,
                g_ffn, w_dense_gate, w_dense_up, w_dense_down, w_router, w_moe_gate, w_moe_up, w_moe_down,
                g_ple, w_ple_gate, w_ple_up, out):
    _, SEQ, D = x_in.shape
    DEPTH = p_in.shape[0]
    PLE = p_in.shape[3]
    IN = w_in.shape[2]
    D_FF = w_dense_gate.shape[2]
    EXPERTS = w_moe_gate.shape[1]
    TILES = SEQ // P
    KD = D // P
    HW = HEADS * P
    SW = SW_HEADS * HEAD_DIM
    KV = KV_HEADS * HEAD_DIM
    STEPS = D_FF // BANK
    EXTRA = 3
    ITEMS = EXPERTS + EXTRA + 1
    assert DEPTH == 2 and TILES == 2 and D == 1024 and HW == BANK and SW == BANK and D_FF % BANK == 0
    assert PLE == 2 * P and TOP_K * SEQ < (EXTRA + 1) * (P + 1) and KV * 2 == 256
    assert IN == 4 * HW + SW + 2 * KV + 2 * D

    def rows(w, k0, n):
        return w[k0 * P:(k0 + n) * P, :].rearrange("(k p) n -> p k n", p=P)

    IN_COLUMNS = [(0, BANK), (3 * HW, BANK), (HW, BANK), (2 * HW, BANK), (4 * HW, BANK), (4 * HW + SW, 2 * KV)]
    IN_COLUMNS += [(4 * HW + SW + 2 * KV + c * BANK, BANK) for c in range(2 * D // BANK)]
    OUTS = len(IN_COLUMNS) * TILES
    MIX_OUTS = 6 * TILES
    PER_STEP = 2 * KD * BANK // UNIT + BANK // P * D // UNIT
    G_UNITS = KD * BANK // UNIT
    D_UNITS = BANK // P * D // UNIT
    PER_ITEM = STEPS * PER_STEP
    assert PER_ITEM % SLOTS == 0

    def in_units(layer):
        units = []
        for c0, width in IN_COLUMNS:
            per = UNIT // width
            for k0 in range(0, KD, per):
                units.append(rows(w_in[layer], k0, per)[:, :, c0:c0 + width])
        return units

    def wide_units(w):
        return [rows(w, k0, UNIT // D) for k0 in range(0, w.shape[0] // P, UNIT // D)]

    MIX_UNITS = [in_units(i) + wide_units(w_pa[i]) + wide_units(w_pb[i]) + wide_units(w_o[i]) for i in range(DEPTH)]
    PLE_UNITS = [wide_units(w_ple_gate[i]) + wide_units(w_ple_up[i]) for i in range(DEPTH)]
    IN_UNITS = len(in_units(0))
    COLUMN_UNIT = [sum(KD * width // UNIT for _, width in IN_COLUMNS[:c]) for c in range(len(IN_COLUMNS) + 1)]
    GATE_UNITS = D * D // P // UNIT
    PA_AT, PB_AT = IN_UNITS, IN_UNITS + 2
    WO_AT = IN_UNITS + 4

    def column_units(w, step):
        return [rows(w, k0, UNIT // BANK)[:, :, step * BANK:(step + 1) * BANK]
                for k0 in range(0, KD, UNIT // BANK)]

    def down_units(w, step):
        kt = BANK // P
        return [rows(w, step * kt + k0, UNIT // D) for k0 in range(0, kt, UNIT // D)]

    DENSE_UNITS = []
    for s in range(STEPS):
        DENSE_UNITS += column_units(w_dense_gate[0], s) + column_units(w_dense_up[0], s) + down_units(w_dense_down[0], s)
    MIX0 = 0
    DENSE0 = len(MIX_UNITS[0])
    PLE0 = DENSE0 + len(DENSE_UNITS)
    MIX1 = PLE0 + len(PLE_UNITS[0])
    MOE = MIX1 + len(MIX_UNITS[1])
    LAYER0 = [MIX0, MIX1]
    LEVEL_HALF = [64, 32, 16, 8, 4, 2, 1, 128]
    LEVEL_COUNT = len(LEVEL_HALF)

    def item_gate(s):
        return 0 if s == 0 else 2 * G_UNITS + (s - 1) * PER_STEP

    def item_up(s):
        return item_gate(s) + G_UNITS

    def item_down(s):
        return item_up(s + 1) + G_UNITS if s + 1 < STEPS else PER_ITEM - D_UNITS

    with ExitStack() as ctx:
        def sb(name, shape, dt=F32):
            return ctx.enter_context(nc.sbuf_tensor(name, shape, dt))

        def sem(name):
            return ctx.enter_context(nc.semaphore(name))

        ring = sb("ring", [P, SLOTS, UNIT])
        x = sb("x", [P, TILES, D])
        normed = sb("normed", [P, TILES, D])
        hT = sb("hT", [P, KD, SEQ])
        arena = sb("arena", [P, 4096 + 3584 + 5120 + 1536 + 1280])
        wide = arena[:, 0:4096]
        q_tok = wide[:, 0:1024].rearrange("p (t n) -> p t n", t=TILES)
        f_tok = wide[:, 1024:2048].rearrange("p (t n) -> p t n", t=TILES)
        branch = wide.rearrange("p (t n) -> p t n", t=TILES)
        act = [wide[:, n * BANK:(n + 1) * BANK] for n in range(2)]
        actT = [wide[:, 1024 + n * BANK:1024 + (n + 1) * BANK].rearrange("p (k t) -> p k t", k=4) for n in range(2)]
        gatheredT = wide[:, 2048:3072].rearrange("p (k t) -> p k t", k=KD)
        y_item = wide[:, 3072:4096]
        toks = arena[:, 4096:7680]
        silu_g = toks[:, 0:1024].rearrange("p (t n) -> p t n", t=TILES)
        i_tok = toks[:, 1024:2048].rearrange("p (t n) -> p t n", t=TILES)
        qkv = toks[:, 2048:3584].rearrange("p (t n) -> p t n", t=TILES)
        ple_gate = toks[:, 0:2048].rearrange("p (t n) -> p t n", t=TILES)
        deep = arena[:, 7680:12800]
        qT, kT, bT = (deep[:, n * 1024:(n + 1) * 1024] for n in range(3))
        level_tile = [deep[:, (3 + n) * 1024:(4 + n) * 1024] for n in range(2)]
        yaT = qT.rearrange("p (h t) -> p h t", h=HEADS)
        sw_s = deep[:, 1024:3072]
        sw_pT = deep[:, 3072:5120]
        score_mem = arena[:, 12800:14336]
        sc_tile = score_mem[:, 0:1024].rearrange("p (n t) -> p n t", t=P)
        sc_cross = score_mem[:, 1024:1536].rearrange("p (n t) -> p n t", t=P)
        sw_sq = score_mem[:, 0:TILES * (SW + KV)].rearrange("p (t n) -> p t n", t=TILES)
        ybT = score_mem[:, 0:1024].rearrange("p (h t) -> p h t", h=HEADS)
        pT = score_mem[:, 0:PLE * TILES].rearrange("p (k t) -> p k t", k=PLE // P)
        qk_mem = arena[:, 14336:15616]
        qbT = qk_mem[:, 0:1024].rearrange("p (h t) -> p h t", h=HEADS)
        kbT = qk_mem[:, 1024:1280]
        pick = qk_mem[:, 0:256].rearrange("p (t s) -> p t s", t=TILES)
        pick_gate = qk_mem[:, 256:512].rearrange("p (t s) -> p t s", t=TILES)
        spread = qk_mem[:, 512:768]
        p_tok = sb("p_tok", [P, TILES, PLE])

        ident = sb("ident", [P, P])
        later = sb("later", [P, P])
        ones = sb("ones", [P, P])
        column = sb("column", [P, P])
        LEVELS = [64, 32, 16, 8, 4, 2, 1]
        masks = sb("masks", [P, 1 + len(LEVELS), P], U8)
        int_a = toks[:, 0:P].bitcast(I32)
        int_b = toks[:, P:2 * P].bitcast(I32)
        sw_mask = [sb("sw_mask0", [P, P]), sb("sw_mask1", [P, 2 * P])]
        before = sb("before", [P, EXPERTS, EXPERTS])
        param_rows = sb("param_rows", [P, P])
        params = sb("params", [P, P])
        lb = sb("lb", [P, DEPTH, HEADS])
        lb_rest = sb("lb_rest", [P, DEPTH, HEADS])
        lb_tmp = sb("lb_tmp", [P, 6, HEADS])
        sink_row = sb("sink_row", [P, DEPTH, SW_HEADS])
        router = sb("router", [P, KD, EXPERTS])
        minus_half = sb("minus_half", [P, 32])
        sumsq = sb("sumsq", [P, TILES])
        meansq = sb("meansq", [P, TILES])
        rstd = sb("rstd", [P, TILES])
        head_sumsq = sb("head_sumsq", [P, 20])
        head_meansq = sb("head_meansq", [P, 20])
        head_rstd = sb("head_rstd", [P, 20])
        sw_max = sb("sw_max", [P, SW_HEADS])
        sw_negmax = sb("sw_negmax", [P, SW_HEADS])
        sw_sink = sb("sw_sink", [P, SW_HEADS])
        sw_sum = sb("sw_sum", [P, SW_HEADS])
        sw_total = sb("sw_total", [P, SW_HEADS])
        sw_recip = sb("sw_recip", [P, SW_HEADS])
        logits = sb("logits", [P, TILES, EXPERTS])
        pairs_mem = score_mem[:, 0:2 * TILES * EXPERTS * EXPERTS].rearrange("p (n t e f) -> p n t e f", n=2, t=TILES, e=EXPERTS)
        pair_a, pair_b = pairs_mem[:, 0], pairs_mem[:, 1]
        rank = sb("rank", [P, TILES, EXPERTS])
        chosen = sb("chosen", [P, TILES, EXPERTS])
        gate_w = sb("gate_w", [P, TILES, EXPERTS])
        top = sb("top", [P, TILES])
        place = sb("place", [P, TILES, EXPERTS])
        over = sb("over", [P, EXPERTS])
        over_before = sb("over_before", [P, EXPERTS])
        extra_of = sb("extra_of", [P, EXTRA, EXPERTS])
        item_place = sb("item_place", [P, TILES, ITEMS])
        item_gate_w = sb("item_gate_w", [P, TILES, ITEMS])
        item_expert = sb("item_expert", [P, ITEMS])
        item_expert_i = sb("item_expert_i", [P, ITEMS], I32)
        n_items = sb("n_items", [P, 1])
        n_items_i = sb("n_items_i", [P, 1], I32)

        ps = ctx.enter_context(nc.psum_tensor("ps", [P, 8, BANK], F32))
        GATE, UP, TRA, TRB = 4, 5, 6, 7

        def banks(b, n=1):
            return ps[:, b:b + n, :].rearrange("p b n -> p (b n)")

        x_loaded = sem("x_loaded")
        params_loaded = sem("params_loaded")
        p_loaded = sem("p_loaded")
        slot_filled = [sem(f"slot{s}_filled") for s in range(SLOTS)]
        units_used = sem("units_used")
        pool_constants = sem("pool_constants")
        vector_constants = sem("vector_constants")
        params_transposed = sem("params_transposed")
        lb_exps = sem("lb_exps")
        lb_diffs = sem("lb_diffs")
        vector_step = sem("vector_step")
        pool_step = sem("pool_step")
        squares_ready = sem("squares_ready")
        rstd_ready = sem("rstd_ready")
        normed_ready = sem("normed_ready")
        normed_transposed = sem("normed_transposed")
        hT_ready = sem("hT_ready")
        proj_done = sem("proj_done")
        proj_taken = sem("proj_taken")
        f_transposed = sem("f_transposed")
        f_taken = sem("f_taken")
        f_clamped = sem("f_clamped")
        logf_ready = sem("logf_ready")
        q_transposed = sem("q_transposed")
        q_taken = sem("q_taken")
        sw_squares = sem("sw_squares")
        head_sums = sem("head_sums")
        head_rstds = sem("head_rstds")
        qk_normed = sem("qk_normed")
        qk_transposed = sem("qk_transposed")
        qkT_ready = sem("qkT_ready")
        level_exponents = sem("level_exponents")
        level_exps = sem("level_exps")
        level_ready = sem("level_ready")
        level_scores = sem("level_scores")
        level_taken = sem("level_taken")
        hgrn_out = sem("hgrn_out")
        hgrn_squares = sem("hgrn_squares")
        ya_ready = sem("ya_ready")
        ya_transposed = sem("ya_transposed")
        yaT_ready = sem("yaT_ready")
        sw_scores = sem("sw_scores")
        sw_scores_taken = sem("sw_scores_taken")
        sw_max_ready = sem("sw_max_ready")
        sw_probs = sem("sw_probs")
        sw_probs_transposed = sem("sw_probs_transposed")
        sw_pT_ready = sem("sw_pT_ready")
        sw_out = sem("sw_out")
        yb_ready = sem("yb_ready")
        yb_transposed = sem("yb_transposed")
        ybT_ready = sem("ybT_ready")
        branch_ready = sem("branch_ready")
        pa_done = sem("pa_done")
        pb_done = sem("pb_done")
        merged_ready = sem("merged_ready")
        merged_transposed = sem("merged_transposed")
        mergedT_ready = sem("mergedT_ready")
        wo_done = sem("wo_done")
        x_updated = sem("x_updated")
        gate_done = sem("gate_done")
        up_done = sem("up_done")
        silu_done = sem("silu_done")
        act_ready = sem("act_ready")
        act_transposed = sem("act_transposed")
        actT_ready = sem("actT_ready")
        logits_done = sem("logits_done")
        top_ready = sem("top_ready")
        route_exps = sem("route_exps")
        chosen_ready = sem("chosen_ready")
        places_done = sem("places_done")
        routed = sem("routed")
        picks_ready = sem("picks_ready")
        gathered = sem("gathered")
        gatheredT_ready = sem("gatheredT_ready")
        pick_transposed = sem("pick_transposed")
        spread_ready = sem("spread_ready")
        item_silu = sem("item_silu")
        item_act = sem("item_act")
        item_act_transposed = sem("item_act_transposed")
        item_actT = sem("item_actT")
        item_y_taken = sem("item_y_taken")
        item_combined = sem("item_combined")
        item_added = sem("item_added")
        p_transposed = sem("p_transposed")
        pT_ready = sem("pT_ready")
        ple_gate_done = sem("ple_gate_done")
        ple_gate_ready = sem("ple_gate_ready")
        ple_up_done = sem("ple_up_done")
        stored = sem("stored")

        MIX_GAIN, FFN_GAIN, PLE_GAIN = 0, DEPTH * KD, 2 * DEPTH * KD
        HGRN_GAIN = 3 * DEPTH * KD
        LB_AT = HGRN_GAIN + DEPTH * HEADS
        Q_GAIN = LB_AT + DEPTH * HEADS
        K_GAIN = Q_GAIN + DEPTH
        PARAM_ROWS = K_GAIN + DEPTH
        PARAM_DMAS = 3 + 2 + 4 + 2

        block = ctx.enter_context(nc.Block())

        @block.sync
        def _(sp):
            sp.dma_start(x[:, :, :], x_in[0].rearrange("(t p) d -> p t d", p=P)).then_inc(x_loaded, 16)

            def load_unit(n, source, more=0):
                if n >= SLOTS:
                    sp.wait_ge(units_used, n - SLOTS + 1 + more)
                k, width = source.shape[1], source.shape[2]
                dst = ring[:, n % SLOTS, :].rearrange("p (k n) -> p k n", k=k)
                sp.dma_start(dst, source).then_inc(slot_filled[n % SLOTS], 16)

            for n, source in enumerate(MIX_UNITS[0][:2]):
                load_unit(n, source)
            for base, w in ((MIX_GAIN, g_mix), (FFN_GAIN, g_ffn), (PLE_GAIN, g_ple)):
                sp.dma_start(param_rows[base:base + DEPTH * KD, :],
                             w.rearrange("l (k p) -> (l k) p", p=P)).then_inc(params_loaded, 16)
            for base, w in ((HGRN_GAIN, hgrn_norm), (LB_AT, lb_logits)):
                sp.dma_start(param_rows[base:base + DEPTH * HEADS, :],
                             w.rearrange("l (h p) -> (l h) p", p=P)).then_inc(params_loaded, 16)
            for base, w in ((Q_GAIN, q_norm), (K_GAIN, k_norm)):
                for half in range(2):
                    sp.dma_start(param_rows[base:base + DEPTH, half * HEAD_DIM:(half + 1) * HEAD_DIM],
                                 w).then_inc(params_loaded, 16)
            sp.dma_start(sink_row[:, :, :], sinks.unsqueeze(0).to_broadcast([P, DEPTH, SW_HEADS])).then_inc(params_loaded, 16)
            sp.dma_start(router[:, :, :], w_router[0].rearrange("(k p) e -> p k e", p=P)).then_inc(params_loaded, 16)

            def load_p(layer):
                sp.dma_start(p_tok[:, :, :], p_in[layer, 0].rearrange("(t p) d -> p t d", p=P)).then_inc(p_loaded, 16)

            load_p(0)
            for n, source in list(enumerate(MIX_UNITS[0] + DENSE_UNITS + PLE_UNITS[0]))[2:]:
                load_unit(n, source)
            sp.wait_ge(p_transposed, 1)
            load_p(1)
            for n, source in enumerate(MIX_UNITS[1]):
                load_unit(MIX1 + n, source)
            sp.wait_ge(routed, 1)
            count = sp.value_load(n_items_i[0:1, 0:1], min_val=EXPERTS, max_val=EXPERTS + EXTRA)
            with sp.Fori(0, count) as t:
                e = sp.value_load(item_expert_i[0:1, bass.ds(t, 1)], min_val=0, max_val=EXPERTS - 1)

                def expert(w):
                    return w[0, bass.ds(e, 1), :, :].rearrange("e k n -> (e k) n")

                for s in range(STEPS):
                    for i, source in enumerate(column_units(expert(w_moe_gate), s)):
                        load_unit(MOE + item_gate(s) + i, source, t * PER_ITEM)
                    for i, source in enumerate(column_units(expert(w_moe_up), s)):
                        load_unit(MOE + item_up(s) + i, source, t * PER_ITEM)
                    for d in ([s - 1] if s else []) + ([s] if s == STEPS - 1 else []):
                        for i, source in enumerate(down_units(expert(w_moe_down), d)):
                            load_unit(MOE + item_down(d) + i, source, t * PER_ITEM)
            for n, source in enumerate(PLE_UNITS[1]):
                load_unit(MOE + n, source, count * PER_ITEM)
            sp.wait_ge(x_updated, 5)
            sp.dma_start(out[0].rearrange("(t p) d -> p t d", p=P), x[:, :, :]).then_inc(stored, 16)
            sp.wait_ge(stored, 16)

        @block.gpsimd
        def _(pool):
            steps = [0]

            def link(ins):
                steps[0] += 1
                ins.then_inc(pool_step, 1)
                pool.wait_ge(pool_step, steps[0])

            nc.gpsimd.memset(minus_half[:, :], -0.5)
            nc.gpsimd.memset(ones[:, :], 1.0)
            link(nc.gpsimd.memset(before[:, :, :], 1.0))
            nc.gpsimd.affine_select(out=before[:, :, :], in_=before[:, :, :], pattern=[[1, EXPERTS], [-1, EXPERTS]],
                                    compare_op=ALU.is_gt, fill=0.0, base=0, channel_multiplier=0)
            nc.gpsimd.iota(int_a, pattern=[[1, P]], base=0, channel_multiplier=0)
            nc.gpsimd.iota(int_b, pattern=[[0, P]], base=0, channel_multiplier=1).then_inc(pool_constants, 1)

            def norm_rstd(n):
                pool.wait_ge(squares_ready, TILES * (n + 1))
                link(nc.gpsimd.tensor_scalar(meansq[:, :], sumsq[:, :], 1.0 / D, EPS, ALU.mult, ALU.add))
                nc.gpsimd.tensor_tensor(rstd[:, :], meansq[:, :], minus_half[:, 0:TILES], ALU.pow).then_inc(rstd_ready, 1)

            def heads_rstd(n, heads, width):
                pool.wait_ge(head_sums, n + 1)
                link(nc.gpsimd.tensor_scalar(head_meansq[:, 0:heads], head_sumsq[:, 0:heads], 1.0 / width, EPS,
                                             ALU.mult, ALU.add))
                nc.gpsimd.tensor_tensor(head_rstd[:, 0:heads], head_meansq[:, 0:heads], minus_half[:, 0:heads],
                                        ALU.pow).then_inc(head_rstds, 1)

            for layer in range(DEPTH):
                norm_rstd(3 * layer)
                heads_rstd(2 * layer, TILES * (SW_HEADS + KV_HEADS), HEAD_DIM)
                heads_rstd(2 * layer + 1, TILES * HEADS, P)
                norm_rstd(3 * layer + 1)
                norm_rstd(3 * layer + 2)

        @block.scalar
        def _(act_e):
            items = [None]

            def norm_squares(n):
                if n == 0:
                    act_e.wait_ge(x_loaded, 16)
                elif n == 5:
                    act_e.wait_ge(item_added, items[0] * TILES)
                else:
                    act_e.wait_ge(x_updated, n)
                for t in range(TILES):
                    nc.scalar.activation(normed[:, t, :], x[:, t, :], ACT.Square,
                                         accum_out=sumsq[:, t:t + 1]).then_inc(squares_ready, 1)

            def take(layer, o, dst, func):
                c, t = o // TILES, o % TILES
                if t == 0:
                    act_e.wait_ge(proj_done, layer * (OUTS // TILES) + c + 1)
                else:
                    act_e.wait_ge(units_used, LAYER0[layer] + COLUMN_UNIT[c + 1])
                src = banks(o % 4)[:, 0:IN_COLUMNS[c][1]]
                if len(dst.shape) > 2:
                    src = src.rearrange("p (g h d) -> p g h d", g=KV_HEADS, d=HEAD_DIM)
                nc.scalar.activation(dst, src, func).then_inc(proj_taken, 1)

            def mixer(layer):
                for t in range(TILES):
                    take(layer, t, q_tok[:, t, :], ACT.Silu)
                for t in range(TILES):
                    take(layer, 2 + t, silu_g[:, t, :], ACT.Silu)
                for t in range(TILES):
                    take(layer, 4 + t, f_tok[:, t, :], ACT.Sigmoid)
                for t in range(TILES):
                    take(layer, 6 + t, i_tok[:, t, :], ACT.Copy)
                for t in range(TILES):
                    take(layer, 8 + t, qkv[:, t, 0:SW].rearrange("p (h g d) -> p g h d", g=KV_HEADS, d=HEAD_DIM), ACT.Copy)
                for t in range(TILES):
                    take(layer, 10 + t, qkv[:, t, SW:SW + 2 * KV], ACT.Copy)
                act_e.wait_ge(proj_taken, layer * OUTS + MIX_OUTS)
                nc.scalar.activation(sw_sq[:, :, :], qkv[:, :, 0:SW + KV], ACT.Square).then_inc(sw_squares, 1)
                act_e.wait_ge(f_clamped, layer + 1)
                nc.scalar.activation(level_tile[0], level_tile[0], ACT.Ln).then_inc(logf_ready, 1)
                gate_out = [MIX_OUTS]

                def take_gate():
                    o = gate_out[0]
                    c, t = (o - MIX_OUTS) // TILES, o % TILES
                    take(layer, o, branch[:, t, c * BANK:(c + 1) * BANK], ACT.Copy)
                    gate_out[0] += 1

                take_gate()
                take_gate()
                for j in range(LEVEL_COUNT):
                    act_e.wait_ge(level_exponents, layer * LEVEL_COUNT + j + 1)
                    nc.scalar.activation(level_tile[j % 2], level_tile[j % 2], ACT.Exp).then_inc(level_exps, 1)
                    if gate_out[0] < OUTS:
                        take_gate()
                act_e.wait_ge(hgrn_out, TILES * (layer + 1))
                nc.scalar.activation(level_tile[0], banks(0, 2), ACT.Square).then_inc(hgrn_squares, 1)
                for t in range(TILES):
                    keys = (t + 1) * P
                    act_e.wait_ge(sw_max_ready, TILES * layer + t + 1)
                    nc.scalar.activation(sw_sink[:, :], sw_sink[:, :], ACT.Exp)
                    for h in range(SW_HEADS):
                        last = nc.scalar.activation(sw_s[:, h * keys:(h + 1) * keys], sw_s[:, h * keys:(h + 1) * keys],
                                                    ACT.Exp, bias=sw_negmax[:, h:h + 1], accum_out=sw_sum[:, h:h + 1])
                    last.then_inc(sw_probs, 1)
                    act_e.wait_ge(sw_probs_transposed, TILES * layer + t + 1)
                    nc.scalar.activation(sw_pT[:, 0:1024], banks(TRA if t == 0 else GATE, 2), ACT.Copy).then_inc(sw_pT_ready, 1)
                nc.scalar.activation(wide, wide, ACT.Sigmoid).then_inc(branch_ready, 1)

            def dense():
                def copy_actT(b):
                    act_e.wait_ge(act_transposed, b + 1)
                    nc.scalar.activation(actT[b % 2].rearrange("p k t -> p (k t)"), banks(TRA + b % 2),
                                         ACT.Copy).then_inc(actT_ready, 1)

                for b in range(STEPS * TILES):
                    if b % TILES == 0:
                        act_e.wait_ge(gate_done, b // TILES + 1)
                    else:
                        act_e.wait_ge(units_used, DENSE0 + b // TILES * PER_STEP + G_UNITS)
                    nc.scalar.activation(act[b % 2], banks(GATE), ACT.Silu).then_inc(silu_done, 1)
                    if b:
                        copy_actT(b - 1)
                copy_actT(STEPS * TILES - 1)

            def experts():
                act_e.wait_ge(top_ready, 1)
                nc.scalar.activation(gate_w[:, :, :], gate_w[:, :, :], ACT.Exp).then_inc(route_exps, 1)
                act_e.wait_ge(routed, 1)
                items[0] = act_e.value_load(n_items_i[0:1, 0:1], min_val=EXPERTS, max_val=EXPERTS + EXTRA)
                with act_e.Fori(0, items[0]) as t:
                    def copy_actT(s):
                        act_e.wait_ge(item_act_transposed, t * STEPS + s + 1)
                        nc.scalar.activation(actT[s % 2].rearrange("p k t -> p (k t)"), banks(TRA + s % 2),
                                             ACT.Copy).then_inc(item_actT, 1)

                    for s in range(STEPS):
                        act_e.wait_ge(units_used, t * PER_ITEM + MOE + item_gate(s) + G_UNITS)
                        nc.scalar.activation(act[s % 2], banks(GATE), ACT.Silu).then_inc(item_silu, 1)
                        if s:
                            copy_actT(s - 1)
                    copy_actT(STEPS - 1)
                    act_e.wait_ge(units_used, t * PER_ITEM + MOE + PER_ITEM)
                    nc.scalar.activation(y_item, banks(0, 2), ACT.Copy).then_inc(item_y_taken, 1)

            def embedding(layer):
                for t in range(TILES):
                    if t == 0:
                        act_e.wait_ge(ple_gate_done, layer + 1)
                    elif layer == 0:
                        act_e.wait_ge(units_used, PLE0 + GATE_UNITS)
                    else:
                        act_e.wait_ge(units_used, items[0] * PER_ITEM + MOE + GATE_UNITS)
                    nc.scalar.activation(ple_gate[:, t, :], banks(2 * t, 2), ACT.Sigmoid).then_inc(ple_gate_ready, 1)

            norm_squares(0)
            act_e.wait_ge(lb_diffs, 1)
            nc.scalar.activation(lb_tmp[:, 1:3, :], lb_tmp[:, 1:3, :], ACT.Exp).then_inc(lb_exps, 1)
            mixer(0)
            norm_squares(1)
            dense()
            norm_squares(2)
            embedding(0)
            norm_squares(3)
            mixer(1)
            norm_squares(4)
            experts()
            norm_squares(5)
            embedding(1)

        @block.vector
        def _(dve):
            steps = [0]

            def link(ins):
                steps[0] += 1
                ins.then_inc(vector_step, 1)
                dve.wait_ge(vector_step, steps[0])

            def constants():
                nc.vector.memset(sw_mask[0][:, :], 0.0)
                link(nc.vector.memset(sw_mask[1][:, :], 0.0))
                nc.vector.memset(sw_mask[0][0:CHUNK, CHUNK:2 * CHUNK], MASKED)
                nc.vector.memset(sw_mask[1][0:CHUNK, 0:CHUNK], MASKED)
                nc.vector.memset(sw_mask[1][0:CHUNK, 3 * CHUNK:4 * CHUNK], MASKED)
                nc.vector.memset(sw_mask[1][CHUNK:P, 0:2 * CHUNK], MASKED)
                dve.wait_ge(pool_constants, 1)
                nc.vector.tensor_copy(column[:, :], int_a)
                nc.vector.tensor_tensor(ident[:, :], int_a, int_b, ALU.is_equal)
                link(nc.vector.tensor_tensor(later[:, :], int_a, int_b, ALU.is_gt))
                nc.vector.tensor_copy(masks[:, 0, :], ident[:, :]).then_inc(vector_constants, 1)
                link(nc.vector.tensor_tensor(int_a, int_a, int_b, ALU.bitwise_xor))
                link(nc.vector.tensor_copy(params[:, :], int_a))
                link(nc.vector.tensor_tensor(params[:, :], params[:, :], later[:, :], ALU.mult))
                for n, half in enumerate(LEVELS):
                    link(nc.vector.tensor_scalar(hT[:, 0, 0:P], params[:, :], float(half), None, ALU.is_ge))
                    link(nc.vector.scalar_tensor_tensor(masks[:, 1 + n, :], params[:, :], float(2 * half), hT[:, 0, 0:P],
                                                        ALU.is_lt, ALU.mult))
                dve.wait_ge(params_transposed, 1)
                link(nc.vector.tensor_copy(params[:, 0:PARAM_ROWS], banks(0)[:, 0:PARAM_ROWS]))
                l0 = params[:, LB_AT:LB_AT + HEADS]
                l1 = params[:, LB_AT + HEADS:LB_AT + 2 * HEADS]
                link(nc.vector.tensor_tensor(lb_tmp[:, 0, :], l0, l1, ALU.max))
                nc.vector.tensor_tensor(lb_tmp[:, 1, :], l0, lb_tmp[:, 0, :], ALU.subtract)
                nc.vector.tensor_tensor(lb_tmp[:, 2, :], l1, lb_tmp[:, 0, :], ALU.subtract).then_inc(lb_diffs, 1)
                dve.wait_ge(lb_exps, 1)
                link(nc.vector.tensor_tensor(lb_tmp[:, 3, :], lb_tmp[:, 1, :], lb_tmp[:, 2, :], ALU.add))
                link(nc.vector.reciprocal(lb_tmp[:, 3, :], lb_tmp[:, 3, :]))
                link(nc.vector.tensor_tensor(lb_tmp[:, 4, :], lb_tmp[:, 1, :], lb_tmp[:, 3, :], ALU.mult))
                link(nc.vector.tensor_tensor(lb_tmp[:, 5, :], lb_tmp[:, 2, :], lb_tmp[:, 3, :], ALU.mult))
                link(nc.vector.tensor_tensor(lb_tmp[:, 5, :], lb_tmp[:, 4, :], lb_tmp[:, 5, :], ALU.add))
                nc.vector.tensor_tensor(lb[:, 0, :], lb_tmp[:, 4, :], lb_tmp[:, 4, :], ALU.subtract)
                link(nc.vector.tensor_tensor(lb[:, 1, :], lb_tmp[:, 5, :], lb_tmp[:, 4, :], ALU.subtract))
                link(nc.vector.tensor_scalar(lb_rest[:, :, :], lb[:, :, :], -1.0, 1.0, ALU.mult, ALU.add))

            def norm(n, gain):
                dve.wait_ge(rstd_ready, n + 1)
                for t in range(TILES):
                    nc.vector.tensor_scalar(normed[:, t, :], x[:, t, :], rstd[:, t:t + 1], None,
                                            ALU.mult).then_inc(normed_ready, 1)
                for g in range(4):
                    dve.wait_ge(normed_transposed, 4 * n + g + 1)
                    nc.vector.tensor_tensor(hT[:, 2 * g:2 * g + 2, :], banks(4 + g).rearrange("p (k t) -> p k t", k=2),
                                            params[:, gain + 2 * g:gain + 2 * g + 2].unsqueeze(2).to_broadcast([P, 2, SEQ]),
                                            ALU.mult).then_inc(hT_ready, 1)

            def exponents(j):
                half = LEVEL_HALF[j]
                e = level_tile[j % 2]
                if half <= CHUNK:
                    ev = e.rearrange("p (n s j) -> p n s j", s=2, j=half)
                    bv = bT.rearrange("p (n s j) -> p n s j", s=2, j=half)
                    n = bv.shape[1]
                    mid = bv[:, :, 0, half - 1:half].to_broadcast([P, n, half])
                    nc.vector.tensor_tensor(ev[:, :, 0, :], mid, bv[:, :, 0, :], ALU.subtract)
                    if half < CHUNK:
                        last = nc.vector.tensor_tensor(ev[:, :, 1, :], bv[:, :, 1, :], mid, ALU.subtract)
                    else:
                        last = nc.vector.tensor_copy(ev[:, :, 1, :], bv[:, :, 1, :])
                else:
                    ev = e.rearrange("p (h c j) -> p h c j", h=HEADS, c=4)
                    bv = bT.rearrange("p (h c j) -> p h c j", h=HEADS, c=4)

                    def end(c):
                        return bv[:, :, c, CHUNK - 1:CHUNK].to_broadcast([P, HEADS, CHUNK])

                    nc.vector.tensor_tensor(ev[:, :, 0, :], end(0), bv[:, :, 0, :], ALU.subtract)
                    nc.vector.tensor_tensor(ev[:, :, 1, :], end(1), bv[:, :, 1, :], ALU.subtract)
                    nc.vector.tensor_copy(ev[:, :, 2, :], bv[:, :, 2, :])
                    link(nc.vector.tensor_tensor(ev[:, :, 3, :], bv[:, :, 3, :], end(2), ALU.add))
                    last = nc.vector.tensor_tensor(ev[:, :, 0, :], ev[:, :, 0, :], end(1), ALU.add)
                last.then_inc(level_exponents, 1)

            def weigh(layer, j):
                half = LEVEL_HALF[j]
                dve.wait_ge(level_exps, layer * LEVEL_COUNT + j + 1)
                ev, kv, qv = (a.rearrange("p (n s j) -> p n s j", s=2, j=half) for a in (level_tile[j % 2], kT, qT))
                nc.vector.tensor_tensor(ev[:, :, 0, :], ev[:, :, 0, :], kv[:, :, 0, :], ALU.mult)
                nc.vector.tensor_tensor(ev[:, :, 1, :], ev[:, :, 1, :], qv[:, :, 1, :], ALU.mult).then_inc(level_ready, 1)

            def keep_scores(layer, g):
                dve.wait_ge(level_scores, layer * (LEVEL_COUNT + 1) + g + 1)
                if g:
                    dve.wait_ge(level_taken, layer * (LEVEL_COUNT + 1) + g)
                src = banks(GATE if g % 2 == 0 else TRA, 2)
                if g > 0 and LEVEL_HALF[g - 1] > CHUNK:
                    ins = nc.vector.tensor_copy(sc_cross[:, :, :], src[:, 0:HEADS * P].rearrange("p (n t) -> p n t", t=P))
                else:
                    m = 0 if g == 0 else 1 + LEVELS.index(LEVEL_HALF[g - 1])
                    ins = nc.vector.copy_predicated(sc_tile[:, :, :],
                                                    masks[:, m:m + 1, :].to_broadcast([P, HEADS * TILES, P]),
                                                    src.rearrange("p (n t) -> p n t", t=P))
                ins.then_inc(level_taken, 1)

            def mixer(layer):
                lf = level_tile[0]
                dve.wait_ge(f_transposed, layer + 1)
                fv = lf.rearrange("p (h t) -> p h t", h=HEADS)
                for h in range(HEADS):
                    last = nc.vector.tensor_scalar(fv[:, h, :], banks(TRA, 2)[:, h * SEQ:(h + 1) * SEQ],
                                                   lb_rest[:, layer, h:h + 1], lb[:, layer, h:h + 1], ALU.mult, ALU.add)
                last.then_inc(f_taken, 1)
                dve.wait_ge(f_taken, layer + 1)
                link(nc.vector.tensor_scalar(kT, lf, -1.0, 1.0, ALU.mult, ALU.add))
                nc.vector.tensor_scalar_max(lf, lf, F_LEAST).then_inc(f_clamped, 1)
                dve.wait_ge(q_transposed, layer + 1)
                nc.vector.tensor_copy(qT, banks(GATE, 2)).then_inc(q_taken, 1)
                reset = level_tile[1]
                link(nc.vector.memset(reset, 1.0))
                link(nc.vector.memset(reset.rearrange("p (n j) -> p n j", j=CHUNK)[:, :, 0:1], 0.0))
                dve.wait_ge(sw_squares, layer + 1)
                nc.vector.reduce_sum(head_sumsq[:, 0:20].rearrange("p (t h) -> p t h", t=TILES),
                                     sw_sq[:, :, :].rearrange("p t (h d) -> p t h d", d=HEAD_DIM), AX_X).then_inc(head_sums, 1)
                dve.wait_ge(logf_ready, layer + 1)
                link(nc.vector.tensor_tensor_scan(bT, reset, lf, 0.0, ALU.mult, ALU.add))
                exponents(0)
                dve.wait_ge(head_rstds, 2 * layer + 1)
                for t in range(TILES):
                    v = qkv[:, t, 0:SW + KV].rearrange("p (h d) -> p h d", d=HEAD_DIM)
                    nc.vector.tensor_tensor(v, v, head_rstd[:, 10 * t:10 * t + 10].unsqueeze(2).to_broadcast([P, 10, HEAD_DIM]),
                                            ALU.mult).then_inc(qk_normed, 1)
                link(nc.vector.memset(sc_tile[:, :, :], 0.0))
                exponents(1)
                dve.wait_ge(qk_transposed, layer + 1)
                nc.vector.tensor_scalar(qbT.rearrange("p h t -> p (h t)"), banks(TRA, 2),
                                        params[:, Q_GAIN + layer:Q_GAIN + layer + 1], HEAD_DIM ** -0.5, ALU.mult, ALU.mult)
                nc.vector.tensor_scalar(kbT, banks(GATE)[:, 0:SEQ], params[:, K_GAIN + layer:K_GAIN + layer + 1],
                                        None, ALU.mult).then_inc(qkT_ready, 1)
                for j in range(LEVEL_COUNT):
                    weigh(layer, j)
                    keep_scores(layer, j)
                    if j + 2 < LEVEL_COUNT:
                        dve.wait_ge(level_scores, layer * (LEVEL_COUNT + 1) + j + 2)
                        exponents(j + 2)
                keep_scores(layer, LEVEL_COUNT)
                dve.wait_ge(hgrn_squares, layer + 1)
                nc.vector.reduce_sum(head_sumsq[:, 0:TILES * HEADS], level_tile[0].rearrange("p (n d) -> p n d", d=P),
                                     AX_X).then_inc(head_sums, 1)
                dve.wait_ge(head_rstds, 2 * layer + 2)
                for t in range(TILES):
                    for h in range(HEADS):
                        cols = slice(h * P, (h + 1) * P)
                        last = nc.vector.scalar_tensor_tensor(silu_g[:, t, cols], banks(t)[:, cols],
                                                              head_rstd[:, t * HEADS + h:t * HEADS + h + 1],
                                                              silu_g[:, t, cols], ALU.mult, ALU.mult)
                last.then_inc(ya_ready, 1)
                dve.wait_ge(ya_transposed, layer + 1)
                g0 = HGRN_GAIN + layer * HEADS
                nc.vector.tensor_tensor(yaT, banks(GATE, 2).rearrange("p (h t) -> p h t", h=HEADS),
                                        params[:, g0:g0 + HEADS].unsqueeze(2).to_broadcast([P, HEADS, SEQ]),
                                        ALU.mult).then_inc(yaT_ready, 1)
                for t in range(TILES):
                    keys = (t + 1) * P
                    sv = sw_s[:, 0:SW_HEADS * keys].rearrange("p (h k) -> p h k", h=SW_HEADS)
                    src = (banks(2, 2) if t == 0 else banks(0, 4)).rearrange("p (h k) -> p h k", h=SW_HEADS)
                    dve.wait_ge(sw_scores, TILES * layer + t + 1)
                    nc.vector.tensor_tensor(sv, src, sw_mask[t][:, :].unsqueeze(1).to_broadcast([P, SW_HEADS, keys]),
                                            ALU.add).then_inc(sw_scores_taken, 1)
                    dve.wait_ge(sw_scores_taken, TILES * layer + t + 1)
                    sink = sink_row[:, layer, :]
                    link(nc.vector.reduce_max(sw_max[:, :], sv, AX_X))
                    link(nc.vector.tensor_tensor(sw_max[:, :], sw_max[:, :], sink, ALU.max))
                    nc.vector.tensor_scalar(sw_negmax[:, :], sw_max[:, :], -1.0, None, ALU.mult)
                    nc.vector.tensor_tensor(sw_sink[:, :], sink, sw_max[:, :], ALU.subtract).then_inc(sw_max_ready, 1)
                    dve.wait_ge(sw_probs, TILES * layer + t + 1)
                    link(nc.vector.tensor_tensor(sw_total[:, :], sw_sum[:, :], sw_sink[:, :], ALU.add))
                    link(nc.vector.reciprocal(sw_recip[:, :], sw_total[:, :]))
                    if t == 1:
                        dve.wait_ge(sw_probs_transposed, TILES * layer + t + 1)
                        nc.vector.tensor_copy(sw_pT[:, 1024:2048], banks(TRA, 2)).then_inc(sw_pT_ready, 1)
                    dve.wait_ge(sw_out, TILES * layer + t + 1)
                    nc.vector.tensor_tensor(qkv[:, t, 0:SW].rearrange("p (h d) -> p h d", d=HEAD_DIM),
                                            banks(GATE if t == 0 else 0).rearrange("p (h d) -> p h d", d=HEAD_DIM),
                                            sw_recip[:, :].unsqueeze(2).to_broadcast([P, SW_HEADS, HEAD_DIM]),
                                            ALU.mult).then_inc(yb_ready, 1)
                    dve.wait_ge(yb_transposed, TILES * layer + t + 1)
                    nc.vector.tensor_copy(ybT[:, :, t * P:(t + 1) * P],
                                          banks(UP).rearrange("p (h t) -> p h t", h=4)).then_inc(ybT_ready, 1)
                dve.wait_ge(branch_ready, layer + 1)
                for t in range(TILES):
                    if t == 0:
                        dve.wait_ge(pa_done, layer + 1)
                    else:
                        dve.wait_ge(units_used, LAYER0[layer] + PB_AT)
                    nc.vector.tensor_tensor(branch[:, t, 0:D], branch[:, t, 0:D], banks(2 * t, 2), ALU.mult)
                for t in range(TILES):
                    if t == 0:
                        dve.wait_ge(pb_done, layer + 1)
                    else:
                        dve.wait_ge(units_used, LAYER0[layer] + WO_AT)
                    link(nc.vector.tensor_tensor(branch[:, t, D:2 * D], branch[:, t, D:2 * D], banks(4 + 2 * t, 2), ALU.mult))
                    nc.vector.tensor_tensor(branch[:, t, 0:D], branch[:, t, 0:D], branch[:, t, D:2 * D],
                                            ALU.add).then_inc(merged_ready, 1)
                for g in range(4):
                    dve.wait_ge(merged_transposed, 4 * layer + g + 1)
                    nc.vector.tensor_copy(hT[:, 2 * g:2 * g + 2, :],
                                          banks(4 + g).rearrange("p (k t) -> p k t", k=2)).then_inc(mergedT_ready, 1)
                dve.wait_ge(units_used, LAYER0[layer] + WO_AT + GATE_UNITS)
                add_to_x()

            def add_to_x():
                nc.vector.tensor_tensor(x[:, 0, :], x[:, 0, :], banks(0, 2), ALU.add)
                nc.vector.tensor_tensor(x[:, 1, :], x[:, 1, :], banks(2, 2), ALU.add).then_inc(x_updated, 1)

            def dense():
                for b in range(STEPS * TILES):
                    dve.wait_ge(silu_done, b + 1)
                    if b % TILES == 0:
                        dve.wait_ge(up_done, b // TILES + 1)
                    else:
                        dve.wait_ge(units_used, DENSE0 + b // TILES * PER_STEP + 2 * G_UNITS)
                    nc.vector.tensor_tensor(act[b % 2], act[b % 2], banks(UP), ALU.mult).then_inc(act_ready, 1)
                dve.wait_ge(units_used, PLE0)
                add_to_x()

            def route():
                e2 = [P, TILES, EXPERTS, EXPERTS]
                dve.wait_ge(logits_done, 1)
                link(nc.vector.tensor_copy(logits[:, :, :], banks(GATE)[:, 0:TILES * EXPERTS].rearrange("p (t e) -> p t e", t=TILES)))
                other = logits[:, :, :].unsqueeze(2).to_broadcast(e2)
                own = logits[:, :, :].unsqueeze(3).to_broadcast(e2)
                link(nc.vector.reduce_max(top[:, :], logits[:, :, :], AX_X))
                nc.vector.tensor_tensor(gate_w[:, :, :], logits[:, :, :], top[:, :].unsqueeze(2).to_broadcast([P, TILES, EXPERTS]),
                                        ALU.subtract).then_inc(top_ready, 1)
                nc.vector.tensor_tensor(pair_a[:, :, :, :], other, own, ALU.is_gt)
                link(nc.vector.tensor_tensor(pair_b[:, :, :, :], other, own, ALU.is_equal))
                link(nc.vector.tensor_tensor(pair_b[:, :, :, :], pair_b[:, :, :, :],
                                             before[:, :, :].unsqueeze(1).to_broadcast(e2), ALU.mult))
                link(nc.vector.tensor_tensor(pair_a[:, :, :, :], pair_a[:, :, :, :], pair_b[:, :, :, :], ALU.add))
                link(nc.vector.reduce_sum(rank[:, :, :], pair_a[:, :, :, :], AX_X))
                nc.vector.tensor_scalar(chosen[:, :, :], rank[:, :, :], TOP_K - 0.5, None, ALU.is_lt).then_inc(chosen_ready, 1)
                dve.wait_ge(chosen_ready, 1)
                dve.wait_ge(route_exps, 1)
                link(nc.vector.tensor_tensor(gate_w[:, :, :], gate_w[:, :, :], chosen[:, :, :], ALU.mult))
                link(nc.vector.reduce_sum(top[:, :], gate_w[:, :, :], AX_X))
                link(nc.vector.reciprocal(top[:, :], top[:, :]))
                link(nc.vector.tensor_tensor(gate_w[:, :, :], gate_w[:, :, :],
                                             top[:, :].unsqueeze(2).to_broadcast([P, TILES, EXPERTS]), ALU.mult))
                dve.wait_ge(places_done, 1)
                place_ps = banks(UP)[:, 0:TILES * EXPERTS].rearrange("p (t e) -> p t e", t=TILES)
                count_ps = banks(UP)[:, TILES * EXPERTS:(TILES + 1) * EXPERTS]
                nc.vector.scalar_tensor_tensor(place[:, :, :], place_ps, 1.0, chosen[:, :, :], ALU.add, ALU.mult)
                link(nc.vector.tensor_scalar(over[:, :], count_ps, P + 0.5, None, ALU.is_gt))
                pa1 = pair_a[:, 0, :, :]
                link(nc.vector.tensor_tensor(pa1, over[:, :].unsqueeze(1).to_broadcast([P, EXPERTS, EXPERTS]), before[:, :, :], ALU.mult))
                link(nc.vector.reduce_sum(over_before[:, :], pa1, AX_X))
                for r in range(EXTRA):
                    last = nc.vector.scalar_tensor_tensor(extra_of[:, r, :], over_before[:, :], float(r), over[:, :],
                                                          ALU.is_equal, ALU.mult)
                link(last)
                link(nc.vector.reduce_sum(n_items[:, :], over[:, :], AX_X))
                nc.vector.tensor_scalar(n_items_i[:, :], n_items[:, :], float(EXPERTS), None, ALU.add)
                pairs = [P, TILES, EXTRA, EXPERTS]
                extra = extra_of[:, :, :].unsqueeze(1).to_broadcast(pairs)
                link(nc.vector.tensor_tensor(pair_a[:, :, 0:EXTRA, :], place[:, :, :].unsqueeze(2).to_broadcast(pairs), extra, ALU.mult))
                nc.vector.memset(item_place[:, :, ITEMS - 1:ITEMS], -1.0)
                nc.vector.memset(item_gate_w[:, :, ITEMS - 1:ITEMS], 0.0)
                link(nc.vector.tensor_tensor(pair_b[:, :, 0:EXTRA, :], gate_w[:, :, :].unsqueeze(2).to_broadcast(pairs), extra, ALU.mult))
                link(nc.vector.reduce_sum(item_place[:, :, EXPERTS:ITEMS - 1], pair_a[:, :, 0:EXTRA, :], AX_X))
                nc.vector.reduce_sum(item_gate_w[:, :, EXPERTS:ITEMS - 1], pair_b[:, :, 0:EXTRA, :], AX_X)
                nc.vector.tensor_scalar(item_place[:, :, EXPERTS:ITEMS - 1], item_place[:, :, EXPERTS:ITEMS - 1],
                                        -1.0 - P, None, ALU.add)
                nc.vector.tensor_scalar(item_place[:, :, 0:EXPERTS], place[:, :, :], -1.0, None, ALU.add)
                nc.vector.tensor_copy(item_gate_w[:, :, 0:EXPERTS], gate_w[:, :, :])
                nc.vector.memset(item_expert[:, :], 0.0)
                link(nc.vector.tensor_tensor(pair_a[:, 0, 0:EXTRA, :], extra_of[:, :, :],
                                             column[:, 0:EXPERTS].unsqueeze(1).to_broadcast([P, EXTRA, EXPERTS]), ALU.mult))
                nc.vector.tensor_copy(item_expert[:, 0:EXPERTS], column[:, 0:EXPERTS])
                link(nc.vector.reduce_sum(item_expert[:, EXPERTS:ITEMS - 1], pair_a[:, 0, 0:EXTRA, :], AX_X))
                nc.vector.tensor_copy(item_expert_i[:, :], item_expert[:, :]).then_inc(routed, 1)
                dve.wait_ge(routed, 1)

            def make_picks(item):
                for t in range(TILES):
                    where = item_place[:, t, item]
                    nc.vector.tensor_scalar(pick[:, t, :], column[:, :], where, None, ALU.is_equal)
                    last = nc.vector.tensor_scalar(pick_gate[:, t, :], column[:, :], where, item_gate_w[:, t, item],
                                                   ALU.is_equal, ALU.mult)
                last.then_inc(picks_ready, 1)

            def take_gathered(first, count):
                g0 = FFN_GAIN + KD
                for n in range(2):
                    if n == 0:
                        dve.wait_ge(gathered, count)
                    nc.vector.tensor_tensor(gatheredT[:, 4 * n:4 * n + 4, :], banks(GATE + n).rearrange("p (k t) -> p k t", k=4),
                                            params[:, g0 + 4 * n:g0 + 4 * n + 4].unsqueeze(2).to_broadcast([P, 4, P]),
                                            ALU.mult).then_inc(gatheredT_ready, 1)

            def experts():
                route()
                make_picks(slice(0, 1))
                take_gathered(0, 1)
                count = dve.value_load(n_items_i[0:1, 0:1], min_val=EXPERTS, max_val=EXPERTS + EXTRA)
                with dve.Fori(0, count) as t:
                    dve.wait_ge(pick_transposed, t + 1)
                    nc.vector.tensor_copy(spread, banks(TRB)[:, 0:SEQ]).then_inc(spread_ready, 1)
                    for s in range(STEPS):
                        dve.wait_ge(item_silu, t * STEPS + s + 1)
                        dve.wait_ge(units_used, t * PER_ITEM + MOE + item_up(s) + G_UNITS)
                        nc.vector.tensor_tensor(act[s % 2], act[s % 2], banks(UP), ALU.mult).then_inc(item_act, 1)
                        if s == 0:
                            make_picks(bass.ds(t + 1, 1))
                    take_gathered(t + 1, t + 2)
                    for n in range(TILES):
                        dve.wait_ge(item_combined, t * TILES + n + 1)
                        nc.vector.tensor_tensor(x[:, n, :], x[:, n, :], banks(2 if n == 0 else TRA, 2), ALU.add).then_inc(item_added, 1)
                return count

            def embedding(layer, count=None):
                dve.wait_ge(p_transposed, layer + 1)
                nc.vector.tensor_copy(pT, banks(GATE).rearrange("p (k t) -> p k t", k=2)).then_inc(pT_ready, 1)
                norm(3 * layer + 2, PLE_GAIN + layer * KD)
                for t in range(TILES):
                    dve.wait_ge(ple_gate_ready, TILES * layer + t + 1)
                    if t == 0:
                        dve.wait_ge(ple_up_done, layer + 1)
                    elif layer == 0:
                        dve.wait_ge(units_used, MIX1)
                    else:
                        dve.wait_ge(units_used, count * PER_ITEM + MOE + GATE_UNITS + 1)
                    link(nc.vector.tensor_tensor(ple_gate[:, t, :], ple_gate[:, t, :], banks(4 + 2 * t, 2), ALU.mult))
                    last = nc.vector.tensor_tensor(x[:, t, :], x[:, t, :], ple_gate[:, t, :], ALU.add)
                last.then_inc(x_updated, 1)

            constants()
            norm(0, MIX_GAIN)
            mixer(0)
            norm(1, FFN_GAIN)
            dense()
            embedding(0)
            norm(3, MIX_GAIN + KD)
            mixer(1)
            norm(4, FFN_GAIN + KD)
            embedding(1, experts())

        @block.tensor
        def _(pe):
            def wait_unit(n, more=0):
                pe.wait_ge(slot_filled[n % SLOTS], 16 * (n // SLOTS + 1) + more)

            def unit(n, width):
                return ring[:, n % SLOTS, :].rearrange("p (k n) -> p k n", n=width)

            def mm(o, lhsT, rhs, start, stop):
                return nc.tensor.matmul(o, lhsT, rhs, start=start, stop=stop)

            def transpose_tokens(src, done, ready, ready_at):
                for g in range(4):
                    for kk in range(2):
                        for t in range(TILES):
                            if g == 0 and kk == 0:
                                pe.wait_ge(ready, ready_at + t + 1)
                            k = 2 * g + kk
                            last = nc.tensor.transpose(banks(4 + g)[:, kk * SEQ + t * P:kk * SEQ + (t + 1) * P],
                                                       src[:, t, k * P:(k + 1) * P], ident[:, :])
                    last.then_inc(done, 1)

            def wide_product(base, n_units, lhs, bank0, first_done, more_fill=0):
                for u in range(n_units):
                    wait_unit(base + u, more_fill)
                    w = unit(base + u, D)
                    for t in range(TILES):
                        for half in range(2):
                            for kk in range(2):
                                k = 2 * u + kk
                                last = mm(banks(bank0 + 2 * t + half), lhs[:, k, t * P:(t + 1) * P],
                                          w[:, kk, half * BANK:(half + 1) * BANK], k == 0, k == 2 * n_units - 1)
                        if u == n_units - 1 and t == 0:
                            last.then_inc(first_done, 1)
                    last.then_inc(units_used, 1)

            def project(layer, o):
                c, t = o // TILES, o % TILES
                width = IN_COLUMNS[c][1]
                per = UNIT // width
                if o >= 4:
                    pe.wait_ge(proj_taken, layer * OUTS + o - 3)
                for k in range(KD):
                    n = LAYER0[layer] + COLUMN_UNIT[c] + k // per
                    if t == 0 and k % per == 0:
                        wait_unit(n)
                    last = mm(banks(o % 4)[:, 0:width], hT[:, k, t * P:(t + 1) * P], unit(n, width)[:, k % per, :],
                              k == 0, k == KD - 1)
                if t == 0:
                    last.then_inc(proj_done, 1)
                else:
                    last.then_inc(units_used, KD // per)

            def level_product(layer, g):
                b = GATE if g % 2 == 0 else TRA
                if g >= 2:
                    pe.wait_ge(level_taken, layer * (LEVEL_COUNT + 1) + g - 1)
                if g == 0:
                    pe.wait_ge(q_taken, layer + 1)
                    left, right = kT, qT
                else:
                    pe.wait_ge(level_ready, layer * LEVEL_COUNT + g)
                    left = right = level_tile[(g - 1) % 2]
                if g > 0 and LEVEL_HALF[g - 1] > CHUNK:
                    for h in range(HEADS):
                        last = mm(banks(b)[:, h * P:(h + 1) * P], left[:, h * SEQ:h * SEQ + P],
                                  right[:, h * SEQ + P:(h + 1) * SEQ], True, True)
                else:
                    for n in range(HEADS * TILES):
                        last = mm(banks(b, 2)[:, n * P:(n + 1) * P], left[:, n * P:(n + 1) * P],
                                  right[:, n * P:(n + 1) * P], True, True)
                last.then_inc(level_scores, 1)

            def mixer(layer):
                pe.wait_ge(hT_ready, 4 * (3 * layer + 1))
                for o in range(10):
                    project(layer, o)
                for src, b, taken, done in ((f_tok, TRA, 6, f_transposed), (q_tok, GATE, 2, q_transposed)):
                    pe.wait_ge(proj_taken, layer * OUTS + taken)
                    for h in range(HEADS):
                        for t in range(TILES):
                            last = nc.tensor.transpose(banks(b, 2)[:, h * SEQ + t * P:h * SEQ + (t + 1) * P],
                                                       src[:, t, h * P:(h + 1) * P], ident[:, :])
                    last.then_inc(done, 1)
                for o in range(10, 13):
                    project(layer, o)
                pe.wait_ge(qk_normed, TILES * (layer + 1))
                pe.wait_ge(f_taken, layer + 1)
                pe.wait_ge(q_taken, layer + 1)
                for t in range(TILES):
                    for h in range(4):
                        nc.tensor.transpose(banks(TRA, 2)[:, h * SEQ + t * P:h * SEQ + (t + 1) * P], qkv[:, t, h * P:(h + 1) * P],
                                            ident[:, :])
                    last = nc.tensor.transpose(banks(GATE)[:, t * P:(t + 1) * P], qkv[:, t, SW:SW + KV], ident[:, :])
                last.then_inc(qk_transposed, 1)
                project(layer, 13)
                pe.wait_ge(qkT_ready, layer + 1)
                level_product(layer, 0)
                for g in range(1, LEVEL_COUNT + 1):
                    if 13 + g < OUTS:
                        project(layer, 13 + g)
                    level_product(layer, g)
                pe.wait_ge(level_taken, (layer + 1) * (LEVEL_COUNT + 1))
                pe.wait_ge(proj_taken, (layer + 1) * OUTS)
                for h in range(HEADS):
                    last = mm(banks(0)[:, h * P:(h + 1) * P], sc_tile[:, 2 * h, :], i_tok[:, 0, h * P:(h + 1) * P], True, True)
                last.then_inc(hgrn_out, 1)
                for h in range(HEADS):
                    mm(banks(1)[:, h * P:(h + 1) * P], sc_cross[:, h, :], i_tok[:, 0, h * P:(h + 1) * P], True, False)
                    last = mm(banks(1)[:, h * P:(h + 1) * P], sc_tile[:, 2 * h + 1, :], i_tok[:, 1, h * P:(h + 1) * P], False, True)
                last.then_inc(hgrn_out, 1)

                def attention_scores(t):
                    keys = (t + 1) * P
                    b = banks(2, 2) if t == 0 else banks(0, 4)
                    for h in range(SW_HEADS):
                        kv0 = (h // 4) * HEAD_DIM
                        last = mm(b[:, h * keys:(h + 1) * keys], qbT[kv0:kv0 + HEAD_DIM, h % 4, t * P:(t + 1) * P],
                                  kbT[kv0:kv0 + HEAD_DIM, 0:keys], True, True)
                    last.then_inc(sw_scores, 1)

                def attention_out(t):
                    keys = (t + 1) * P
                    pe.wait_ge(sw_probs, TILES * layer + t + 1)
                    for kb in range(t + 1):
                        for h in range(SW_HEADS):
                            b = banks(TRA if t == 0 else GATE, 2 * (t + 1))
                            last = nc.tensor.transpose(b[:, (kb * SW_HEADS + h) * P:(kb * SW_HEADS + h + 1) * P],
                                                       sw_s[:, h * keys + kb * P:h * keys + (kb + 1) * P], ident[:, :])
                    last.then_inc(sw_probs_transposed, 1)
                    pe.wait_ge(sw_pT_ready, 3 * layer + (1 if t == 0 else 3))
                    b = banks(GATE if t == 0 else 0)
                    for h in range(SW_HEADS):
                        v0 = SW + KV + (h // 4) * HEAD_DIM
                        for kb in range(t + 1):
                            last = mm(b[:, h * HEAD_DIM:(h + 1) * HEAD_DIM],
                                      sw_pT[:, (kb * SW_HEADS + h) * P:(kb * SW_HEADS + h + 1) * P],
                                      qkv[:, kb, v0:v0 + HEAD_DIM], kb == 0, kb == t)
                    last.then_inc(sw_out, 1)
                    pe.wait_ge(yb_ready, TILES * layer + t + 1)
                    for k in range(4):
                        last = nc.tensor.transpose(banks(UP)[:, k * P:(k + 1) * P], qkv[:, t, k * P:(k + 1) * P], ident[:, :])
                    last.then_inc(yb_transposed, 1)

                attention_scores(0)
                pe.wait_ge(ya_ready, layer + 1)
                for h in range(HEADS):
                    for t in range(TILES):
                        last = nc.tensor.transpose(banks(GATE, 2)[:, h * SEQ + t * P:h * SEQ + (t + 1) * P],
                                                   silu_g[:, t, h * P:(h + 1) * P], ident[:, :])
                last.then_inc(ya_transposed, 1)
                pe.wait_ge(yaT_ready, layer + 1)
                attention_out(0)
                attention_scores(1)
                pe.wait_ge(ybT_ready, TILES * layer + 1)
                attention_out(1)
                base = LAYER0[layer]
                wide_product(base + PA_AT, 2, yaT, 0, pa_done)
                pe.wait_ge(ybT_ready, TILES * (layer + 1))
                wide_product(base + PB_AT, 2, ybT, 4, pb_done)
                transpose_tokens(branch, merged_transposed, merged_ready, TILES * layer)
                pe.wait_ge(mergedT_ready, 4 * (layer + 1))
                wide_product(base + WO_AT, 4, hT, 0, wo_done)

            def dense():
                blocks = STEPS * TILES
                pe.wait_ge(hT_ready, 8)

                def inner(b, first_unit, bank, first_done):
                    s, t = b // TILES, b % TILES
                    for k in range(KD):
                        n = DENSE0 + s * PER_STEP + first_unit + k // 4
                        if t == 0 and k % 4 == 0:
                            wait_unit(n)
                        last = mm(banks(bank), hT[:, k, t * P:(t + 1) * P], unit(n, BANK)[:, k % 4, :], k == 0, k == KD - 1)
                    if t == 0:
                        last.then_inc(first_done, 1)
                    else:
                        last.then_inc(units_used, G_UNITS)

                def flip(b):
                    pe.wait_ge(act_ready, b + 1)
                    for k in range(4):
                        last = nc.tensor.transpose(banks(TRA + b % 2)[:, k * P:(k + 1) * P],
                                                   act[b % 2][:, k * P:(k + 1) * P], ident[:, :])
                    last.then_inc(act_transposed, 1)

                def down(b):
                    s, t = b // TILES, b % TILES
                    pe.wait_ge(actT_ready, b + 1)
                    for k in range(4):
                        n = DENSE0 + s * PER_STEP + 2 * G_UNITS + k // 2
                        if t == 0 and k % 2 == 0:
                            wait_unit(n)
                        for half in range(2):
                            last = mm(banks(2 * t + half), actT[b % 2][:, k, :],
                                      unit(n, D)[:, k % 2, half * BANK:(half + 1) * BANK],
                                      s == 0 and k == 0, s == STEPS - 1 and k == 3)
                    if t == 1:
                        last.then_inc(units_used, D_UNITS)

                for b in range(blocks):
                    if b:
                        pe.wait_ge(silu_done, b)
                    inner(b, 0, GATE, gate_done)
                    if b:
                        flip(b - 1)
                    inner(b, G_UNITS, UP, up_done)
                    if b:
                        down(b - 1)
                flip(blocks - 1)
                down(blocks - 1)

            def route():
                pe.wait_ge(hT_ready, 20)
                pe.wait_ge(params_loaded, 16 * PARAM_DMAS)
                for t in range(TILES):
                    for k in range(KD):
                        last = mm(banks(GATE)[:, t * EXPERTS:(t + 1) * EXPERTS], hT[:, k, t * P:(t + 1) * P],
                                  router[:, k, :], k == 0, k == KD - 1)
                last.then_inc(logits_done, 1)
                pe.wait_ge(chosen_ready, 1)
                b = banks(UP)
                mm(b[:, 0:EXPERTS], later[:, :], chosen[:, 0, :], True, True)
                mm(b[:, EXPERTS:2 * EXPERTS], ones[:, :], chosen[:, 0, :], True, False)
                mm(b[:, EXPERTS:2 * EXPERTS], later[:, :], chosen[:, 1, :], False, True)
                mm(b[:, 2 * EXPERTS:3 * EXPERTS], ones[:, :], chosen[:, 0, :], True, False)
                mm(b[:, 2 * EXPERTS:3 * EXPERTS], ones[:, :], chosen[:, 1, :], False, True).then_inc(places_done, 1)

            def gather(count):
                pe.wait_ge(picks_ready, count)
                for k in range(KD):
                    for t in range(TILES):
                        last = mm(banks(GATE, 2)[:, k * P:(k + 1) * P], normed[:, t, k * P:(k + 1) * P], pick[:, t, :],
                                  t == 0, t == TILES - 1)
                last.then_inc(gathered, 1)

            def experts():
                route()
                pe.wait_ge(routed, 1)
                gather(1)
                count = pe.value_load(n_items_i[0:1, 0:1], min_val=EXPERTS, max_val=EXPERTS + EXTRA)
                with pe.Fori(0, count) as t:
                    fill = t * (16 * (PER_ITEM // SLOTS))

                    def inner(first_unit, bank):
                        for k in range(KD):
                            n = MOE + first_unit + k // 4
                            if k % 4 == 0:
                                wait_unit(n, fill)
                            last = mm(banks(bank), gatheredT[:, k, :], unit(n, BANK)[:, k % 4, :], k == 0, k == KD - 1)
                        last.then_inc(units_used, G_UNITS)

                    def flip(s):
                        pe.wait_ge(item_act, t * STEPS + s + 1)
                        for k in range(4):
                            last = nc.tensor.transpose(banks(TRA + s % 2)[:, k * P:(k + 1) * P],
                                                       act[s % 2][:, k * P:(k + 1) * P], ident[:, :])
                        last.then_inc(item_act_transposed, 1)

                    def down(s):
                        pe.wait_ge(item_actT, t * STEPS + s + 1)
                        for k in range(4):
                            n = MOE + item_down(s) + k // 2
                            if k % 2 == 0:
                                wait_unit(n, fill)
                            for half in range(2):
                                last = mm(banks(half), actT[s % 2][:, k, :],
                                          unit(n, D)[:, k % 2, half * BANK:(half + 1) * BANK],
                                          s == 0 and k == 0, s == STEPS - 1 and k == 3)
                        last.then_inc(units_used, D_UNITS)

                    pe.wait_ge(gatheredT_ready, t * 2 + 2)
                    for s in range(STEPS):
                        if s:
                            pe.wait_ge(item_silu, t * STEPS + s)
                        inner(item_gate(s), GATE)
                        if s:
                            flip(s - 1)
                        else:
                            pe.wait_ge(item_added, t * TILES)
                            for n in range(TILES):
                                last = nc.tensor.transpose(banks(TRB)[:, n * P:(n + 1) * P], pick_gate[:, n, :], ident[:, :])
                            last.then_inc(pick_transposed, 1)
                        inner(item_up(s), UP)
                        if s:
                            down(s - 1)
                    pe.wait_ge(item_act, t * STEPS + STEPS)
                    gather(t + 2)
                    flip(STEPS - 1)
                    down(STEPS - 1)
                    pe.wait_ge(item_y_taken, t + 1)
                    pe.wait_ge(spread_ready, t + 1)
                    for n in range(TILES):
                        for half in range(2):
                            last = mm(banks((2 if n == 0 else TRA) + half), spread[:, n * P:(n + 1) * P],
                                      y_item[:, half * BANK:(half + 1) * BANK], True, True)
                        last.then_inc(item_combined, 1)
                return count

            def embedding(layer, count=None):
                if layer:
                    pe.wait_ge(gatheredT_ready, count * 2 + 2)
                pe.wait_ge(p_loaded, 16 * (layer + 1))
                for k in range(PLE // P):
                    for t in range(TILES):
                        last = nc.tensor.transpose(banks(GATE)[:, k * SEQ + t * P:k * SEQ + (t + 1) * P],
                                                   p_tok[:, t, k * P:(k + 1) * P], ident[:, :])
                last.then_inc(p_transposed, 1)
                pe.wait_ge(pT_ready, layer + 1)
                n = 3 * layer + 2
                transpose_tokens(normed, normed_transposed, normed_ready, TILES * n)
                pe.wait_ge(hT_ready, 4 * (n + 1))
                base = PLE0 if layer == 0 else MOE
                fill = count * (16 * (PER_ITEM // SLOTS)) if layer else 0
                wide_product(base, GATE_UNITS, hT, 0, ple_gate_done, more_fill=fill)
                wide_product(base + GATE_UNITS, 1, pT, 4, ple_up_done, more_fill=fill)

            pe.wait_ge(params_loaded, 16 * PARAM_DMAS)
            pe.wait_ge(vector_constants, 1)
            nc.tensor.transpose(banks(0)[:, 0:PARAM_ROWS], param_rows[0:PARAM_ROWS, :],
                                ident[0:PARAM_ROWS, 0:PARAM_ROWS]).then_inc(params_transposed, 1)
            transpose_tokens(normed, normed_transposed, normed_ready, 0)
            mixer(0)
            transpose_tokens(normed, normed_transposed, normed_ready, TILES)
            dense()
            embedding(0)
            transpose_tokens(normed, normed_transposed, normed_ready, 3 * TILES)
            mixer(1)
            transpose_tokens(normed, normed_transposed, normed_ready, 4 * TILES)
            embedding(1, experts())


_INS = ["x", "p", "lb_logits", "g_mix", "w_in", "q_norm", "k_norm", "sinks", "hgrn_norm", "w_pa", "w_pb", "w_o",
        "g_ffn", "w_dense_gate", "w_dense_up", "w_dense_down", "w_router", "w_moe_gate", "w_moe_up", "w_moe_down",
        "g_ple", "w_ple_gate", "w_ple_up"]


def kernel(**inputs):
    import numpy as _np
    import concourse.bacc as _bacc
    from concourse import mybir as _mybir
    from concourse.bass_utils import run_bass_kernel_spmd as _run

    nc = _bacc.Bacc("TRN2", target_bir_lowering=False, num_devices=1)
    arrays, args = {}, []
    for name in _INS:
        a = _np.ascontiguousarray(inputs[name])
        arrays[f"in_{name}"] = a
        args.append(nc.dram_tensor(f"in_{name}", a.shape, _mybir.dt.from_np(a.dtype), kind="ExternalInput").ap())
    shape = inputs["x"].shape
    args.append(nc.dram_tensor("trunk_out", shape, _mybir.dt.float32, kind="ExternalOutput").ap())
    build_trunk(nc, *args)
    r = _run(nc, [arrays], core_ids=[0])
    return r.results[0]["trunk_out"]
```

```python
from contextlib import ExitStack

import concourse.bass as bass
from concourse import mybir

ALU = mybir.AluOpType
ACT = mybir.ActivationFunctionType
F32 = mybir.dt.float32
F32R = mybir.dt.float32r
I32 = mybir.dt.int32
U8 = mybir.dt.uint8
AX_X = mybir.AxisListType.X

P = 128
BANK = 512
EPS = 1e-6
CHUNK = 64
HEADS = 4
SW_HEADS = 8
KV_HEADS = 2
HEAD_DIM = 64
TOP_K = 2
RAW_SLOTS = 6
SLOTS = 3
UNIT = 2048
MASKED = -1e30
F_LEAST = 1e-19


def build_trunk(nc, x_in, p_in, lb_logits, g_mix, w_in, q_norm, k_norm, sinks, hgrn_norm, w_pa, w_pb, w_o,
                g_ffn, w_dense_gate, w_dense_up, w_dense_down, w_router, w_moe_gate, w_moe_up, w_moe_down,
                g_ple, w_ple_gate, w_ple_up, out):
    _, SEQ, D = x_in.shape
    DEPTH = p_in.shape[0]
    PLE = p_in.shape[3]
    IN = w_in.shape[2]
    D_FF = w_dense_gate.shape[2]
    EXPERTS = w_moe_gate.shape[1]
    TILES = SEQ // P
    KD = D // P
    HW = HEADS * P
    SW = SW_HEADS * HEAD_DIM
    KV = KV_HEADS * HEAD_DIM
    STEPS = D_FF // BANK
    EXTRA = 3
    ITEMS = EXPERTS + EXTRA + 1
    assert DEPTH == 2 and TILES == 2 and D == 1024 and HW == BANK and SW == BANK and D_FF % BANK == 0
    assert PLE == 2 * P and TOP_K * SEQ < (EXTRA + 1) * (P + 1) and KV * 2 == 256
    assert IN == 4 * HW + SW + 2 * KV + 2 * D

    def rows(w, k0, n):
        return w[k0 * P:(k0 + n) * P, :].rearrange("(k p) n -> p k n", p=P)

    IN_COLUMNS = [(0, BANK), (3 * HW, BANK), (HW, BANK), (2 * HW, BANK), (4 * HW, BANK), (4 * HW + SW, 2 * KV)]
    IN_COLUMNS += [(4 * HW + SW + 2 * KV + c * BANK, BANK) for c in range(2 * D // BANK)]
    OUTS = len(IN_COLUMNS) * TILES
    MIX_OUTS = 6 * TILES
    PER_STEP = 2 * KD * BANK // UNIT + BANK // P * D // UNIT
    G_UNITS = KD * BANK // UNIT
    D_UNITS = BANK // P * D // UNIT
    PER_ITEM = STEPS * PER_STEP
    assert PER_ITEM % SLOTS == 0 and PER_ITEM % RAW_SLOTS == 0

    def in_units(layer):
        units = []
        for c0, width in IN_COLUMNS:
            per = UNIT // width
            for k0 in range(0, KD, per):
                units.append(rows(w_in[layer], k0, per)[:, :, c0:c0 + width])
        return units

    def wide_units(w):
        return [rows(w, k0, UNIT // D) for k0 in range(0, w.shape[0] // P, UNIT // D)]

    MIX_UNITS = [in_units(i) + wide_units(w_pa[i]) + wide_units(w_pb[i]) + wide_units(w_o[i]) for i in range(DEPTH)]
    PLE_UNITS = [wide_units(w_ple_gate[i]) + wide_units(w_ple_up[i]) for i in range(DEPTH)]
    IN_UNITS = len(in_units(0))
    COLUMN_UNIT = [sum(KD * width // UNIT for _, width in IN_COLUMNS[:c]) for c in range(len(IN_COLUMNS) + 1)]
    GATE_UNITS = D * D // P // UNIT
    PA_AT, PB_AT = IN_UNITS, IN_UNITS + 2
    WO_AT = IN_UNITS + 4

    def column_units(w, step):
        return [rows(w, k0, UNIT // BANK)[:, :, step * BANK:(step + 1) * BANK]
                for k0 in range(0, KD, UNIT // BANK)]

    def down_units(w, step):
        kt = BANK // P
        return [rows(w, step * kt + k0, UNIT // D) for k0 in range(0, kt, UNIT // D)]

    def mixer_units(gate, up, down):
        units = []
        for s in range(STEPS):
            units += column_units(gate, s) + column_units(up, s)
            if s:
                units += down_units(down, s - 1)
        return units + down_units(down, STEPS - 1)

    DENSE_UNITS = mixer_units(w_dense_gate[0], w_dense_up[0], w_dense_down[0])
    MIX0 = 0
    DENSE0 = len(MIX_UNITS[0])
    PLE0 = DENSE0 + len(DENSE_UNITS)
    MIX1 = PLE0 + len(PLE_UNITS[0])
    MOE = MIX1 + len(MIX_UNITS[1])
    LAYER0 = [MIX0, MIX1]
    END = MOE + len(PLE_UNITS[1])
    LEVEL_HALF = [64, 32, 16, 8, 4, 2, 1, 128]
    LEVEL_COUNT = len(LEVEL_HALF)
    LEVELS_AFTER = {6: [0, 1], 7: [2, 3], 8: [4, 5], 9: [6, 7]}
    BLOCKS_BEFORE = [7, 8, 8, 9, 9] + [10] * (LEVEL_COUNT - 4)

    def item_gate(s):
        return 0 if s == 0 else 2 * G_UNITS + (s - 1) * PER_STEP

    def item_up(s):
        return item_gate(s) + G_UNITS

    def item_down(s):
        return item_up(s + 1) + G_UNITS if s + 1 < STEPS else PER_ITEM - D_UNITS

    with ExitStack() as ctx:
        def sb(name, shape, dt=F32):
            return ctx.enter_context(nc.sbuf_tensor(name, shape, dt))

        def sem(name):
            return ctx.enter_context(nc.semaphore(name))

        raw = sb("raw", [P, RAW_SLOTS, UNIT])
        w_hi = sb("w_hi", [P, SLOTS, UNIT], F32R)
        w_lo = sb("w_lo", [P, SLOTS, UNIT], F32R)
        x = sb("x", [P, TILES, D])
        normed = sb("normed", [P, TILES, D])
        hT = [sb("hT_hi", [P, KD, SEQ], F32R), sb("hT_lo", [P, KD, SEQ], F32R)]
        inner = [sb("inner_hi", [P, 4 * SEQ], F32R), sb("inner_lo", [P, 4 * SEQ], F32R)]
        innerT = [a[:, :].rearrange("p (k t) -> p k t", k=4) for a in inner]
        arena = sb("arena", [P, 4096 + 3584 + 5120 + 1536 + 1280])
        wide = arena[:, 0:4096]
        q_tok = wide[:, 0:1024].rearrange("p (t n) -> p t n", t=TILES)
        f_tok = wide[:, 1024:2048].rearrange("p (t n) -> p t n", t=TILES)
        branch = wide.rearrange("p (t n) -> p t n", t=TILES)
        act = [wide[:, n * BANK:(n + 1) * BANK] for n in range(2)]
        y_item = wide[:, 3072:4096]
        toks = arena[:, 4096:7680]
        silu_g = toks[:, 0:1024].rearrange("p (t n) -> p t n", t=TILES)
        i_tok = toks[:, 1024:2048].rearrange("p (t n) -> p t n", t=TILES)
        qkv = toks[:, 2048:3584].rearrange("p (t n) -> p t n", t=TILES)
        ple_gate = toks[:, 0:2048].rearrange("p (t n) -> p t n", t=TILES)
        deep = arena[:, 7680:12800]
        qT, kT, bT = (deep[:, n * 1024:(n + 1) * 1024] for n in range(3))
        level_tile = [deep[:, (3 + n) * 1024:(4 + n) * 1024] for n in range(2)]
        sw_s = deep[:, 1024:3072]
        sw_pT = deep[:, 3072:5120]
        score_mem = arena[:, 12800:14336]
        sc_tile = score_mem[:, 0:1024].rearrange("p (n t) -> p n t", t=P)
        sc_cross = score_mem[:, 1024:1536].rearrange("p (n t) -> p n t", t=P)
        sw_sq = score_mem[:, 0:TILES * (SW + KV)].rearrange("p (t n) -> p t n", t=TILES)
        qk_mem = arena[:, 14336:15616]
        qbT = qk_mem[:, 0:1024].rearrange("p (h t) -> p h t", h=HEADS)
        kbT = qk_mem[:, 1024:1280]
        pick = qk_mem[:, 0:256].rearrange("p (t s) -> p t s", t=TILES)
        pick_gate = qk_mem[:, 256:512].rearrange("p (t s) -> p t s", t=TILES)
        spread = qk_mem[:, 512:768]
        p_tok = sb("p_tok", [P, TILES, PLE])

        ident = sb("ident", [P, P])
        later = sb("later", [P, P])
        ones = sb("ones", [P, P])
        column = sb("column", [P, P])
        LEVELS = [64, 32, 16, 8, 4, 2, 1]
        masks = sb("masks", [P, 1 + len(LEVELS), P], U8)
        int_a = toks[:, 0:P].bitcast(I32)
        int_b = toks[:, P:2 * P].bitcast(I32)
        sw_mask = [sb("sw_mask0", [P, P]), sb("sw_mask1", [P, 2 * P])]
        before = sb("before", [P, EXPERTS, EXPERTS])
        param_rows = sb("param_rows", [P, P])
        params = sb("params", [P, P])
        lb = sb("lb", [P, DEPTH, HEADS])
        lb_rest = sb("lb_rest", [P, DEPTH, HEADS])
        lb_tmp = sb("lb_tmp", [P, 6, HEADS])
        sink_row = sb("sink_row", [P, DEPTH, SW_HEADS])
        router = sb("router", [P, KD, EXPERTS])
        minus_half = sb("minus_half", [P, 32])
        sumsq = sb("sumsq", [P, TILES])
        meansq = sb("meansq", [P, TILES])
        rstd = sb("rstd", [P, TILES])
        head_sumsq = sb("head_sumsq", [P, 20])
        head_meansq = sb("head_meansq", [P, 20])
        head_rstd = sb("head_rstd", [P, 20])
        sw_max = sb("sw_max", [P, SW_HEADS])
        sw_negmax = sb("sw_negmax", [P, SW_HEADS])
        sw_sink = sb("sw_sink", [P, SW_HEADS])
        sw_sum = sb("sw_sum", [P, SW_HEADS])
        sw_total = sb("sw_total", [P, SW_HEADS])
        sw_recip = sb("sw_recip", [P, SW_HEADS])
        logits = sb("logits", [P, TILES, EXPERTS])
        pairs_mem = score_mem[:, 0:2 * TILES * EXPERTS * EXPERTS].rearrange("p (n t e f) -> p n t e f", n=2, t=TILES, e=EXPERTS)
        pair_a, pair_b = pairs_mem[:, 0], pairs_mem[:, 1]
        rank = sb("rank", [P, TILES, EXPERTS])
        chosen = sb("chosen", [P, TILES, EXPERTS])
        gate_w = sb("gate_w", [P, TILES, EXPERTS])
        top = sb("top", [P, TILES])
        place = sb("place", [P, TILES, EXPERTS])
        over = sb("over", [P, EXPERTS])
        over_before = sb("over_before", [P, EXPERTS])
        extra_of = sb("extra_of", [P, EXTRA, EXPERTS])
        item_place = sb("item_place", [P, TILES, ITEMS])
        item_gate_w = sb("item_gate_w", [P, TILES, ITEMS])
        item_expert = sb("item_expert", [P, ITEMS])
        item_expert_i = sb("item_expert_i", [P, ITEMS], I32)
        n_items = sb("n_items", [P, 1])
        n_items_i = sb("n_items_i", [P, 1], I32)

        ps = ctx.enter_context(nc.psum_tensor("ps", [P, 8, BANK], F32))
        GATE, UP, TRA, TRB = 4, 5, 6, 7

        def banks(b, n=1):
            return ps[:, b:b + n, :].rearrange("p b n -> p (b n)")

        x_loaded = sem("x_loaded")
        params_loaded = sem("params_loaded")
        p_loaded = sem("p_loaded")
        raw_filled = [sem(f"raw{s}_filled") for s in range(RAW_SLOTS)]
        high_ready = sem("high_ready")
        low_ready = sem("low_ready")
        units_used = sem("units_used")
        pool_constants = sem("pool_constants")
        vector_constants = sem("vector_constants")
        params_transposed = sem("params_transposed")
        lb_exps = sem("lb_exps")
        lb_diffs = sem("lb_diffs")
        vector_step = sem("vector_step")
        pool_step = sem("pool_step")
        squares_ready = sem("squares_ready")
        rstd_ready = sem("rstd_ready")
        normed_ready = sem("normed_ready")
        normed_transposed = sem("normed_transposed")
        hT_high = sem("hT_high")
        hT_ready = sem("hT_ready")
        proj_taken = sem("proj_taken")
        f_transposed = sem("f_transposed")
        f_taken = sem("f_taken")
        f_clamped = sem("f_clamped")
        logf_ready = sem("logf_ready")
        q_transposed = sem("q_transposed")
        q_taken = sem("q_taken")
        sw_squares = sem("sw_squares")
        head_sums = sem("head_sums")
        head_rstds = sem("head_rstds")
        qk_normed = sem("qk_normed")
        qk_transposed = sem("qk_transposed")
        qkT_ready = sem("qkT_ready")
        level_exponents = sem("level_exponents")
        level_exps = sem("level_exps")
        level_ready = sem("level_ready")
        level_scores = sem("level_scores")
        level_taken = sem("level_taken")
        hgrn_out = sem("hgrn_out")
        hgrn_squares = sem("hgrn_squares")
        ya_ready = sem("ya_ready")
        ya_transposed = sem("ya_transposed")
        yaT_high = sem("yaT_high")
        yaT_ready = sem("yaT_ready")
        sw_scores = sem("sw_scores")
        sw_scores_taken = sem("sw_scores_taken")
        sw_max_ready = sem("sw_max_ready")
        sw_probs = sem("sw_probs")
        sw_probs_transposed = sem("sw_probs_transposed")
        sw_pT_ready = sem("sw_pT_ready")
        sw_out = sem("sw_out")
        yb_ready = sem("yb_ready")
        yb_transposed = sem("yb_transposed")
        ybT_high = sem("ybT_high")
        ybT_ready = sem("ybT_ready")
        branch_ready = sem("branch_ready")
        merged_ready = sem("merged_ready")
        merged_transposed = sem("merged_transposed")
        mergedT_high = sem("mergedT_high")
        mergedT_ready = sem("mergedT_ready")
        x_updated = sem("x_updated")
        silu_done = sem("silu_done")
        act_ready = sem("act_ready")
        act_transposed = sem("act_transposed")
        actT_high = sem("actT_high")
        actT_ready = sem("actT_ready")
        logits_done = sem("logits_done")
        top_ready = sem("top_ready")
        route_exps = sem("route_exps")
        chosen_ready = sem("chosen_ready")
        places_done = sem("places_done")
        routed = sem("routed")
        picks_ready = sem("picks_ready")
        gathered = sem("gathered")
        gatheredT_high = sem("gatheredT_high")
        gatheredT_ready = sem("gatheredT_ready")
        pick_transposed = sem("pick_transposed")
        spread_ready = sem("spread_ready")
        item_silu = sem("item_silu")
        item_act = sem("item_act")
        item_act_transposed = sem("item_act_transposed")
        item_actT_high = sem("item_actT_high")
        item_actT = sem("item_actT")
        item_y_done = sem("item_y_done")
        item_y_taken = sem("item_y_taken")
        item_combined = sem("item_combined")
        item_added = sem("item_added")
        p_transposed = sem("p_transposed")
        pT_high = sem("pT_high")
        pT_ready = sem("pT_ready")
        ple_gate_ready = sem("ple_gate_ready")
        stored = sem("stored")

        MIX_GAIN, FFN_GAIN, PLE_GAIN = 0, DEPTH * KD, 2 * DEPTH * KD
        HGRN_GAIN = 3 * DEPTH * KD
        LB_AT = HGRN_GAIN + DEPTH * HEADS
        Q_GAIN = LB_AT + DEPTH * HEADS
        K_GAIN = Q_GAIN + DEPTH
        PARAM_ROWS = K_GAIN + DEPTH
        PARAM_DMAS = 3 + 2 + 4 + 2

        block = ctx.enter_context(nc.Block())

        @block.sync
        def _(sp):
            sp.dma_start(x[:, :, :], x_in[0].rearrange("(t p) d -> p t d", p=P)).then_inc(x_loaded, 16)

            def load_unit(n, source, items=0):
                if n >= RAW_SLOTS:
                    sp.wait_ge(low_ready, n - RAW_SLOTS + 1 + items * PER_ITEM)
                k = source.shape[1]
                dst = raw[:, n % RAW_SLOTS, :].rearrange("p (k n) -> p k n", k=k)
                sp.dma_start(dst, source).then_inc(raw_filled[n % RAW_SLOTS], 16)

            for n, source in enumerate(MIX_UNITS[0][:2]):
                load_unit(n, source)
            for base, w in ((MIX_GAIN, g_mix), (FFN_GAIN, g_ffn), (PLE_GAIN, g_ple)):
                sp.dma_start(param_rows[base:base + DEPTH * KD, :],
                             w.rearrange("l (k p) -> (l k) p", p=P)).then_inc(params_loaded, 16)
            for base, w in ((HGRN_GAIN, hgrn_norm), (LB_AT, lb_logits)):
                sp.dma_start(param_rows[base:base + DEPTH * HEADS, :],
                             w.rearrange("l (h p) -> (l h) p", p=P)).then_inc(params_loaded, 16)
            for base, w in ((Q_GAIN, q_norm), (K_GAIN, k_norm)):
                for half in range(2):
                    sp.dma_start(param_rows[base:base + DEPTH, half * HEAD_DIM:(half + 1) * HEAD_DIM],
                                 w).then_inc(params_loaded, 16)
            sp.dma_start(sink_row[:, :, :], sinks.unsqueeze(0).to_broadcast([P, DEPTH, SW_HEADS])).then_inc(params_loaded, 16)
            sp.dma_start(router[:, :, :], w_router[0].rearrange("(k p) e -> p k e", p=P)).then_inc(params_loaded, 16)

            def load_p(layer):
                sp.dma_start(p_tok[:, :, :], p_in[layer, 0].rearrange("(t p) d -> p t d", p=P)).then_inc(p_loaded, 16)

            load_p(0)
            for n, source in list(enumerate(MIX_UNITS[0] + DENSE_UNITS + PLE_UNITS[0]))[2:]:
                load_unit(n, source)
            sp.wait_ge(p_transposed, 1)
            load_p(1)
            for n, source in enumerate(MIX_UNITS[1]):
                load_unit(MIX1 + n, source)
            for n, source in enumerate(mixer_units(w_moe_gate[0, 0], w_moe_up[0, 0], w_moe_down[0, 0])):
                load_unit(MOE + n, source)
            sp.wait_ge(routed, 1)
            count = sp.value_load(n_items_i[0:1, 0:1], min_val=EXPERTS, max_val=EXPERTS + EXTRA)
            with sp.Fori(1, count) as t:
                e = sp.value_load(item_expert_i[0:1, bass.ds(t, 1)], min_val=0, max_val=EXPERTS - 1)

                def expert(w):
                    return w[0, bass.ds(e, 1), :, :].rearrange("e k n -> (e k) n")

                for n, source in enumerate(mixer_units(expert(w_moe_gate), expert(w_moe_up), expert(w_moe_down))):
                    load_unit(MOE + n, source, t)
            for n, source in enumerate(PLE_UNITS[1]):
                load_unit(MOE + n, source, count)
            sp.wait_ge(x_updated, 5)
            sp.dma_start(out[0].rearrange("(t p) d -> p t d", p=P), x[:, :, :]).then_inc(stored, 16)
            sp.wait_ge(stored, 16)

        @block.gpsimd
        def _(pool):
            steps = [0]

            def link(ins):
                steps[0] += 1
                ins.then_inc(pool_step, 1)
                pool.wait_ge(pool_step, steps[0])

            nc.gpsimd.memset(minus_half[:, :], -0.5)
            nc.gpsimd.memset(ones[:, :], 1.0)
            link(nc.gpsimd.memset(before[:, :, :], 1.0))
            nc.gpsimd.affine_select(out=before[:, :, :], in_=before[:, :, :], pattern=[[1, EXPERTS], [-1, EXPERTS]],
                                    compare_op=ALU.is_gt, fill=0.0, base=0, channel_multiplier=0)
            nc.gpsimd.iota(int_a, pattern=[[1, P]], base=0, channel_multiplier=0)
            nc.gpsimd.iota(int_b, pattern=[[0, P]], base=0, channel_multiplier=1).then_inc(pool_constants, 1)

            def norm_rstd(n):
                pool.wait_ge(squares_ready, TILES * (n + 1))
                link(nc.gpsimd.tensor_scalar(meansq[:, :], sumsq[:, :], 1.0 / D, EPS, ALU.mult, ALU.add))
                nc.gpsimd.tensor_tensor(rstd[:, :], meansq[:, :], minus_half[:, 0:TILES], ALU.pow).then_inc(rstd_ready, 1)

            def heads_rstd(n, heads, width):
                pool.wait_ge(head_sums, n + 1)
                link(nc.gpsimd.tensor_scalar(head_meansq[:, 0:heads], head_sumsq[:, 0:heads], 1.0 / width, EPS,
                                             ALU.mult, ALU.add))
                nc.gpsimd.tensor_tensor(head_rstd[:, 0:heads], head_meansq[:, 0:heads], minus_half[:, 0:heads],
                                        ALU.pow).then_inc(head_rstds, 1)

            for layer in range(DEPTH):
                norm_rstd(3 * layer)
                heads_rstd(2 * layer, TILES * (SW_HEADS + KV_HEADS), HEAD_DIM)
                heads_rstd(2 * layer + 1, TILES * HEADS, P)
                norm_rstd(3 * layer + 1)
                norm_rstd(3 * layer + 2)

        @block.scalar
        def _(act_e):
            split = [0]

            def keep_up(used, items=0, end=None):
                while split[0] < (used + SLOTS if end is None else min(used + SLOTS, end)):
                    n = split[0]
                    act_e.wait_ge(raw_filled[n % RAW_SLOTS], 16 * (n // RAW_SLOTS + 1) + items * (16 * PER_ITEM // RAW_SLOTS))
                    if n >= SLOTS:
                        act_e.wait_ge(units_used, n - SLOTS + 1 + items * PER_ITEM)
                    nc.scalar.activation(w_hi[:, n % SLOTS, :], raw[:, n % RAW_SLOTS, :], ACT.Copy).then_inc(high_ready, 1)
                    split[0] += 1

            def norm_squares(n, used, items=0):
                keep_up(used, items, END if n == 5 else None)
                if n == 0:
                    act_e.wait_ge(x_loaded, 16)
                elif n == 5:
                    act_e.wait_ge(item_added, items * 2)
                else:
                    act_e.wait_ge(x_updated, n)
                for t in range(TILES):
                    nc.scalar.activation(normed[:, t, :], x[:, t, :], ACT.Square,
                                         accum_out=sumsq[:, t:t + 1]).then_inc(squares_ready, 1)

            def norm_high(n, gain):
                for k in range(KD):
                    if k % 2 == 0:
                        act_e.wait_ge(normed_transposed, 4 * n + k // 2 + 1)
                    nc.scalar.activation(hT[0][:, k, :], banks(4 + k // 2)[:, k % 2 * SEQ:(k % 2 + 1) * SEQ], ACT.Copy,
                                         scale=params[:, gain + k:gain + k + 1]).then_inc(hT_high, 1)

            def mixer(layer):
                base = LAYER0[layer]

                def take(c, dst, func, of_heads=False):
                    keep_up(base + COLUMN_UNIT[c + 1])
                    act_e.wait_ge(units_used, base + COLUMN_UNIT[c + 1])
                    for t in range(TILES):
                        src = banks(c % 2 * 2 + t)[:, 0:IN_COLUMNS[c][1]]
                        if of_heads:
                            src = src.rearrange("p (g h d) -> p g h d", g=KV_HEADS, d=HEAD_DIM)
                        nc.scalar.activation(dst(t), src, func).then_inc(proj_taken, 1)

                take(0, lambda t: q_tok[:, t, :], ACT.Silu)
                take(1, lambda t: silu_g[:, t, :], ACT.Silu)
                take(2, lambda t: f_tok[:, t, :], ACT.Sigmoid)
                take(3, lambda t: i_tok[:, t, :], ACT.Copy)
                take(4, lambda t: qkv[:, t, 0:SW].rearrange("p (h g d) -> p g h d", g=KV_HEADS, d=HEAD_DIM), ACT.Copy, True)
                take(5, lambda t: qkv[:, t, SW:SW + 2 * KV], ACT.Copy)
                act_e.wait_ge(proj_taken, layer * OUTS + MIX_OUTS)
                nc.scalar.activation(sw_sq[:, :, :], qkv[:, :, 0:SW + KV], ACT.Square).then_inc(sw_squares, 1)
                act_e.wait_ge(f_clamped, layer + 1)
                nc.scalar.activation(level_tile[0], level_tile[0], ACT.Ln).then_inc(logf_ready, 1)
                for c in range(6, len(IN_COLUMNS)):
                    take(c, lambda t: branch[:, t, (c - 6) * BANK:(c - 5) * BANK], ACT.Copy)
                    for j in LEVELS_AFTER[c]:
                        act_e.wait_ge(level_exponents, layer * LEVEL_COUNT + j + 1)
                        nc.scalar.activation(level_tile[j % 2], level_tile[j % 2], ACT.Exp).then_inc(level_exps, 1)
                act_e.wait_ge(hgrn_out, TILES * (layer + 1))
                nc.scalar.activation(level_tile[0], banks(0, 2), ACT.Square).then_inc(hgrn_squares, 1)
                act_e.wait_ge(ya_transposed, layer + 1)
                g0 = HGRN_GAIN + layer * HEADS
                for h in range(HEADS):
                    nc.scalar.activation(innerT[0][:, h, :], banks(GATE, 2)[:, h * SEQ:(h + 1) * SEQ], ACT.Copy,
                                         scale=params[:, g0 + h:g0 + h + 1]).then_inc(yaT_high, 1)
                for t in range(TILES):
                    keys = (t + 1) * P
                    act_e.wait_ge(sw_max_ready, TILES * layer + t + 1)
                    nc.scalar.activation(sw_sink[:, :], sw_sink[:, :], ACT.Exp)
                    for h in range(SW_HEADS):
                        last = nc.scalar.activation(sw_s[:, h * keys:(h + 1) * keys], sw_s[:, h * keys:(h + 1) * keys],
                                                    ACT.Exp, bias=sw_negmax[:, h:h + 1], accum_out=sw_sum[:, h:h + 1])
                    last.then_inc(sw_probs, 1)
                    act_e.wait_ge(sw_probs_transposed, TILES * layer + t + 1)
                    nc.scalar.activation(sw_pT[:, 0:1024], banks(TRA if t == 0 else GATE, 2), ACT.Copy).then_inc(sw_pT_ready, 1)
                    act_e.wait_ge(yb_transposed, TILES * layer + t + 1)
                    nc.scalar.activation(hT[0][:, 0:4, t * P:(t + 1) * P], banks(UP).rearrange("p (h t) -> p h t", h=4),
                                         ACT.Copy).then_inc(ybT_high, 1)
                nc.scalar.activation(wide, wide, ACT.Sigmoid).then_inc(branch_ready, 1)
                keep_up(base + PB_AT)
                keep_up(base + WO_AT)
                for g in range(4):
                    act_e.wait_ge(merged_transposed, 4 * layer + g + 1)
                    nc.scalar.activation(hT[0][:, 2 * g:2 * g + 2, :], banks(4 + g).rearrange("p (k t) -> p k t", k=2),
                                         ACT.Copy).then_inc(mergedT_high, 1)

            def dense():
                for s in range(STEPS):
                    keep_up(DENSE0 + item_gate(s) + G_UNITS)
                    act_e.wait_ge(units_used, DENSE0 + item_gate(s) + G_UNITS)
                    for t in range(TILES):
                        nc.scalar.activation(act[t], banks(4 + t), ACT.Silu).then_inc(silu_done, 1)
                    keep_up(DENSE0 + item_up(s) + G_UNITS)
                    if s:
                        keep_up(DENSE0 + item_down(s - 1) + D_UNITS)
                    for t in range(TILES):
                        act_e.wait_ge(act_transposed, TILES * s + t + 1)
                        nc.scalar.activation(innerT[0][:, :, t * P:(t + 1) * P], banks(6 + t).rearrange("p (k t) -> p k t", k=4),
                                             ACT.Copy).then_inc(actT_high, 1)

            def experts():
                act_e.wait_ge(top_ready, 1)
                nc.scalar.activation(gate_w[:, :, :], gate_w[:, :, :], ACT.Exp).then_inc(route_exps, 1)
                act_e.wait_ge(routed, 1)

                def gathered_high(count):
                    act_e.wait_ge(gathered, count)
                    for k in range(KD):
                        nc.scalar.activation(hT[0][:, k, 0:P], banks(GATE, 2)[:, k * P:(k + 1) * P], ACT.Copy,
                                             scale=params[:, FFN_GAIN + KD + k:FFN_GAIN + KD + k + 1]).then_inc(gatheredT_high, 1)

                gathered_high(1)
                count = act_e.value_load(n_items_i[0:1, 0:1], min_val=EXPERTS, max_val=EXPERTS + EXTRA)
                with act_e.Fori(0, count) as t:
                    def actT_high_part(s):
                        act_e.wait_ge(item_act_transposed, t * STEPS + s + 1)
                        nc.scalar.activation(innerT[0][:, :, 0:P], banks(TRA).rearrange("p (k t) -> p k t", k=4),
                                             ACT.Copy).then_inc(item_actT_high, 1)

                    for s in range(STEPS):
                        keep_up(MOE + item_gate(s) + G_UNITS, t)
                        act_e.wait_ge(units_used, t * PER_ITEM + MOE + item_gate(s) + G_UNITS)
                        nc.scalar.activation(act[s % 2], banks(GATE), ACT.Silu).then_inc(item_silu, 1)
                        if s:
                            actT_high_part(s - 1)
                        keep_up(MOE + item_up(s) + G_UNITS, t)
                        if s:
                            keep_up(MOE + item_down(s - 1) + D_UNITS, t)
                    actT_high_part(STEPS - 1)
                    gathered_high(t + 2)
                    for half in range(2):
                        if half == 0:
                            act_e.wait_ge(item_y_done, t + 1)
                        else:
                            act_e.wait_ge(units_used, t * PER_ITEM + MOE + PER_ITEM)
                        nc.scalar.activation(y_item[:, half * BANK:(half + 1) * BANK], banks(half),
                                             ACT.Copy).then_inc(item_y_taken, 1)
                    keep_up(MOE + PER_ITEM, t)
                split[0] -= PER_ITEM
                return count

            def embedding(layer, items=0):
                base, end = (PLE0, None) if layer == 0 else (MOE, END)
                keep_up(base, items, end)
                act_e.wait_ge(p_transposed, layer + 1)
                nc.scalar.activation(inner[0][:, 0:PLE * TILES], banks(GATE), ACT.Copy).then_inc(pT_high, 1)
                norm_high(3 * layer + 2, PLE_GAIN + layer * KD)
                keep_up(base + GATE_UNITS, items, end)
                act_e.wait_ge(units_used, base + GATE_UNITS + items * PER_ITEM)
                for t in range(TILES):
                    nc.scalar.activation(ple_gate[:, t, :], banks(2 * t, 2), ACT.Sigmoid).then_inc(ple_gate_ready, 1)

            norm_squares(0, MIX0)
            act_e.wait_ge(lb_diffs, 1)
            nc.scalar.activation(lb_tmp[:, 1:3, :], lb_tmp[:, 1:3, :], ACT.Exp).then_inc(lb_exps, 1)
            norm_high(0, MIX_GAIN)
            mixer(0)
            norm_squares(1, DENSE0)
            norm_high(1, FFN_GAIN)
            dense()
            norm_squares(2, PLE0)
            embedding(0)
            norm_squares(3, MIX1)
            norm_high(3, MIX_GAIN + KD)
            mixer(1)
            norm_squares(4, MOE)
            norm_high(4, FFN_GAIN + KD)
            count = experts()
            norm_squares(5, MOE, count)
            embedding(1, count)

        @block.vector
        def _(dve):
            steps = [0]

            def link(ins):
                steps[0] += 1
                ins.then_inc(vector_step, 1)
                dve.wait_ge(vector_step, steps[0])

            split = [0]

            def keep_up(used, items=0, end=None):
                while split[0] < (used + SLOTS if end is None else min(used + SLOTS, end)):
                    n = split[0]
                    dve.wait_ge(high_ready, n + 1 + items * PER_ITEM)
                    nc.vector.tensor_tensor(w_lo[:, n % SLOTS, :], raw[:, n % RAW_SLOTS, :],
                                            w_hi[:, n % SLOTS, :].bitcast(F32), ALU.subtract).then_inc(low_ready, 1)
                    split[0] += 1

            def low(part, full, cols):
                return nc.vector.tensor_tensor(part[1][cols], full, part[0][cols].bitcast(F32), ALU.subtract)

            def constants():
                nc.vector.memset(sw_mask[0][:, :], 0.0)
                link(nc.vector.memset(sw_mask[1][:, :], 0.0))
                nc.vector.memset(sw_mask[0][0:CHUNK, CHUNK:2 * CHUNK], MASKED)
                nc.vector.memset(sw_mask[1][0:CHUNK, 0:CHUNK], MASKED)
                nc.vector.memset(sw_mask[1][0:CHUNK, 3 * CHUNK:4 * CHUNK], MASKED)
                nc.vector.memset(sw_mask[1][CHUNK:P, 0:2 * CHUNK], MASKED)
                dve.wait_ge(pool_constants, 1)
                nc.vector.tensor_copy(column[:, :], int_a)
                nc.vector.tensor_tensor(ident[:, :], int_a, int_b, ALU.is_equal)
                link(nc.vector.tensor_tensor(later[:, :], int_a, int_b, ALU.is_gt))
                nc.vector.tensor_copy(masks[:, 0, :], ident[:, :]).then_inc(vector_constants, 1)
                link(nc.vector.tensor_tensor(int_a, int_a, int_b, ALU.bitwise_xor))
                link(nc.vector.tensor_copy(params[:, :], int_a))
                link(nc.vector.tensor_tensor(params[:, :], params[:, :], later[:, :], ALU.mult))
                for n, half in enumerate(LEVELS):
                    link(nc.vector.tensor_scalar(score_mem[:, 0:P], params[:, :], float(half), None, ALU.is_ge))
                    link(nc.vector.scalar_tensor_tensor(masks[:, 1 + n, :], params[:, :], float(2 * half), score_mem[:, 0:P],
                                                        ALU.is_lt, ALU.mult))
                dve.wait_ge(params_transposed, 1)
                link(nc.vector.tensor_copy(params[:, 0:PARAM_ROWS], banks(0)[:, 0:PARAM_ROWS]))
                l0 = params[:, LB_AT:LB_AT + HEADS]
                l1 = params[:, LB_AT + HEADS:LB_AT + 2 * HEADS]
                link(nc.vector.tensor_tensor(lb_tmp[:, 0, :], l0, l1, ALU.max))
                nc.vector.tensor_tensor(lb_tmp[:, 1, :], l0, lb_tmp[:, 0, :], ALU.subtract)
                nc.vector.tensor_tensor(lb_tmp[:, 2, :], l1, lb_tmp[:, 0, :], ALU.subtract).then_inc(lb_diffs, 1)
                dve.wait_ge(lb_exps, 1)
                link(nc.vector.tensor_tensor(lb_tmp[:, 3, :], lb_tmp[:, 1, :], lb_tmp[:, 2, :], ALU.add))
                link(nc.vector.reciprocal(lb_tmp[:, 3, :], lb_tmp[:, 3, :]))
                link(nc.vector.tensor_tensor(lb_tmp[:, 4, :], lb_tmp[:, 1, :], lb_tmp[:, 3, :], ALU.mult))
                link(nc.vector.tensor_tensor(lb_tmp[:, 5, :], lb_tmp[:, 2, :], lb_tmp[:, 3, :], ALU.mult))
                link(nc.vector.tensor_tensor(lb_tmp[:, 5, :], lb_tmp[:, 4, :], lb_tmp[:, 5, :], ALU.add))
                nc.vector.tensor_tensor(lb[:, 0, :], lb_tmp[:, 4, :], lb_tmp[:, 4, :], ALU.subtract)
                link(nc.vector.tensor_tensor(lb[:, 1, :], lb_tmp[:, 5, :], lb_tmp[:, 4, :], ALU.subtract))
                link(nc.vector.tensor_scalar(lb_rest[:, :, :], lb[:, :, :], -1.0, 1.0, ALU.mult, ALU.add))

            def norm(n, gain, used, items=0):
                keep_up(used, items, END if n == 5 else None)
                dve.wait_ge(rstd_ready, n + 1)
                for t in range(TILES):
                    nc.vector.tensor_scalar(normed[:, t, :], x[:, t, :], rstd[:, t:t + 1], None,
                                            ALU.mult).then_inc(normed_ready, 1)
                for k in range(KD):
                    dve.wait_ge(hT_high, KD * n + k // 2 * 2 + 2)
                    last = nc.vector.scalar_tensor_tensor(hT[1][:, k, :], banks(4 + k // 2)[:, k % 2 * SEQ:(k % 2 + 1) * SEQ],
                                                          params[:, gain + k:gain + k + 1], hT[0][:, k, :].bitcast(F32),
                                                          ALU.mult, ALU.subtract)
                last.then_inc(hT_ready, 1)

            def exponents(j):
                half = LEVEL_HALF[j]
                e = level_tile[j % 2]
                if half <= CHUNK:
                    ev = e.rearrange("p (n s j) -> p n s j", s=2, j=half)
                    bv = bT.rearrange("p (n s j) -> p n s j", s=2, j=half)
                    n = bv.shape[1]
                    mid = bv[:, :, 0, half - 1:half].to_broadcast([P, n, half])
                    nc.vector.tensor_tensor(ev[:, :, 0, :], mid, bv[:, :, 0, :], ALU.subtract)
                    if half < CHUNK:
                        last = nc.vector.tensor_tensor(ev[:, :, 1, :], bv[:, :, 1, :], mid, ALU.subtract)
                    else:
                        last = nc.vector.tensor_copy(ev[:, :, 1, :], bv[:, :, 1, :])
                else:
                    ev = e.rearrange("p (h c j) -> p h c j", h=HEADS, c=4)
                    bv = bT.rearrange("p (h c j) -> p h c j", h=HEADS, c=4)

                    def end(c):
                        return bv[:, :, c, CHUNK - 1:CHUNK].to_broadcast([P, HEADS, CHUNK])

                    nc.vector.tensor_tensor(ev[:, :, 0, :], end(0), bv[:, :, 0, :], ALU.subtract)
                    nc.vector.tensor_tensor(ev[:, :, 1, :], end(1), bv[:, :, 1, :], ALU.subtract)
                    nc.vector.tensor_copy(ev[:, :, 2, :], bv[:, :, 2, :])
                    link(nc.vector.tensor_tensor(ev[:, :, 3, :], bv[:, :, 3, :], end(2), ALU.add))
                    last = nc.vector.tensor_tensor(ev[:, :, 0, :], ev[:, :, 0, :], end(1), ALU.add)
                last.then_inc(level_exponents, 1)

            def weigh(layer, j):
                half = LEVEL_HALF[j]
                dve.wait_ge(level_exps, layer * LEVEL_COUNT + j + 1)
                ev, kv, qv = (a.rearrange("p (n s j) -> p n s j", s=2, j=half) for a in (level_tile[j % 2], kT, qT))
                nc.vector.tensor_tensor(ev[:, :, 0, :], ev[:, :, 0, :], kv[:, :, 0, :], ALU.mult)
                nc.vector.tensor_tensor(ev[:, :, 1, :], ev[:, :, 1, :], qv[:, :, 1, :], ALU.mult).then_inc(level_ready, 1)

            def keep_scores(layer, g):
                dve.wait_ge(level_scores, layer * (LEVEL_COUNT + 1) + g + 1)
                if g:
                    dve.wait_ge(level_taken, layer * (LEVEL_COUNT + 1) + g)
                src = banks(GATE if g % 2 == 0 else TRA, 2)
                if g > 0 and LEVEL_HALF[g - 1] > CHUNK:
                    ins = nc.vector.tensor_copy(sc_cross[:, :, :], src[:, 0:HEADS * P].rearrange("p (n t) -> p n t", t=P))
                else:
                    m = 0 if g == 0 else 1 + LEVELS.index(LEVEL_HALF[g - 1])
                    ins = nc.vector.copy_predicated(sc_tile[:, :, :],
                                                    masks[:, m:m + 1, :].to_broadcast([P, HEADS * TILES, P]),
                                                    src.rearrange("p (n t) -> p n t", t=P))
                ins.then_inc(level_taken, 1)

            def mixer(layer):
                base = LAYER0[layer]
                lf = level_tile[0]
                for c in range(1, 6):
                    keep_up(base + COLUMN_UNIT[c])
                dve.wait_ge(f_transposed, layer + 1)
                fv = lf.rearrange("p (h t) -> p h t", h=HEADS)
                for h in range(HEADS):
                    last = nc.vector.tensor_scalar(fv[:, h, :], banks(TRA, 2)[:, h * SEQ:(h + 1) * SEQ],
                                                   lb_rest[:, layer, h:h + 1], lb[:, layer, h:h + 1], ALU.mult, ALU.add)
                last.then_inc(f_taken, 1)
                dve.wait_ge(f_taken, layer + 1)
                link(nc.vector.tensor_scalar(kT, lf, -1.0, 1.0, ALU.mult, ALU.add))
                nc.vector.tensor_scalar_max(lf, lf, F_LEAST).then_inc(f_clamped, 1)
                dve.wait_ge(q_transposed, layer + 1)
                nc.vector.tensor_copy(qT, banks(GATE, 2)).then_inc(q_taken, 1)
                reset = level_tile[1]
                link(nc.vector.memset(reset, 1.0))
                link(nc.vector.memset(reset.rearrange("p (n j) -> p n j", j=CHUNK)[:, :, 0:1], 0.0))
                keep_up(base + COLUMN_UNIT[6])
                dve.wait_ge(sw_squares, layer + 1)
                nc.vector.reduce_sum(head_sumsq[:, 0:20].rearrange("p (t h) -> p t h", t=TILES),
                                     sw_sq[:, :, :].rearrange("p t (h d) -> p t h d", d=HEAD_DIM), AX_X).then_inc(head_sums, 1)
                dve.wait_ge(logf_ready, layer + 1)
                link(nc.vector.tensor_tensor_scan(bT, reset, lf, 0.0, ALU.mult, ALU.add))
                exponents(0)
                dve.wait_ge(head_rstds, 2 * layer + 1)
                for t in range(TILES):
                    v = qkv[:, t, 0:SW + KV].rearrange("p (h d) -> p h d", d=HEAD_DIM)
                    nc.vector.tensor_tensor(v, v, head_rstd[:, 10 * t:10 * t + 10].unsqueeze(2).to_broadcast([P, 10, HEAD_DIM]),
                                            ALU.mult).then_inc(qk_normed, 1)
                link(nc.vector.memset(sc_tile[:, :, :], 0.0))
                exponents(1)
                keep_up(base + COLUMN_UNIT[7])
                dve.wait_ge(qk_transposed, layer + 1)
                nc.vector.tensor_scalar(qbT.rearrange("p h t -> p (h t)"), banks(TRA, 2),
                                        params[:, Q_GAIN + layer:Q_GAIN + layer + 1], HEAD_DIM ** -0.5, ALU.mult, ALU.mult)
                nc.vector.tensor_scalar(kbT, banks(GATE)[:, 0:SEQ], params[:, K_GAIN + layer:K_GAIN + layer + 1],
                                        None, ALU.mult).then_inc(qkT_ready, 1)
                for j in range(LEVEL_COUNT):
                    weigh(layer, j)
                    keep_scores(layer, j)
                    if j + 2 < LEVEL_COUNT:
                        keep_up(base + COLUMN_UNIT[BLOCKS_BEFORE[j + 1]])
                        dve.wait_ge(level_scores, layer * (LEVEL_COUNT + 1) + j + 2)
                        exponents(j + 2)
                keep_scores(layer, LEVEL_COUNT)
                dve.wait_ge(hgrn_squares, layer + 1)
                nc.vector.reduce_sum(head_sumsq[:, 0:TILES * HEADS], level_tile[0].rearrange("p (n d) -> p n d", d=P),
                                     AX_X).then_inc(head_sums, 1)
                dve.wait_ge(head_rstds, 2 * layer + 2)
                for t in range(TILES):
                    for h in range(HEADS):
                        cols = slice(h * P, (h + 1) * P)
                        last = nc.vector.scalar_tensor_tensor(silu_g[:, t, cols], banks(t)[:, cols],
                                                              head_rstd[:, t * HEADS + h:t * HEADS + h + 1],
                                                              silu_g[:, t, cols], ALU.mult, ALU.mult)
                last.then_inc(ya_ready, 1)
                g0 = HGRN_GAIN + layer * HEADS
                for h in range(HEADS):
                    dve.wait_ge(yaT_high, HEADS * layer + h // 2 * 2 + 2)
                    last = nc.vector.scalar_tensor_tensor(innerT[1][:, h, :], banks(GATE, 2)[:, h * SEQ:(h + 1) * SEQ],
                                                          params[:, g0 + h:g0 + h + 1], innerT[0][:, h, :].bitcast(F32),
                                                          ALU.mult, ALU.subtract)
                last.then_inc(yaT_ready, 1)
                for t in range(TILES):
                    keys = (t + 1) * P
                    sv = sw_s[:, 0:SW_HEADS * keys].rearrange("p (h k) -> p h k", h=SW_HEADS)
                    src = (banks(2, 2) if t == 0 else banks(0, 4)).rearrange("p (h k) -> p h k", h=SW_HEADS)
                    dve.wait_ge(sw_scores, TILES * layer + t + 1)
                    nc.vector.tensor_tensor(sv, src, sw_mask[t][:, :].unsqueeze(1).to_broadcast([P, SW_HEADS, keys]),
                                            ALU.add).then_inc(sw_scores_taken, 1)
                    dve.wait_ge(sw_scores_taken, TILES * layer + t + 1)
                    sink = sink_row[:, layer, :]
                    link(nc.vector.reduce_max(sw_max[:, :], sv, AX_X))
                    link(nc.vector.tensor_tensor(sw_max[:, :], sw_max[:, :], sink, ALU.max))
                    nc.vector.tensor_scalar(sw_negmax[:, :], sw_max[:, :], -1.0, None, ALU.mult)
                    nc.vector.tensor_tensor(sw_sink[:, :], sink, sw_max[:, :], ALU.subtract).then_inc(sw_max_ready, 1)
                    dve.wait_ge(sw_probs, TILES * layer + t + 1)
                    link(nc.vector.tensor_tensor(sw_total[:, :], sw_sum[:, :], sw_sink[:, :], ALU.add))
                    link(nc.vector.reciprocal(sw_recip[:, :], sw_total[:, :]))
                    if t == 1:
                        dve.wait_ge(sw_probs_transposed, TILES * layer + t + 1)
                        nc.vector.tensor_copy(sw_pT[:, 1024:2048], banks(TRA, 2)).then_inc(sw_pT_ready, 1)
                    dve.wait_ge(sw_out, TILES * layer + t + 1)
                    nc.vector.tensor_tensor(qkv[:, t, 0:SW].rearrange("p (h d) -> p h d", d=HEAD_DIM),
                                            banks(GATE if t == 0 else 0).rearrange("p (h d) -> p h d", d=HEAD_DIM),
                                            sw_recip[:, :].unsqueeze(2).to_broadcast([P, SW_HEADS, HEAD_DIM]),
                                            ALU.mult).then_inc(yb_ready, 1)
                    dve.wait_ge(ybT_high, TILES * layer + t + 1)
                    low(hT, banks(UP).rearrange("p (h t) -> p h t", h=4),
                        (slice(None), slice(0, 4), slice(t * P, (t + 1) * P))).then_inc(ybT_ready, 1)
                dve.wait_ge(branch_ready, layer + 1)
                keep_up(base + PB_AT)
                dve.wait_ge(units_used, base + PB_AT)
                for t in range(TILES):
                    nc.vector.tensor_tensor(branch[:, t, 0:D], branch[:, t, 0:D], banks(2 * t, 2), ALU.mult)
                keep_up(base + WO_AT)
                dve.wait_ge(units_used, base + WO_AT)
                for t in range(TILES):
                    link(nc.vector.tensor_tensor(branch[:, t, D:2 * D], branch[:, t, D:2 * D], banks(4 + 2 * t, 2), ALU.mult))
                    nc.vector.tensor_tensor(branch[:, t, 0:D], branch[:, t, 0:D], branch[:, t, D:2 * D],
                                            ALU.add).then_inc(merged_ready, 1)
                for g in range(4):
                    dve.wait_ge(mergedT_high, 4 * layer + g + 1)
                    last = low(hT, banks(4 + g).rearrange("p (k t) -> p k t", k=2), (slice(None), slice(2 * g, 2 * g + 2)))
                last.then_inc(mergedT_ready, 1)
                keep_up(base + WO_AT + GATE_UNITS)
                dve.wait_ge(units_used, base + WO_AT + GATE_UNITS)
                add_to_x()

            def add_to_x():
                nc.vector.tensor_tensor(x[:, 0, :], x[:, 0, :], banks(0, 2), ALU.add)
                nc.vector.tensor_tensor(x[:, 1, :], x[:, 1, :], banks(2, 2), ALU.add).then_inc(x_updated, 1)

            def dense():
                for s in range(STEPS):
                    keep_up(DENSE0 + item_gate(s) + G_UNITS)
                    keep_up(DENSE0 + item_up(s) + G_UNITS)
                    dve.wait_ge(units_used, DENSE0 + item_up(s) + G_UNITS)
                    for t in range(TILES):
                        dve.wait_ge(silu_done, TILES * s + t + 1)
                        nc.vector.tensor_tensor(act[t], act[t], banks(6 + t), ALU.mult).then_inc(act_ready, 1)
                    if s:
                        keep_up(DENSE0 + item_down(s - 1) + D_UNITS)
                    for t in range(TILES):
                        dve.wait_ge(actT_high, TILES * s + t + 1)
                        low(innerT, banks(6 + t).rearrange("p (k t) -> p k t", k=4),
                            (slice(None), slice(None), slice(t * P, (t + 1) * P))).then_inc(actT_ready, 1)
                keep_up(PLE0)
                dve.wait_ge(units_used, PLE0)
                add_to_x()

            def route():
                e2 = [P, TILES, EXPERTS, EXPERTS]
                dve.wait_ge(logits_done, 1)
                link(nc.vector.tensor_copy(logits[:, :, :], banks(GATE)[:, 0:TILES * EXPERTS].rearrange("p (t e) -> p t e", t=TILES)))
                other = logits[:, :, :].unsqueeze(2).to_broadcast(e2)
                own = logits[:, :, :].unsqueeze(3).to_broadcast(e2)
                link(nc.vector.reduce_max(top[:, :], logits[:, :, :], AX_X))
                nc.vector.tensor_tensor(gate_w[:, :, :], logits[:, :, :], top[:, :].unsqueeze(2).to_broadcast([P, TILES, EXPERTS]),
                                        ALU.subtract).then_inc(top_ready, 1)
                nc.vector.tensor_tensor(pair_a[:, :, :, :], other, own, ALU.is_gt)
                link(nc.vector.tensor_tensor(pair_b[:, :, :, :], other, own, ALU.is_equal))
                link(nc.vector.tensor_tensor(pair_b[:, :, :, :], pair_b[:, :, :, :],
                                             before[:, :, :].unsqueeze(1).to_broadcast(e2), ALU.mult))
                link(nc.vector.tensor_tensor(pair_a[:, :, :, :], pair_a[:, :, :, :], pair_b[:, :, :, :], ALU.add))
                link(nc.vector.reduce_sum(rank[:, :, :], pair_a[:, :, :, :], AX_X))
                nc.vector.tensor_scalar(chosen[:, :, :], rank[:, :, :], TOP_K - 0.5, None, ALU.is_lt).then_inc(chosen_ready, 1)
                dve.wait_ge(chosen_ready, 1)
                dve.wait_ge(route_exps, 1)
                link(nc.vector.tensor_tensor(gate_w[:, :, :], gate_w[:, :, :], chosen[:, :, :], ALU.mult))
                link(nc.vector.reduce_sum(top[:, :], gate_w[:, :, :], AX_X))
                link(nc.vector.reciprocal(top[:, :], top[:, :]))
                link(nc.vector.tensor_tensor(gate_w[:, :, :], gate_w[:, :, :],
                                             top[:, :].unsqueeze(2).to_broadcast([P, TILES, EXPERTS]), ALU.mult))
                dve.wait_ge(places_done, 1)
                place_ps = banks(UP)[:, 0:TILES * EXPERTS].rearrange("p (t e) -> p t e", t=TILES)
                count_ps = banks(UP)[:, TILES * EXPERTS:(TILES + 1) * EXPERTS]
                nc.vector.scalar_tensor_tensor(place[:, :, :], place_ps, 1.0, chosen[:, :, :], ALU.add, ALU.mult)
                link(nc.vector.tensor_scalar(over[:, :], count_ps, P + 0.5, None, ALU.is_gt))
                pa1 = pair_a[:, 0, :, :]
                link(nc.vector.tensor_tensor(pa1, over[:, :].unsqueeze(1).to_broadcast([P, EXPERTS, EXPERTS]), before[:, :, :], ALU.mult))
                link(nc.vector.reduce_sum(over_before[:, :], pa1, AX_X))
                for r in range(EXTRA):
                    last = nc.vector.scalar_tensor_tensor(extra_of[:, r, :], over_before[:, :], float(r), over[:, :],
                                                          ALU.is_equal, ALU.mult)
                link(last)
                link(nc.vector.reduce_sum(n_items[:, :], over[:, :], AX_X))
                nc.vector.tensor_scalar(n_items_i[:, :], n_items[:, :], float(EXPERTS), None, ALU.add)
                pairs = [P, TILES, EXTRA, EXPERTS]
                extra = extra_of[:, :, :].unsqueeze(1).to_broadcast(pairs)
                link(nc.vector.tensor_tensor(pair_a[:, :, 0:EXTRA, :], place[:, :, :].unsqueeze(2).to_broadcast(pairs), extra, ALU.mult))
                nc.vector.memset(item_place[:, :, ITEMS - 1:ITEMS], -1.0)
                nc.vector.memset(item_gate_w[:, :, ITEMS - 1:ITEMS], 0.0)
                link(nc.vector.tensor_tensor(pair_b[:, :, 0:EXTRA, :], gate_w[:, :, :].unsqueeze(2).to_broadcast(pairs), extra, ALU.mult))
                link(nc.vector.reduce_sum(item_place[:, :, EXPERTS:ITEMS - 1], pair_a[:, :, 0:EXTRA, :], AX_X))
                nc.vector.reduce_sum(item_gate_w[:, :, EXPERTS:ITEMS - 1], pair_b[:, :, 0:EXTRA, :], AX_X)
                nc.vector.tensor_scalar(item_place[:, :, EXPERTS:ITEMS - 1], item_place[:, :, EXPERTS:ITEMS - 1],
                                        -1.0 - P, None, ALU.add)
                nc.vector.tensor_scalar(item_place[:, :, 0:EXPERTS], place[:, :, :], -1.0, None, ALU.add)
                nc.vector.tensor_copy(item_gate_w[:, :, 0:EXPERTS], gate_w[:, :, :])
                nc.vector.memset(item_expert[:, :], 0.0)
                link(nc.vector.tensor_tensor(pair_a[:, 0, 0:EXTRA, :], extra_of[:, :, :],
                                             column[:, 0:EXPERTS].unsqueeze(1).to_broadcast([P, EXTRA, EXPERTS]), ALU.mult))
                nc.vector.tensor_copy(item_expert[:, 0:EXPERTS], column[:, 0:EXPERTS])
                link(nc.vector.reduce_sum(item_expert[:, EXPERTS:ITEMS - 1], pair_a[:, 0, 0:EXTRA, :], AX_X))
                nc.vector.tensor_copy(item_expert_i[:, :], item_expert[:, :]).then_inc(routed, 1)
                dve.wait_ge(routed, 1)

            def make_picks(item):
                for t in range(TILES):
                    where = item_place[:, t, item]
                    nc.vector.tensor_scalar(pick[:, t, :], column[:, :], where, None, ALU.is_equal)
                    last = nc.vector.tensor_scalar(pick_gate[:, t, :], column[:, :], where, item_gate_w[:, t, item],
                                                   ALU.is_equal, ALU.mult)
                last.then_inc(picks_ready, 1)

            def gathered_low(count):
                g0 = FFN_GAIN + KD
                for k in range(KD):
                    dve.wait_ge(gatheredT_high, (count - 1) * KD + k // 4 * 4 + 4)
                    last = nc.vector.scalar_tensor_tensor(hT[1][:, k, 0:P], banks(GATE, 2)[:, k * P:(k + 1) * P],
                                                          params[:, g0 + k:g0 + k + 1], hT[0][:, k, 0:P].bitcast(F32),
                                                          ALU.mult, ALU.subtract)
                last.then_inc(gatheredT_ready, 1)

            def experts():
                route()
                make_picks(slice(0, 1))
                gathered_low(1)
                count = dve.value_load(n_items_i[0:1, 0:1], min_val=EXPERTS, max_val=EXPERTS + EXTRA)
                with dve.Fori(0, count) as t:
                    def actT_low_part(s):
                        dve.wait_ge(item_actT_high, t * STEPS + s + 1)
                        low(innerT, banks(TRA).rearrange("p (k t) -> p k t", k=4),
                            (slice(None), slice(None), slice(0, P))).then_inc(item_actT, 1)

                    for s in range(STEPS):
                        keep_up(MOE + item_gate(s) + G_UNITS, t)
                        if s == 0:
                            dve.wait_ge(pick_transposed, t + 1)
                            nc.vector.tensor_copy(spread, banks(TRB)[:, 0:SEQ]).then_inc(spread_ready, 1)
                        else:
                            actT_low_part(s - 1)
                        keep_up(MOE + item_up(s) + G_UNITS, t)
                        dve.wait_ge(units_used, t * PER_ITEM + MOE + item_up(s) + G_UNITS)
                        dve.wait_ge(item_silu, t * STEPS + s + 1)
                        nc.vector.tensor_tensor(act[s % 2], act[s % 2], banks(UP), ALU.mult).then_inc(item_act, 1)
                        if s == 0:
                            make_picks(bass.ds(t + 1, 1))
                        else:
                            keep_up(MOE + item_down(s - 1) + D_UNITS, t)
                    actT_low_part(STEPS - 1)
                    gathered_low(t + 2)
                    keep_up(MOE + PER_ITEM, t)
                    for half in range(2):
                        dve.wait_ge(item_combined, t * 2 + half + 1)
                        for n in range(TILES):
                            xv = x[:, n, half * BANK:(half + 1) * BANK]
                            last = nc.vector.tensor_tensor(xv, xv, banks((2 if n == 0 else TRA) + half), ALU.add)
                        last.then_inc(item_added, 1)
                split[0] -= PER_ITEM
                return count

            def embedding(layer, items=0):
                base, end = (PLE0, None) if layer == 0 else (MOE, END)
                keep_up(base, items, end)
                dve.wait_ge(pT_high, layer + 1)
                low(inner, banks(GATE), (slice(None), slice(0, PLE * TILES))).then_inc(pT_ready, 1)
                norm(3 * layer + 2, PLE_GAIN + layer * KD, base, items)
                keep_up(base + GATE_UNITS, items, end)
                keep_up(base + GATE_UNITS + 1, items, end)
                dve.wait_ge(units_used, base + GATE_UNITS + 1 + items * PER_ITEM)
                for t in range(TILES):
                    dve.wait_ge(ple_gate_ready, TILES * layer + t + 1)
                    link(nc.vector.tensor_tensor(ple_gate[:, t, :], ple_gate[:, t, :], banks(4 + 2 * t, 2), ALU.mult))
                    last = nc.vector.tensor_tensor(x[:, t, :], x[:, t, :], ple_gate[:, t, :], ALU.add)
                last.then_inc(x_updated, 1)

            keep_up(MIX0)
            constants()
            norm(0, MIX_GAIN, MIX0)
            mixer(0)
            norm(1, FFN_GAIN, DENSE0)
            dense()
            embedding(0)
            norm(3, MIX_GAIN + KD, MIX1)
            mixer(1)
            norm(4, FFN_GAIN + KD, MOE)
            embedding(1, experts())

        @block.tensor
        def _(pe):
            def products(o, x_parts, x_cols, n, width, k, cols, first, last, items=0):
                parts = [a[:, n % SLOTS, :].rearrange("p (k n) -> p k n", n=width)[:, k, cols] for a in (w_hi, w_lo)]
                if k == 0:
                    pe.wait_ge(low_ready, n + 1 + items * PER_ITEM)
                nc.tensor.matmul(o, x_parts[0][x_cols], parts[0], start=first, stop=False)
                nc.tensor.matmul(o, x_parts[0][x_cols], parts[1], start=False, stop=False)
                return nc.tensor.matmul(o, x_parts[1][x_cols], parts[0], start=False, stop=last)

            def mm(o, lhsT, rhs, start, stop):
                return nc.tensor.matmul(o, lhsT, rhs, start=start, stop=stop)

            def transpose_tokens(src, done, ready, ready_at):
                for g in range(4):
                    for kk in range(2):
                        for t in range(TILES):
                            if g == 0 and kk == 0:
                                pe.wait_ge(ready, ready_at + t + 1)
                            k = 2 * g + kk
                            last = nc.tensor.transpose(banks(4 + g)[:, kk * SEQ + t * P:kk * SEQ + (t + 1) * P],
                                                       src[:, t, k * P:(k + 1) * P], ident[:, :])
                    last.then_inc(done, 1)

            def columns(k, t):
                return (slice(None), k, slice(t * P, (t + 1) * P))

            def wide_product(base, n_units, x_parts, bank0, items=0):
                for u in range(n_units):
                    for kk in range(2):
                        k = 2 * u + kk
                        for t in range(TILES):
                            for half in range(2):
                                last = products(banks(bank0 + 2 * t + half), x_parts, columns(k, t), base + u, D, kk,
                                                slice(half * BANK, (half + 1) * BANK), k == 0, k == 2 * n_units - 1, items)
                    last.then_inc(units_used, 1)

            def column_product(n0, width, bank0):
                per = UNIT // width
                for k in range(KD):
                    for t in range(TILES):
                        last = products(banks(bank0 + t)[:, 0:width], hT, columns(k, t), n0 + k // per, width, k % per,
                                        slice(0, width), k == 0, k == KD - 1)
                    if k % per == per - 1:
                        last.then_inc(units_used, 1)

            def project(layer, c):
                if c >= 2:
                    pe.wait_ge(proj_taken, layer * OUTS + 2 * (c - 1))
                column_product(LAYER0[layer] + COLUMN_UNIT[c], IN_COLUMNS[c][1], c % 2 * 2)

            def level_product(layer, g):
                b = GATE if g % 2 == 0 else TRA
                if g >= 2:
                    pe.wait_ge(level_taken, layer * (LEVEL_COUNT + 1) + g - 1)
                if g == 0:
                    pe.wait_ge(q_taken, layer + 1)
                    left, right = kT, qT
                else:
                    pe.wait_ge(level_ready, layer * LEVEL_COUNT + g)
                    left = right = level_tile[(g - 1) % 2]
                if g > 0 and LEVEL_HALF[g - 1] > CHUNK:
                    for h in range(HEADS):
                        last = mm(banks(b)[:, h * P:(h + 1) * P], left[:, h * SEQ:h * SEQ + P],
                                  right[:, h * SEQ + P:(h + 1) * SEQ], True, True)
                else:
                    for n in range(HEADS * TILES):
                        last = mm(banks(b, 2)[:, n * P:(n + 1) * P], left[:, n * P:(n + 1) * P],
                                  right[:, n * P:(n + 1) * P], True, True)
                last.then_inc(level_scores, 1)

            def mixer(layer):
                pe.wait_ge(hT_ready, 3 * layer + 1)
                for c in range(5):
                    project(layer, c)
                for src, b, taken, done in ((f_tok, TRA, 6, f_transposed), (q_tok, GATE, 2, q_transposed)):
                    pe.wait_ge(proj_taken, layer * OUTS + taken)
                    for h in range(HEADS):
                        for t in range(TILES):
                            last = nc.tensor.transpose(banks(b, 2)[:, h * SEQ + t * P:h * SEQ + (t + 1) * P],
                                                       src[:, t, h * P:(h + 1) * P], ident[:, :])
                    last.then_inc(done, 1)
                project(layer, 5)
                project(layer, 6)
                pe.wait_ge(qk_normed, TILES * (layer + 1))
                pe.wait_ge(f_taken, layer + 1)
                pe.wait_ge(q_taken, layer + 1)
                for t in range(TILES):
                    for h in range(4):
                        nc.tensor.transpose(banks(TRA, 2)[:, h * SEQ + t * P:h * SEQ + (t + 1) * P], qkv[:, t, h * P:(h + 1) * P],
                                            ident[:, :])
                    last = nc.tensor.transpose(banks(GATE)[:, t * P:(t + 1) * P], qkv[:, t, SW:SW + KV], ident[:, :])
                last.then_inc(qk_transposed, 1)
                pe.wait_ge(qkT_ready, layer + 1)
                for g in range(LEVEL_COUNT + 1):
                    if g and BLOCKS_BEFORE[g] > BLOCKS_BEFORE[g - 1]:
                        project(layer, BLOCKS_BEFORE[g] - 1)
                    level_product(layer, g)
                pe.wait_ge(level_taken, (layer + 1) * (LEVEL_COUNT + 1))
                pe.wait_ge(proj_taken, (layer + 1) * OUTS)
                for h in range(HEADS):
                    last = mm(banks(0)[:, h * P:(h + 1) * P], sc_tile[:, 2 * h, :], i_tok[:, 0, h * P:(h + 1) * P], True, True)
                last.then_inc(hgrn_out, 1)
                for h in range(HEADS):
                    mm(banks(1)[:, h * P:(h + 1) * P], sc_cross[:, h, :], i_tok[:, 0, h * P:(h + 1) * P], True, False)
                    last = mm(banks(1)[:, h * P:(h + 1) * P], sc_tile[:, 2 * h + 1, :], i_tok[:, 1, h * P:(h + 1) * P], False, True)
                last.then_inc(hgrn_out, 1)

                def attention_scores(t):
                    keys = (t + 1) * P
                    b = banks(2, 2) if t == 0 else banks(0, 4)
                    for h in range(SW_HEADS):
                        kv0 = (h // 4) * HEAD_DIM
                        last = mm(b[:, h * keys:(h + 1) * keys], qbT[kv0:kv0 + HEAD_DIM, h % 4, t * P:(t + 1) * P],
                                  kbT[kv0:kv0 + HEAD_DIM, 0:keys], True, True)
                    last.then_inc(sw_scores, 1)

                def attention_out(t):
                    keys = (t + 1) * P
                    pe.wait_ge(sw_probs, TILES * layer + t + 1)
                    for kb in range(t + 1):
                        for h in range(SW_HEADS):
                            b = banks(TRA if t == 0 else GATE, 2 * (t + 1))
                            last = nc.tensor.transpose(b[:, (kb * SW_HEADS + h) * P:(kb * SW_HEADS + h + 1) * P],
                                                       sw_s[:, h * keys + kb * P:h * keys + (kb + 1) * P], ident[:, :])
                    last.then_inc(sw_probs_transposed, 1)
                    pe.wait_ge(sw_pT_ready, 3 * layer + (1 if t == 0 else 3))
                    b = banks(GATE if t == 0 else 0)
                    for h in range(SW_HEADS):
                        v0 = SW + KV + (h // 4) * HEAD_DIM
                        for kb in range(t + 1):
                            last = mm(b[:, h * HEAD_DIM:(h + 1) * HEAD_DIM],
                                      sw_pT[:, (kb * SW_HEADS + h) * P:(kb * SW_HEADS + h + 1) * P],
                                      qkv[:, kb, v0:v0 + HEAD_DIM], kb == 0, kb == t)
                    last.then_inc(sw_out, 1)
                    pe.wait_ge(yb_ready, TILES * layer + t + 1)
                    for k in range(4):
                        last = nc.tensor.transpose(banks(UP)[:, k * P:(k + 1) * P], qkv[:, t, k * P:(k + 1) * P], ident[:, :])
                    last.then_inc(yb_transposed, 1)

                attention_scores(0)
                pe.wait_ge(ya_ready, layer + 1)
                for h in range(HEADS):
                    for t in range(TILES):
                        last = nc.tensor.transpose(banks(GATE, 2)[:, h * SEQ + t * P:h * SEQ + (t + 1) * P],
                                                   silu_g[:, t, h * P:(h + 1) * P], ident[:, :])
                last.then_inc(ya_transposed, 1)
                pe.wait_ge(yaT_ready, layer + 1)
                attention_out(0)
                attention_scores(1)
                pe.wait_ge(ybT_ready, TILES * layer + 1)
                attention_out(1)
                base = LAYER0[layer]
                wide_product(base + PA_AT, 2, innerT, 0)
                pe.wait_ge(ybT_ready, TILES * (layer + 1))
                wide_product(base + PB_AT, 2, hT, 4)
                transpose_tokens(branch, merged_transposed, merged_ready, TILES * layer)
                pe.wait_ge(mergedT_ready, layer + 1)
                wide_product(base + WO_AT, 4, hT, 0)

            def dense():
                pe.wait_ge(hT_ready, 2)

                def down(s):
                    for k in range(4):
                        for t in range(TILES):
                            for half in range(2):
                                last = products(banks(2 * t + half), innerT, columns(k, t), DENSE0 + item_down(s) + k // 2, D,
                                                k % 2, slice(half * BANK, (half + 1) * BANK), s == 0 and k == 0,
                                                s == STEPS - 1 and k == 3)
                        if k % 2:
                            last.then_inc(units_used, 1)

                for s in range(STEPS):
                    if s:
                        pe.wait_ge(silu_done, TILES * s)
                    column_product(DENSE0 + item_gate(s), BANK, 4)
                    if s:
                        pe.wait_ge(actT_ready, TILES * s)
                    column_product(DENSE0 + item_up(s), BANK, 6)
                    if s:
                        down(s - 1)
                    for t in range(TILES):
                        pe.wait_ge(act_ready, TILES * s + t + 1)
                        for k in range(4):
                            last = nc.tensor.transpose(banks(6 + t)[:, k * P:(k + 1) * P], act[t][:, k * P:(k + 1) * P], ident[:, :])
                        last.then_inc(act_transposed, 1)
                pe.wait_ge(actT_ready, TILES * STEPS)
                down(STEPS - 1)

            def route():
                pe.wait_ge(hT_ready, 5)
                pe.wait_ge(params_loaded, 16 * PARAM_DMAS)
                for t in range(TILES):
                    for k in range(KD):
                        for part in hT:
                            last = mm(banks(GATE)[:, t * EXPERTS:(t + 1) * EXPERTS], part[:, k, t * P:(t + 1) * P].bitcast(F32),
                                      router[:, k, :], k == 0 and part is hT[0], k == KD - 1 and part is hT[1])
                last.then_inc(logits_done, 1)
                pe.wait_ge(chosen_ready, 1)
                b = banks(UP)
                mm(b[:, 0:EXPERTS], later[:, :], chosen[:, 0, :], True, True)
                mm(b[:, EXPERTS:2 * EXPERTS], ones[:, :], chosen[:, 0, :], True, False)
                mm(b[:, EXPERTS:2 * EXPERTS], later[:, :], chosen[:, 1, :], False, True)
                mm(b[:, 2 * EXPERTS:3 * EXPERTS], ones[:, :], chosen[:, 0, :], True, False)
                mm(b[:, 2 * EXPERTS:3 * EXPERTS], ones[:, :], chosen[:, 1, :], False, True).then_inc(places_done, 1)

            def gather(count):
                pe.wait_ge(picks_ready, count)
                for k in range(KD):
                    for t in range(TILES):
                        last = mm(banks(GATE, 2)[:, k * P:(k + 1) * P], normed[:, t, k * P:(k + 1) * P], pick[:, t, :],
                                  t == 0, t == TILES - 1)
                last.then_inc(gathered, 1)

            def experts():
                route()
                pe.wait_ge(routed, 1)
                gather(1)
                count = pe.value_load(n_items_i[0:1, 0:1], min_val=EXPERTS, max_val=EXPERTS + EXTRA)
                with pe.Fori(0, count) as t:
                    def step_product(first_unit, bank):
                        for k in range(KD):
                            last = products(banks(bank), hT, columns(k, 0), MOE + first_unit + k // 4, BANK, k % 4,
                                            slice(0, BANK), k == 0, k == KD - 1, t)
                            if k % 4 == 3:
                                last.then_inc(units_used, 1)

                    def flip(s):
                        pe.wait_ge(item_act, t * STEPS + s + 1)
                        for k in range(4):
                            last = nc.tensor.transpose(banks(TRA)[:, k * P:(k + 1) * P], act[s % 2][:, k * P:(k + 1) * P],
                                                       ident[:, :])
                        last.then_inc(item_act_transposed, 1)

                    def down_tile(s, k, half):
                        return products(banks(half), innerT, columns(k, 0), MOE + item_down(s) + k // 2, D, k % 2,
                                        slice(half * BANK, (half + 1) * BANK), s == 0 and k == 0, s == STEPS - 1 and k == 3, t)

                    pe.wait_ge(gatheredT_ready, t + 1)
                    for s in range(STEPS):
                        if s:
                            pe.wait_ge(item_silu, t * STEPS + s)
                        step_product(item_gate(s), GATE)
                        if s:
                            flip(s - 1)
                        else:
                            pe.wait_ge(item_added, t * 2)
                            for n in range(TILES):
                                last = nc.tensor.transpose(banks(TRB)[:, n * P:(n + 1) * P], pick_gate[:, n, :], ident[:, :])
                            last.then_inc(pick_transposed, 1)
                        step_product(item_up(s), UP)
                        if s:
                            pe.wait_ge(item_actT, t * STEPS + s)
                            for k in range(4):
                                for half in range(2):
                                    last = down_tile(s - 1, k, half)
                                if k % 2:
                                    last.then_inc(units_used, 1)
                    flip(STEPS - 1)
                    gather(t + 2)
                    pe.wait_ge(item_actT, t * STEPS + STEPS)
                    for half in range(2):
                        for k in range(4):
                            last = down_tile(STEPS - 1, k, half)
                        if half == 0:
                            last.then_inc(item_y_done, 1)
                        else:
                            last.then_inc(units_used, D_UNITS)
                    pe.wait_ge(spread_ready, t + 1)
                    for half in range(2):
                        pe.wait_ge(item_y_taken, t * 2 + half + 1)
                        for n in range(TILES):
                            last = mm(banks((2 if n == 0 else TRA) + half), spread[:, n * P:(n + 1) * P],
                                      y_item[:, half * BANK:(half + 1) * BANK], True, True)
                        last.then_inc(item_combined, 1)
                return count

            def embedding(layer, count=0):
                if layer:
                    pe.wait_ge(gatheredT_ready, count + 1)
                pe.wait_ge(p_loaded, 16 * (layer + 1))
                for k in range(PLE // P):
                    for t in range(TILES):
                        last = nc.tensor.transpose(banks(GATE)[:, k * SEQ + t * P:k * SEQ + (t + 1) * P],
                                                   p_tok[:, t, k * P:(k + 1) * P], ident[:, :])
                last.then_inc(p_transposed, 1)
                pe.wait_ge(pT_ready, layer + 1)
                n = 3 * layer + 2
                transpose_tokens(normed, normed_transposed, normed_ready, TILES * n)
                pe.wait_ge(hT_ready, n + 1)
                base = PLE0 if layer == 0 else MOE
                wide_product(base, GATE_UNITS, hT, 0, count)
                wide_product(base + GATE_UNITS, 1, [a[:, :].rearrange("p (k t) -> p k t", k=4) for a in inner], 4, count)

            pe.wait_ge(params_loaded, 16 * PARAM_DMAS)
            pe.wait_ge(vector_constants, 1)
            nc.tensor.transpose(banks(0)[:, 0:PARAM_ROWS], param_rows[0:PARAM_ROWS, :],
                                ident[0:PARAM_ROWS, 0:PARAM_ROWS]).then_inc(params_transposed, 1)
            transpose_tokens(normed, normed_transposed, normed_ready, 0)
            mixer(0)
            transpose_tokens(normed, normed_transposed, normed_ready, TILES)
            dense()
            embedding(0)
            transpose_tokens(normed, normed_transposed, normed_ready, 3 * TILES)
            mixer(1)
            transpose_tokens(normed, normed_transposed, normed_ready, 4 * TILES)
            embedding(1, experts())


_INS = ["x", "p", "lb_logits", "g_mix", "w_in", "q_norm", "k_norm", "sinks", "hgrn_norm", "w_pa", "w_pb", "w_o",
        "g_ffn", "w_dense_gate", "w_dense_up", "w_dense_down", "w_router", "w_moe_gate", "w_moe_up", "w_moe_down",
        "g_ple", "w_ple_gate", "w_ple_up"]


def kernel(**inputs):
    import numpy as _np
    import concourse.bacc as _bacc
    from concourse import mybir as _mybir
    from concourse.bass_utils import run_bass_kernel_spmd as _run

    nc = _bacc.Bacc("TRN2", target_bir_lowering=False, num_devices=1)
    arrays, args = {}, []
    for name in _INS:
        a = _np.ascontiguousarray(inputs[name])
        arrays[f"in_{name}"] = a
        args.append(nc.dram_tensor(f"in_{name}", a.shape, _mybir.dt.from_np(a.dtype), kind="ExternalInput").ap())
    shape = inputs["x"].shape
    args.append(nc.dram_tensor("trunk_out", shape, _mybir.dt.float32, kind="ExternalOutput").ap())
    build_trunk(nc, *args)
    r = _run(nc, [arrays], core_ids=[0])
    return r.results[0]["trunk_out"]
```

```python
from contextlib import ExitStack

import concourse.bass as bass
from concourse import mybir

ALU = mybir.AluOpType
ACT = mybir.ActivationFunctionType
F32 = mybir.dt.float32
F32R = mybir.dt.float32r
I32 = mybir.dt.int32
U8 = mybir.dt.uint8
AX_X = mybir.AxisListType.X

P = 128
BANK = 512
EPS = 1e-6
CHUNK = 64
HEADS = 4
SW_HEADS = 8
KV_HEADS = 2
HEAD_DIM = 64
TOP_K = 2
RAW_SLOTS = 6
SLOTS = 3
UNIT = 2048
MASKED = -1e30
F_LEAST = 1e-19


def build_trunk(nc, x_in, p_in, lb_logits, g_mix, w_in, q_norm, k_norm, sinks, hgrn_norm, w_pa, w_pb, w_o,
                g_ffn, w_dense_gate, w_dense_up, w_dense_down, w_router, w_moe_gate, w_moe_up, w_moe_down,
                g_ple, w_ple_gate, w_ple_up, out):
    _, SEQ, D = x_in.shape
    DEPTH = p_in.shape[0]
    PLE = p_in.shape[3]
    IN = w_in.shape[2]
    D_FF = w_dense_gate.shape[2]
    EXPERTS = w_moe_gate.shape[1]
    TILES = SEQ // P
    KD = D // P
    HW = HEADS * P
    SW = SW_HEADS * HEAD_DIM
    KV = KV_HEADS * HEAD_DIM
    STEPS = D_FF // BANK
    EXTRA = 3
    ITEMS = EXPERTS + EXTRA + 1
    assert DEPTH == 2 and TILES == 2 and D == 1024 and HW == BANK and SW == BANK and D_FF % BANK == 0
    assert PLE == 2 * P and TOP_K * SEQ < (EXTRA + 1) * (P + 1) and KV * 2 == 256
    assert IN == 4 * HW + SW + 2 * KV + 2 * D

    def rows(w, k0, n):
        return w[k0 * P:(k0 + n) * P, :].rearrange("(k p) n -> p k n", p=P)

    F, Q, G, QA, KVA, I, GATES = range(7)
    IN_COLUMNS = [(HW, BANK), (0, BANK), (3 * HW, BANK), (4 * HW, BANK), (4 * HW + SW, 2 * KV), (2 * HW, BANK)]
    COLUMN_BANK = [4, 2, 0, 2, 0, 2, 0, 0, 0, 0]
    IN_COLUMNS += [(4 * HW + SW + 2 * KV + c * BANK, BANK) for c in range(2 * D // BANK)]
    OUTS = len(IN_COLUMNS) * TILES
    PER_STEP = 2 * KD * BANK // UNIT + BANK // P * D // UNIT
    G_UNITS = KD * BANK // UNIT
    D_UNITS = BANK // P * D // UNIT
    PER_ITEM = STEPS * PER_STEP
    assert PER_ITEM % SLOTS == 0 and PER_ITEM % RAW_SLOTS == 0

    def in_units(layer):
        units = []
        for c0, width in IN_COLUMNS:
            per = UNIT // width
            for k0 in range(0, KD, per):
                units.append(rows(w_in[layer], k0, per)[:, :, c0:c0 + width])
        return units

    def wide_units(w):
        return [rows(w, k0, UNIT // D) for k0 in range(0, w.shape[0] // P, UNIT // D)]

    MIX_UNITS = [in_units(i) + wide_units(w_pa[i]) + wide_units(w_pb[i]) + wide_units(w_o[i]) for i in range(DEPTH)]
    PLE_UNITS = [wide_units(w_ple_gate[i]) + wide_units(w_ple_up[i]) for i in range(DEPTH)]
    IN_UNITS = len(in_units(0))
    COLUMN_UNIT = [sum(KD * width // UNIT for _, width in IN_COLUMNS[:c]) for c in range(len(IN_COLUMNS) + 1)]
    GATE_UNITS = D * D // P // UNIT
    PA_AT, PB_AT = IN_UNITS, IN_UNITS + 2
    WO_AT = IN_UNITS + 4

    def column_units(w, step):
        return [rows(w, k0, UNIT // BANK)[:, :, step * BANK:(step + 1) * BANK]
                for k0 in range(0, KD, UNIT // BANK)]

    def down_units(w, step):
        kt = BANK // P
        return [rows(w, step * kt + k0, UNIT // D) for k0 in range(0, kt, UNIT // D)]

    def mixer_units(gate, up, down):
        units = []
        for s in range(STEPS):
            units += column_units(gate, s) + column_units(up, s)
            if s:
                units += down_units(down, s - 1)
        return units + down_units(down, STEPS - 1)

    DENSE_UNITS = mixer_units(w_dense_gate[0], w_dense_up[0], w_dense_down[0])
    MIX0 = 0
    DENSE0 = len(MIX_UNITS[0])
    PLE0 = DENSE0 + len(DENSE_UNITS)
    MIX1 = PLE0 + len(PLE_UNITS[0])
    UP1 = MIX1 + len(MIX_UNITS[1])
    MOE = UP1 + 1
    MIX_AT = [MIX0, MIX1]
    END = MOE + GATE_UNITS
    LEVEL_HALF = [64, 32, 16, 8, 4, 2, 1, 128]
    LEVEL_COUNT = len(LEVEL_HALF)
    TASKS = [(0, 0, 8), (1, 0, 4), (1, 4, 4)]
    OUT_PRODUCTS = 5
    P_BANK = [4, 7]
    OUT_BANK = [2, 2, 6]
    NORM_BANK = [0, 0, 4]

    def item_gate(s):
        return 0 if s == 0 else 2 * G_UNITS + (s - 1) * PER_STEP

    def item_up(s):
        return item_gate(s) + G_UNITS

    def item_down(s):
        return item_up(s + 1) + G_UNITS if s + 1 < STEPS else PER_ITEM - D_UNITS

    with ExitStack() as ctx:
        def sb(name, shape, dt=F32):
            return ctx.enter_context(nc.sbuf_tensor(name, shape, dt))

        def sem(name):
            return ctx.enter_context(nc.semaphore(name))

        raw = sb("raw", [P, RAW_SLOTS, UNIT])
        w_hi = sb("w_hi", [P, SLOTS, UNIT], F32R)
        w_lo = sb("w_lo", [P, SLOTS, UNIT], F32R)
        x = sb("x", [P, TILES, D])
        normed = sb("normed", [P, TILES, D])
        hT = [sb("hT_hi", [P, KD, SEQ], F32R), sb("hT_lo", [P, KD, SEQ], F32R)]
        inner = [sb("inner_hi", [P, 4 * SEQ], F32R), sb("inner_lo", [P, 4 * SEQ], F32R)]
        innerT = [a[:, :].rearrange("p (k t) -> p k t", k=4) for a in inner]
        arena = sb("arena", [P, 4096 + 3584 + 5120 + 1536 + 1280])
        wide = arena[:, 0:4096]
        q_tok = wide[:, 0:1024].rearrange("p (t n) -> p t n", t=TILES)
        f_tok = wide[:, 1024:2048].rearrange("p (t n) -> p t n", t=TILES)
        branch = wide.rearrange("p (t n) -> p t n", t=TILES)
        act = [wide[:, n * BANK:(n + 1) * BANK] for n in range(2)]
        y_item = wide[:, 3072:4096]
        toks = arena[:, 4096:7680]
        silu_g = toks[:, 0:1024].rearrange("p (t n) -> p t n", t=TILES)
        i_tok = toks[:, 1024:2048].rearrange("p (t n) -> p t n", t=TILES)
        qkv = toks[:, 2048:3584].rearrange("p (t n) -> p t n", t=TILES)
        ple_gate = toks[:, 0:2048].rearrange("p (t n) -> p t n", t=TILES)
        deep = arena[:, 7680:12800]
        ple_up = deep[:, 1024:3072].rearrange("p (t n) -> p t n", t=TILES)
        qT, kT, bT = (deep[:, n * 1024:(n + 1) * 1024] for n in range(3))
        level_tile = [deep[:, (3 + n) * 1024:(4 + n) * 1024] for n in range(2)]
        att = normed.rearrange("p t n -> p (t n)")
        sw_s, sw_pT = att[:, 0:1024], att[:, 1024:2048]
        sw_sq = att[:, 0:TILES * (SW + KV)].rearrange("p (t n) -> p t n", t=TILES)
        score_mem = arena[:, 12800:14336]
        sc_tile = score_mem[:, 0:1024].rearrange("p (n t) -> p n t", t=P)
        sc_cross = score_mem[:, 1024:1536].rearrange("p (n t) -> p n t", t=P)
        qk_mem = arena[:, 14336:15616]
        qbT = qk_mem[:, 0:1024].rearrange("p (h t) -> p h t", h=HEADS)
        kbT = qk_mem[:, 1024:1280]
        pick = qk_mem[:, 0:256].rearrange("p (t s) -> p t s", t=TILES)
        pick_gate = qk_mem[:, 256:512].rearrange("p (t s) -> p t s", t=TILES)
        spread = qk_mem[:, 512:768]
        p_tok = sb("p_tok", [P, TILES, PLE])

        ident = sb("ident", [P, P])
        later = sb("later", [P, P])
        ones = sb("ones", [P, P])
        column = sb("column", [P, P])
        LEVELS = [64, 32, 16, 8, 4, 2, 1]
        masks = sb("masks", [P, 1 + len(LEVELS), P], U8)
        int_a = toks[:, 0:P].bitcast(I32)
        int_b = toks[:, P:2 * P].bitcast(I32)
        sw_mask = sb("sw_mask", [P, 2 * P])
        before = sb("before", [P, EXPERTS, EXPERTS])
        param_rows = sb("param_rows", [P, P])
        params = sb("params", [P, P])
        lb = sb("lb", [P, DEPTH, HEADS])
        lb_rest = sb("lb_rest", [P, DEPTH, HEADS])
        lb_tmp = sb("lb_tmp", [P, 6, HEADS])
        sink_row = sb("sink_row", [P, DEPTH, SW_HEADS])
        router_parts = sb("router_parts", [P, KD, 2, EXPERTS], F32R)
        router = deep[:, 0:KD * EXPERTS].rearrange("p (k e) -> p k e", k=KD)
        scratch = [score_mem[:, n * P:(n + 1) * P] for n in range(2)]
        minus_half = sb("minus_half", [P, 32])
        sumsq = sb("sumsq", [P, TILES])
        meansq = sb("meansq", [P, TILES])
        rstd = sb("rstd", [P, TILES])
        head_sumsq = sb("head_sumsq", [P, 20])
        head_meansq = sb("head_meansq", [P, 20])
        head_rstd = sb("head_rstd", [P, 20])
        sw_max = sb("sw_max", [P, SW_HEADS])
        sw_negmax = sb("sw_negmax", [P, SW_HEADS])
        sw_sink = sb("sw_sink", [P, SW_HEADS])
        sw_sum = sb("sw_sum", [P, SW_HEADS])
        sw_total = sb("sw_total", [P, SW_HEADS])
        sw_recip = sb("sw_recip", [P, SW_HEADS])
        logits = sb("logits", [P, TILES, EXPERTS])
        pairs_mem = score_mem[:, 0:2 * TILES * EXPERTS * EXPERTS].rearrange("p (n t e f) -> p n t e f", n=2, t=TILES, e=EXPERTS)
        pair_a, pair_b = pairs_mem[:, 0], pairs_mem[:, 1]
        rank = sb("rank", [P, TILES, EXPERTS])
        chosen = sb("chosen", [P, TILES, EXPERTS])
        gate_w = sb("gate_w", [P, TILES, EXPERTS])
        top = sb("top", [P, TILES])
        place = sb("place", [P, TILES, EXPERTS])
        over = sb("over", [P, EXPERTS])
        over_before = sb("over_before", [P, EXPERTS])
        extra_of = sb("extra_of", [P, EXTRA, EXPERTS])
        item_place = sb("item_place", [P, TILES, ITEMS])
        item_gate_w = sb("item_gate_w", [P, TILES, ITEMS])
        item_expert = sb("item_expert", [P, ITEMS])
        item_expert_i = sb("item_expert_i", [P, ITEMS], I32)
        n_items = sb("n_items", [P, 1])
        n_items_i = sb("n_items_i", [P, 1], I32)

        ps = ctx.enter_context(nc.psum_tensor("ps", [P, 8, BANK], F32))
        GATE, UP, TRA, TRB = 4, 5, 6, 7

        def banks(b, n=1):
            return ps[:, b:b + n, :].rearrange("p b n -> p (b n)")

        x_loaded = sem("x_loaded")
        params_loaded = sem("params_loaded")
        p_loaded = sem("p_loaded")
        raw_filled = [sem(f"raw{s}_filled") for s in range(RAW_SLOTS)]
        high_ready = sem("high_ready")
        low_ready = sem("low_ready")
        units_used = sem("units_used")
        pool_constants = sem("pool_constants")
        vector_constants = sem("vector_constants")
        params_transposed = sem("params_transposed")
        params_ready = sem("params_ready")
        lb_exps = sem("lb_exps")
        lb_diffs = sem("lb_diffs")
        vector_step = sem("vector_step")
        pool_step = sem("pool_step")
        squares_ready = sem("squares_ready")
        rstd_ready = sem("rstd_ready")
        normed_ready = sem("normed_ready")
        x_transposed = sem("x_transposed")
        router_loaded = sem("router_loaded")
        router_high = sem("router_high")
        pb_tile0 = sem("pb_tile0")
        out_tile0 = sem("out_tile0")
        pick_gates_ready = sem("pick_gates_ready")
        hT_high = sem("hT_high")
        hT_ready = sem("hT_ready")
        proj_taken = sem("proj_taken")
        f_transposed = sem("f_transposed")
        f_taken = sem("f_taken")
        f_clamped = sem("f_clamped")
        logf_ready = sem("logf_ready")
        q_transposed = sem("q_transposed")
        q_taken = sem("q_taken")
        sw_squares = sem("sw_squares")
        head_sums = sem("head_sums")
        head_rstds = sem("head_rstds")
        qk_normed = sem("qk_normed")
        qk_transposed = sem("qk_transposed")
        qkT_ready = sem("qkT_ready")
        level_exponents = sem("level_exponents")
        level_exps = sem("level_exps")
        level_ready = sem("level_ready")
        level_scores = sem("level_scores")
        level_taken = sem("level_taken")
        hgrn_out = sem("hgrn_out")
        hgrn_squares = sem("hgrn_squares")
        ya_ready = sem("ya_ready")
        ya_transposed = sem("ya_transposed")
        yaT_high = sem("yaT_high")
        yaT_ready = sem("yaT_ready")
        sw_scores = sem("sw_scores")
        sw_max_ready = sem("sw_max_ready")
        sw_probs = sem("sw_probs")
        sw_probs_transposed = sem("sw_probs_transposed")
        sw_pT_ready = sem("sw_pT_ready")
        sw_out = sem("sw_out")
        yb_ready = sem("yb_ready")
        yb_transposed = sem("yb_transposed")
        ybT_high = sem("ybT_high")
        ybT_ready = sem("ybT_ready")
        branch_ready = sem("branch_ready")
        merged_ready = sem("merged_ready")
        merged_transposed = sem("merged_transposed")
        mergedT_high = sem("mergedT_high")
        mergedT_ready = sem("mergedT_ready")
        x_updated = sem("x_updated")
        silu_done = sem("silu_done")
        act_ready = sem("act_ready")
        act_transposed = sem("act_transposed")
        actT_high = sem("actT_high")
        actT_ready = sem("actT_ready")
        logits_done = sem("logits_done")
        top_ready = sem("top_ready")
        route_exps = sem("route_exps")
        chosen_ready = sem("chosen_ready")
        places_done = sem("places_done")
        routed = sem("routed")
        picks_ready = sem("picks_ready")
        gathered = sem("gathered")
        gatheredT_high = sem("gatheredT_high")
        gatheredT_ready = sem("gatheredT_ready")
        pick_transposed = sem("pick_transposed")
        spread_ready = sem("spread_ready")
        item_silu = sem("item_silu")
        item_act = sem("item_act")
        item_act_transposed = sem("item_act_transposed")
        item_actT_high = sem("item_actT_high")
        item_actT = sem("item_actT")
        item_y_done = sem("item_y_done")
        item_y_taken = sem("item_y_taken")
        item_combined = sem("item_combined")
        item_added = [sem(f"item_added{half}") for half in range(2)]
        p_transposed = sem("p_transposed")
        pT_high = sem("pT_high")
        pT_ready = sem("pT_ready")
        ple_gate_ready = sem("ple_gate_ready")
        ple_up_tile0 = sem("ple_up_tile0")
        ple_up_taken = sem("ple_up_taken")
        stored = sem("stored")

        MIX_GAIN, FFN_GAIN, PLE_GAIN = 0, DEPTH * KD, 2 * DEPTH * KD
        HGRN_GAIN = 3 * DEPTH * KD
        LB_AT = HGRN_GAIN + DEPTH * HEADS
        Q_GAIN = LB_AT + DEPTH * HEADS
        K_GAIN = Q_GAIN + DEPTH
        PARAM_ROWS = K_GAIN + DEPTH
        PARAM_DMAS = 3 + 2 + 4

        block = ctx.enter_context(nc.Block())

        @block.sync
        def _(sp):
            for t in range(TILES):
                sp.dma_start(x[:, t, :], x_in[0, t * P:(t + 1) * P, :]).then_inc(x_loaded, 16)

            def load_unit(n, source, items=0):
                if n >= RAW_SLOTS:
                    sp.wait_ge(low_ready, n - RAW_SLOTS + 1 + items * PER_ITEM)
                k = source.shape[1]
                dst = raw[:, n % RAW_SLOTS, :].rearrange("p (k n) -> p k n", k=k)
                sp.dma_start(dst, source).then_inc(raw_filled[n % RAW_SLOTS], 16)

            load_unit(0, MIX_UNITS[0][0])
            for base, w in ((MIX_GAIN, g_mix), (FFN_GAIN, g_ffn), (PLE_GAIN, g_ple)):
                sp.dma_start(param_rows[base:base + DEPTH * KD, :],
                             w.rearrange("l (k p) -> (l k) p", p=P)).then_inc(params_loaded, 16)
            for base, w in ((HGRN_GAIN, hgrn_norm), (LB_AT, lb_logits)):
                sp.dma_start(param_rows[base:base + DEPTH * HEADS, :],
                             w.rearrange("l (h p) -> (l h) p", p=P)).then_inc(params_loaded, 16)
            for base, w in ((Q_GAIN, q_norm), (K_GAIN, k_norm)):
                for half in range(2):
                    sp.dma_start(param_rows[base:base + DEPTH, half * HEAD_DIM:(half + 1) * HEAD_DIM],
                                 w).then_inc(params_loaded, 16)
            load_unit(1, MIX_UNITS[0][1])
            sp.dma_start(router[:, :, :], w_router[0].rearrange("(k p) e -> p k e", p=P)).then_inc(router_loaded, 16)
            sp.dma_start(sink_row[:, :, :], sinks.unsqueeze(0).to_broadcast([P, DEPTH, SW_HEADS])).then_inc(router_loaded, 16)

            def load_p(layer):
                sp.dma_start(p_tok[:, :, :], p_in[layer, 0].rearrange("(t p) d -> p t d", p=P)).then_inc(p_loaded, 16)

            load_p(0)
            for n, source in list(enumerate(MIX_UNITS[0] + DENSE_UNITS + PLE_UNITS[0]))[2:]:
                load_unit(n, source)
            sp.wait_ge(p_transposed, 1)
            load_p(1)
            for n, source in enumerate(MIX_UNITS[1] + PLE_UNITS[1][GATE_UNITS:]):
                load_unit(MIX1 + n, source)
            for n, source in enumerate(mixer_units(w_moe_gate[0, 0], w_moe_up[0, 0], w_moe_down[0, 0])):
                load_unit(MOE + n, source)
            sp.wait_ge(routed, 1)
            count = sp.value_load(n_items_i[0:1, 0:1], min_val=EXPERTS, max_val=EXPERTS + EXTRA)
            with sp.Fori(1, count) as t:
                e = sp.value_load(item_expert_i[0:1, bass.ds(t, 1)], min_val=0, max_val=EXPERTS - 1)

                def expert(w):
                    return w[0, bass.ds(e, 1), :, :].rearrange("e k n -> (e k) n")

                for n, source in enumerate(mixer_units(expert(w_moe_gate), expert(w_moe_up), expert(w_moe_down))):
                    load_unit(MOE + n, source, t)
            for n, source in enumerate(PLE_UNITS[1][:GATE_UNITS]):
                load_unit(MOE + n, source, count)
            for t in range(TILES):
                sp.wait_ge(x_updated, TILES * 4 + t + 1)
                sp.dma_start(out[0, t * P:(t + 1) * P, :], x[:, t, :]).then_inc(stored, 16)
            sp.wait_ge(stored, 16 * TILES)

        @block.gpsimd
        def _(pool):
            steps = [0]

            def link(ins):
                steps[0] += 1
                ins.then_inc(pool_step, 1)
                pool.wait_ge(pool_step, steps[0])

            nc.gpsimd.memset(minus_half[:, :], -0.5)
            nc.gpsimd.memset(ones[:, :], 1.0)
            link(nc.gpsimd.memset(before[:, :, :], 1.0))
            nc.gpsimd.affine_select(out=before[:, :, :], in_=before[:, :, :], pattern=[[1, EXPERTS], [-1, EXPERTS]],
                                    compare_op=ALU.is_gt, fill=0.0, base=0, channel_multiplier=0)
            nc.gpsimd.iota(int_a, pattern=[[1, P]], base=0, channel_multiplier=0)
            nc.gpsimd.iota(int_b, pattern=[[0, P]], base=0, channel_multiplier=1).then_inc(pool_constants, 1)

            def norm_rstd(n):
                pool.wait_ge(squares_ready, TILES * (n + 1))
                link(nc.gpsimd.tensor_scalar(meansq[:, :], sumsq[:, :], 1.0 / D, EPS, ALU.mult, ALU.add))
                nc.gpsimd.tensor_tensor(rstd[:, :], meansq[:, :], minus_half[:, 0:TILES], ALU.pow).then_inc(rstd_ready, 1)

            def heads_rstd(n, heads, width):
                pool.wait_ge(head_sums, n + 1)
                link(nc.gpsimd.tensor_scalar(head_meansq[:, 0:heads], head_sumsq[:, 0:heads], 1.0 / width, EPS,
                                             ALU.mult, ALU.add))
                nc.gpsimd.tensor_tensor(head_rstd[:, 0:heads], head_meansq[:, 0:heads], minus_half[:, 0:heads],
                                        ALU.pow).then_inc(head_rstds, 1)

            for layer in range(DEPTH):
                norm_rstd(3 * layer)
                heads_rstd(2 * layer, TILES * (SW_HEADS + KV_HEADS), HEAD_DIM)
                heads_rstd(2 * layer + 1, TILES * HEADS, P)
                norm_rstd(3 * layer + 1)
                norm_rstd(3 * layer + 2)

        @block.scalar
        def _(act_e):
            split = [0]

            def keep_up(used, items=0, end=None):
                while split[0] < (used + SLOTS if end is None else min(used + SLOTS, end)):
                    n = split[0]
                    act_e.wait_ge(raw_filled[n % RAW_SLOTS], 16 * (n // RAW_SLOTS + 1) + items * (16 * PER_ITEM // RAW_SLOTS))
                    if n >= SLOTS:
                        act_e.wait_ge(units_used, n - SLOTS + 1 + items * PER_ITEM)
                    nc.scalar.activation(w_hi[:, n % SLOTS, :], raw[:, n % RAW_SLOTS, :], ACT.Copy).then_inc(high_ready, 1)
                    split[0] += 1

            def take_p(layer):
                act_e.wait_ge(p_transposed, layer + 1)
                nc.scalar.activation(inner[0][:, 0:PLE * TILES], banks(P_BANK[layer]), ACT.Copy).then_inc(pT_high, 1)

            def norm(n, gain, used, items=0):
                for k in range(KD):
                    if k % 2 == 0:
                        act_e.wait_ge(x_transposed, 4 * n + k // 2 + 1)
                    nc.scalar.activation(hT[0][:, k, :], banks(NORM_BANK[n % 3] + k // 2)[:, k % 2 * SEQ:(k % 2 + 1) * SEQ],
                                         ACT.Copy, scale=params[:, gain + k:gain + k + 1]).then_inc(hT_high, 1)
                if n == 4:
                    take_p(1)
                else:
                    keep_up(used, items, END if n == 5 else None)
                for t in range(TILES):
                    nc.scalar.activation(normed[:, t, :], x[:, t, :], ACT.Square,
                                         accum_out=sumsq[:, t:t + 1]).then_inc(squares_ready, 1)
                keep_up(used, items, END if n == 5 else None)

            def mixer(layer):
                base = MIX_AT[layer]
                tasks = len(TASKS) * layer

                def take(c, dst, func, of_heads=False):
                    used = base + COLUMN_UNIT[c + 1]
                    keep_up(used - 1)
                    act_e.wait_ge(units_used, used)
                    for t in range(TILES):
                        src = banks(COLUMN_BANK[c] + t)[:, 0:IN_COLUMNS[c][1]]
                        if of_heads:
                            src = src.rearrange("p (g h d) -> p g h d", g=KV_HEADS, d=HEAD_DIM)
                        nc.scalar.activation(dst(t), src, func, scale=rstd[:, t:t + 1]).then_inc(proj_taken, 1)

                def take_gates(c):
                    take(c, lambda t: branch[:, t, (c - GATES) * BANK:(c - GATES + 1) * BANK], ACT.Copy)

                def level_exp(j):
                    act_e.wait_ge(level_exponents, layer * LEVEL_COUNT + j + 1)
                    nc.scalar.activation(level_tile[j % 2], level_tile[j % 2], ACT.Exp).then_inc(level_exps, 1)

                def softmax_exp(a):
                    _, h0, heads = TASKS[a]
                    act_e.wait_ge(sw_max_ready, tasks + a + 1)
                    nc.scalar.activation(sw_sink[:, h0:h0 + heads], sw_sink[:, h0:h0 + heads], ACT.Exp)
                    keys = 1024 // heads
                    for h in range(heads):
                        last = nc.scalar.activation(sw_s[:, h * keys:(h + 1) * keys], sw_s[:, h * keys:(h + 1) * keys],
                                                    ACT.Exp, bias=sw_negmax[:, h0 + h:h0 + h + 1],
                                                    accum_out=sw_sum[:, h0 + h:h0 + h + 1])
                    last.then_inc(sw_probs, 1)

                def take_probs(a):
                    act_e.wait_ge(sw_probs_transposed, tasks + a + 1)
                    nc.scalar.activation(sw_pT, banks(2, 2), ACT.Copy).then_inc(sw_pT_ready, 1)

                act_e.wait_ge(rstd_ready, 3 * layer + 1)
                take(F, lambda t: f_tok[:, t, :], ACT.Sigmoid)
                take(Q, lambda t: q_tok[:, t, :], ACT.Silu)
                take(G, lambda t: silu_g[:, t, :], ACT.Silu)
                act_e.wait_ge(f_clamped, layer + 1)
                nc.scalar.activation(level_tile[0], level_tile[0], ACT.Ln).then_inc(logf_ready, 1)
                take(QA, lambda t: qkv[:, t, 0:SW].rearrange("p (h g d) -> p g h d", g=KV_HEADS, d=HEAD_DIM), ACT.Copy, True)
                level_exp(0)
                level_exp(1)
                take(KVA, lambda t: qkv[:, t, SW:SW + 2 * KV], ACT.Copy)
                act_e.wait_ge(proj_taken, layer * OUTS + TILES * (KVA + 1))
                nc.scalar.activation(sw_sq[:, :, :], qkv[:, :, 0:SW + KV], ACT.Square).then_inc(sw_squares, 1)
                level_exp(2)
                keep_up(base + 9)
                level_exp(3)
                take(I, lambda t: i_tok[:, t, :], ACT.Copy)
                level_exp(4)
                level_exp(5)
                keep_up(base + 11)
                take_gates(GATES)
                level_exp(6)
                softmax_exp(0)
                level_exp(7)
                keep_up(base + 13)
                take_probs(0)
                take_gates(GATES + 1)
                keep_up(base + 15)
                softmax_exp(1)
                act_e.wait_ge(hgrn_out, TILES * (layer + 1))
                nc.scalar.activation(level_tile[0], banks(TRA, 2), ACT.Square).then_inc(hgrn_squares, 1)
                take_probs(1)
                take_gates(GATES + 2)
                softmax_exp(2)
                keep_up(base + 17)
                act_e.wait_ge(ya_transposed, layer + 1)
                g0 = HGRN_GAIN + layer * HEADS
                for h in range(HEADS):
                    nc.scalar.activation(innerT[0][:, h, :], banks(GATE, 2)[:, h * SEQ:(h + 1) * SEQ], ACT.Copy,
                                         scale=params[:, g0 + h:g0 + h + 1]).then_inc(yaT_high, 1)
                take_probs(2)
                take_gates(GATES + 3)
                keep_up(base + 19)
                for h in range(2):
                    act_e.wait_ge(yb_transposed, 2 * layer + h + 1)
                    nc.scalar.activation(hT[0][:, 2 * h:2 * h + 2, :], banks(GATE + h).rearrange("p (h t) -> p h t", h=2),
                                         ACT.Copy).then_inc(ybT_high, 1)
                nc.scalar.activation(branch[:, :, 0:D], branch[:, :, 0:D], ACT.Sigmoid).then_inc(branch_ready, 1)
                keep_up(base + PB_AT)
                nc.scalar.activation(branch[:, :, D:2 * D], branch[:, :, D:2 * D], ACT.Sigmoid).then_inc(branch_ready, 1)
                keep_up(base + WO_AT - 1)
                for g in range(4):
                    act_e.wait_ge(merged_transposed, 4 * layer + g + 1)
                    nc.scalar.activation(hT[0][:, 2 * g:2 * g + 2, :], banks(g).rearrange("p (k t) -> p k t", k=2),
                                         ACT.Copy).then_inc(mergedT_high, 1)
                keep_up(base + WO_AT + GATE_UNITS - 1)

            def dense():
                act_e.wait_ge(rstd_ready, 2)
                for s in range(STEPS):
                    keep_up(DENSE0 + item_gate(s) + G_UNITS - 1)
                    act_e.wait_ge(units_used, DENSE0 + item_gate(s) + G_UNITS)
                    for t in range(TILES):
                        nc.scalar.activation(act[t], banks(4 + t), ACT.Silu, scale=rstd[:, t:t + 1]).then_inc(silu_done, 1)
                    keep_up(DENSE0 + (item_down(s - 1) + D_UNITS if s else item_up(s) + G_UNITS) - 1)
                    for t in range(TILES):
                        act_e.wait_ge(act_transposed, TILES * s + t + 1)
                        nc.scalar.activation(innerT[0][:, :, t * P:(t + 1) * P], banks(6 + t).rearrange("p (k t) -> p k t", k=4),
                                             ACT.Copy).then_inc(actT_high, 1)
                keep_up(PLE0 - 1)

            def take_ple_up(t):
                if t == 0:
                    act_e.wait_ge(ple_up_tile0, 1)
                else:
                    act_e.wait_ge(units_used, UP1 + 1)
                nc.scalar.activation(ple_up[:, t, :], banks(2 * t, 2), ACT.Copy).then_inc(ple_up_taken, 1)

            def experts():
                act_e.wait_ge(rstd_ready, 5)
                for t in range(TILES):
                    nc.scalar.activation(normed[:, t, :], x[:, t, :], ACT.Copy, scale=rstd[:, t:t + 1]).then_inc(normed_ready, 1)
                act_e.wait_ge(top_ready, 1)
                nc.scalar.activation(gate_w[:, :, :], gate_w[:, :, :], ACT.Exp).then_inc(route_exps, 1)
                for t in range(TILES):
                    take_ple_up(t)

                def gathered_high(count):
                    for k in range(KD):
                        if k % 4 == 0:
                            act_e.wait_ge(gathered, count * 2 + (k // 4 - 1))
                        nc.scalar.activation(hT[0][:, k, 0:P], banks(GATE, 2)[:, k * P:(k + 1) * P], ACT.Copy,
                                             scale=params[:, FFN_GAIN + KD + k:FFN_GAIN + KD + k + 1]).then_inc(gatheredT_high, 1)

                gathered_high(1)
                keep_up(MOE)
                act_e.wait_ge(routed, 1)
                count = act_e.value_load(n_items_i[0:1, 0:1], min_val=EXPERTS, max_val=EXPERTS + EXTRA)
                with act_e.Fori(0, count) as t:
                    def actT_high_part(s):
                        act_e.wait_ge(item_act_transposed, t * STEPS + s + 1)
                        nc.scalar.activation(innerT[0][:, :, 0:P], banks(TRA).rearrange("p (k t) -> p k t", k=4),
                                             ACT.Copy).then_inc(item_actT_high, 1)

                    for s in range(STEPS):
                        keep_up(MOE + item_gate(s) + G_UNITS, t)
                        act_e.wait_ge(units_used, t * PER_ITEM + MOE + item_gate(s) + G_UNITS)
                        nc.scalar.activation(act[s % 2], banks(GATE), ACT.Silu).then_inc(item_silu, 1)
                        if s:
                            actT_high_part(s - 1)
                        keep_up(MOE + item_up(s) + G_UNITS, t)
                        if s:
                            keep_up(MOE + item_down(s - 1) + D_UNITS - (s == STEPS - 1), t)
                    actT_high_part(STEPS - 1)
                    gathered_high(t + 2)
                    for half in range(2):
                        if half == 0:
                            act_e.wait_ge(item_y_done, t + 1)
                        else:
                            act_e.wait_ge(units_used, t * PER_ITEM + MOE + PER_ITEM)
                        nc.scalar.activation(y_item[:, half * BANK:(half + 1) * BANK], banks(half),
                                             ACT.Copy).then_inc(item_y_taken, 1)
                    keep_up(MOE + PER_ITEM, t)
                split[0] -= PER_ITEM
                return count

            def embedding(layer, items=0):
                base, end = (PLE0, None) if layer == 0 else (MOE, END)
                norm(3 * layer + 2, PLE_GAIN + layer * KD, base, items)
                if layer == 0:
                    take_p(0)
                nc.scalar.activation(lb_tmp[:, 0, :], ones[:, 0:HEADS], ACT.Sigmoid)
                keep_up(base + GATE_UNITS - 1, items, end)
                act_e.wait_ge(rstd_ready, 3 * layer + 3)
                for t in range(TILES):
                    if layer and t == 0:
                        act_e.wait_ge(out_tile0, OUT_PRODUCTS)
                    else:
                        act_e.wait_ge(units_used, base + GATE_UNITS + items * PER_ITEM)
                    nc.scalar.activation(ple_gate[:, t, :], banks(2 * t, 2), ACT.Sigmoid,
                                         scale=rstd[:, t:t + 1]).then_inc(ple_gate_ready, 1)

            act_e.wait_ge(pool_constants, 1)
            nc.scalar.activation(lb_tmp[:, 0, :], ones[:, 0:HEADS], ACT.Copy)
            keep_up(MIX0 + 1 - SLOTS)
            act_e.wait_ge(params_ready, 1)
            norm(0, MIX_GAIN, MIX0)
            act_e.wait_ge(router_loaded, 32)
            nc.scalar.activation(router_parts[:, :, 0, :], router[:, :, :], ACT.Copy).then_inc(router_high, 1)
            keep_up(MIX0 + 1)
            act_e.wait_ge(lb_diffs, 1)
            nc.scalar.activation(lb_tmp[:, 1:3, :], lb_tmp[:, 1:3, :], ACT.Exp).then_inc(lb_exps, 1)
            mixer(0)
            norm(1, FFN_GAIN, DENSE0)
            dense()
            embedding(0)
            norm(3, MIX_GAIN + KD, MIX1)
            mixer(1)
            norm(4, FFN_GAIN + KD, UP1)
            embedding(1, experts())

        @block.vector
        def _(dve):
            steps = [0]

            def link(ins):
                steps[0] += 1
                ins.then_inc(vector_step, 1)
                dve.wait_ge(vector_step, steps[0])

            split = [0]

            def keep_up(used, items=0, end=None):
                while split[0] < (used + SLOTS if end is None else min(used + SLOTS, end)):
                    n = split[0]
                    dve.wait_ge(high_ready, n + 1 + items * PER_ITEM)
                    nc.vector.tensor_tensor(w_lo[:, n % SLOTS, :], raw[:, n % RAW_SLOTS, :],
                                            w_hi[:, n % SLOTS, :].bitcast(F32), ALU.subtract).then_inc(low_ready, 1)
                    split[0] += 1

            def low(part, full, cols):
                return nc.vector.tensor_tensor(part[1][cols], full, part[0][cols].bitcast(F32), ALU.subtract)

            def first_constants():
                dve.wait_ge(pool_constants, 1)
                nc.vector.tensor_tensor(ident[:, :], int_a, int_b, ALU.is_equal).then_inc(vector_constants, 1)
                dve.wait_ge(params_transposed, 1)
                nc.vector.memset(sw_mask[:, :], 0.0)
                nc.vector.tensor_copy(params[:, 0:PARAM_ROWS], banks(TRB)[:, 0:PARAM_ROWS]).then_inc(params_ready, 1)
                dve.wait_ge(params_ready, 1)

            def constants():
                nc.vector.memset(sw_mask[0:CHUNK, 0:CHUNK], MASKED)
                nc.vector.memset(sw_mask[0:CHUNK, 3 * CHUNK:4 * CHUNK], MASKED)
                nc.vector.memset(sw_mask[CHUNK:P, 0:2 * CHUNK], MASKED)
                nc.vector.tensor_copy(column[:, :], int_a)
                link(nc.vector.tensor_tensor(later[:, :], int_a, int_b, ALU.is_gt))
                nc.vector.tensor_copy(masks[:, 0, :], ident[:, :])
                link(nc.vector.tensor_tensor(int_a, int_a, int_b, ALU.bitwise_xor))
                link(nc.vector.tensor_copy(scratch[0], int_a))
                link(nc.vector.tensor_tensor(scratch[0], scratch[0], later[:, :], ALU.mult))
                for n, half in enumerate(LEVELS):
                    link(nc.vector.tensor_scalar(scratch[1], scratch[0], float(half), None, ALU.is_ge))
                    link(nc.vector.scalar_tensor_tensor(masks[:, 1 + n, :], scratch[0], float(2 * half), scratch[1],
                                                        ALU.is_lt, ALU.mult))
                keep_up(MIX0 + 1)
                dve.wait_ge(router_high, 1)
                nc.vector.tensor_tensor(router_parts[:, :, 1, :], router[:, :, :], router_parts[:, :, 0, :].bitcast(F32), ALU.subtract)
                l0 = params[:, LB_AT:LB_AT + HEADS]
                l1 = params[:, LB_AT + HEADS:LB_AT + 2 * HEADS]
                link(nc.vector.tensor_tensor(lb_tmp[:, 0, :], l0, l1, ALU.max))
                nc.vector.tensor_tensor(lb_tmp[:, 1, :], l0, lb_tmp[:, 0, :], ALU.subtract)
                nc.vector.tensor_tensor(lb_tmp[:, 2, :], l1, lb_tmp[:, 0, :], ALU.subtract).then_inc(lb_diffs, 1)
                dve.wait_ge(lb_exps, 1)
                link(nc.vector.tensor_tensor(lb_tmp[:, 3, :], lb_tmp[:, 1, :], lb_tmp[:, 2, :], ALU.add))
                link(nc.vector.reciprocal(lb_tmp[:, 3, :], lb_tmp[:, 3, :]))
                link(nc.vector.tensor_tensor(lb_tmp[:, 4, :], lb_tmp[:, 1, :], lb_tmp[:, 3, :], ALU.mult))
                link(nc.vector.tensor_tensor(lb_tmp[:, 5, :], lb_tmp[:, 2, :], lb_tmp[:, 3, :], ALU.mult))
                link(nc.vector.tensor_tensor(lb_tmp[:, 5, :], lb_tmp[:, 4, :], lb_tmp[:, 5, :], ALU.add))
                nc.vector.tensor_tensor(lb[:, 0, :], lb_tmp[:, 4, :], lb_tmp[:, 4, :], ALU.subtract)
                link(nc.vector.tensor_tensor(lb[:, 1, :], lb_tmp[:, 5, :], lb_tmp[:, 4, :], ALU.subtract))
                link(nc.vector.tensor_scalar(lb_rest[:, :, :], lb[:, :, :], -1.0, 1.0, ALU.mult, ALU.add))

            def norm_low(n, gain):
                for k in range(KD):
                    dve.wait_ge(hT_high, KD * n + k // 2 * 2 + 2)
                    last = nc.vector.scalar_tensor_tensor(hT[1][:, k, :],
                                                          banks(NORM_BANK[n % 3] + k // 2)[:, k % 2 * SEQ:(k % 2 + 1) * SEQ],
                                                          params[:, gain + k:gain + k + 1], hT[0][:, k, :].bitcast(F32),
                                                          ALU.mult, ALU.subtract)
                    if k % 2:
                        last.then_inc(hT_ready, 1)

            def exponents(j):
                half = LEVEL_HALF[j]
                e = level_tile[j % 2]
                if half <= CHUNK:
                    ev = e.rearrange("p (n s j) -> p n s j", s=2, j=half)
                    bv = bT.rearrange("p (n s j) -> p n s j", s=2, j=half)
                    n = bv.shape[1]
                    mid = bv[:, :, 0, half - 1:half].to_broadcast([P, n, half])
                    nc.vector.tensor_tensor(ev[:, :, 0, :], mid, bv[:, :, 0, :], ALU.subtract)
                    if half < CHUNK:
                        last = nc.vector.tensor_tensor(ev[:, :, 1, :], bv[:, :, 1, :], mid, ALU.subtract)
                    else:
                        last = nc.vector.tensor_copy(ev[:, :, 1, :], bv[:, :, 1, :])
                else:
                    ev = e.rearrange("p (h c j) -> p h c j", h=HEADS, c=4)
                    bv = bT.rearrange("p (h c j) -> p h c j", h=HEADS, c=4)

                    def end(c):
                        return bv[:, :, c, CHUNK - 1:CHUNK].to_broadcast([P, HEADS, CHUNK])

                    nc.vector.tensor_tensor(ev[:, :, 0, :], end(0), bv[:, :, 0, :], ALU.subtract)
                    nc.vector.tensor_tensor(ev[:, :, 1, :], end(1), bv[:, :, 1, :], ALU.subtract)
                    nc.vector.tensor_copy(ev[:, :, 2, :], bv[:, :, 2, :])
                    link(nc.vector.tensor_tensor(ev[:, :, 3, :], bv[:, :, 3, :], end(2), ALU.add))
                    last = nc.vector.tensor_tensor(ev[:, :, 0, :], ev[:, :, 0, :], end(1), ALU.add)
                last.then_inc(level_exponents, 1)

            def weigh(layer, j):
                half = LEVEL_HALF[j]
                dve.wait_ge(level_exps, layer * LEVEL_COUNT + j + 1)
                ev, kv, qv = (a.rearrange("p (n s j) -> p n s j", s=2, j=half) for a in (level_tile[j % 2], kT, qT))
                nc.vector.tensor_tensor(ev[:, :, 0, :], ev[:, :, 0, :], kv[:, :, 0, :], ALU.mult)
                nc.vector.tensor_tensor(ev[:, :, 1, :], ev[:, :, 1, :], qv[:, :, 1, :], ALU.mult).then_inc(level_ready, 1)

            def keep_scores(layer, g):
                dve.wait_ge(level_scores, layer * (LEVEL_COUNT + 1) + g + 1)
                if g:
                    dve.wait_ge(level_taken, layer * (LEVEL_COUNT + 1) + g)
                src = banks(GATE if g % 2 == 0 else TRA, 2)
                if g > 0 and LEVEL_HALF[g - 1] > CHUNK:
                    ins = nc.vector.tensor_copy(sc_cross[:, :, :], src[:, 0:HEADS * P].rearrange("p (n t) -> p n t", t=P))
                else:
                    m = 0 if g == 0 else 1 + LEVELS.index(LEVEL_HALF[g - 1])
                    ins = nc.vector.copy_predicated(sc_tile[:, :, :],
                                                    masks[:, m:m + 1, :].to_broadcast([P, HEADS * TILES, P]),
                                                    src.rearrange("p (n t) -> p n t", t=P))
                ins.then_inc(level_taken, 1)

            def level_step(layer, g):
                if g < LEVEL_COUNT:
                    weigh(layer, g)
                dve.wait_ge(level_scores, layer * (LEVEL_COUNT + 1) + g + 1)
                if 0 < g < LEVEL_COUNT - 1:
                    exponents(g + 1)
                keep_scores(layer, g)

            def softmax_max(layer, a):
                t, h0, heads = TASKS[a]
                dve.wait_ge(sw_scores, len(TASKS) * layer + a + 1)
                sv = sw_s.rearrange("p (h k) -> p h k", h=heads)
                src = banks(2, 2).rearrange("p (h k) -> p h k", h=heads)
                hs = slice(h0, h0 + heads)
                sink = sink_row[:, layer, hs]
                link(nc.vector.tensor_tensor(sv, src, sw_mask[:, P - t * P:2 * P].unsqueeze(1).to_broadcast([P, heads, (t + 1) * P]),
                                             ALU.add))
                link(nc.vector.reduce_max(sw_max[:, hs], sv, AX_X))
                link(nc.vector.tensor_tensor(sw_max[:, hs], sw_max[:, hs], sink, ALU.max))
                nc.vector.tensor_scalar(sw_negmax[:, hs], sw_max[:, hs], -1.0, None, ALU.mult)
                nc.vector.tensor_tensor(sw_sink[:, hs], sink, sw_max[:, hs], ALU.subtract).then_inc(sw_max_ready, 1)

            def attention_norm(layer, a):
                t, h0, heads = TASKS[a]
                hs = slice(h0, h0 + heads)
                dve.wait_ge(sw_probs, len(TASKS) * layer + a + 1)
                link(nc.vector.tensor_tensor(sw_total[:, hs], sw_sum[:, hs], sw_sink[:, hs], ALU.add))
                link(nc.vector.reciprocal(sw_recip[:, hs], sw_total[:, hs]))
                dve.wait_ge(sw_out, len(TASKS) * layer + a + 1)
                width = heads * HEAD_DIM
                nc.vector.tensor_tensor(qkv[:, t, h0 * HEAD_DIM:h0 * HEAD_DIM + width].rearrange("p (h d) -> p h d", d=HEAD_DIM),
                                        banks(OUT_BANK[a])[:, 0:width].rearrange("p (h d) -> p h d", d=HEAD_DIM),
                                        sw_recip[:, hs].unsqueeze(2).to_broadcast([P, heads, HEAD_DIM]),
                                        ALU.mult).then_inc(yb_ready, 1)

            def mixer(layer):
                base = MIX_AT[layer]
                lf = level_tile[0]
                reset = level_tile[1]
                link(nc.vector.memset(reset, 1.0))
                nc.vector.memset(reset.rearrange("p (n j) -> p n j", j=CHUNK)[:, :, 0:1], 0.0)
                link(nc.vector.memset(sc_tile[:, :, :], 0.0))
                keep_up(base + 3)
                dve.wait_ge(f_transposed, layer + 1)
                fv = lf.rearrange("p (h t) -> p h t", h=HEADS)
                for h in range(HEADS):
                    last = nc.vector.tensor_scalar(fv[:, h, :], banks(TRA, 2)[:, h * SEQ:(h + 1) * SEQ],
                                                   lb_rest[:, layer, h:h + 1], lb[:, layer, h:h + 1], ALU.mult, ALU.add)
                last.then_inc(f_taken, 1)
                dve.wait_ge(f_taken, layer + 1)
                link(nc.vector.tensor_scalar(kT, lf, -1.0, 1.0, ALU.mult, ALU.add))
                nc.vector.tensor_scalar_max(lf, lf, F_LEAST).then_inc(f_clamped, 1)
                keep_up(base + 5)
                dve.wait_ge(q_transposed, layer + 1)
                nc.vector.tensor_copy(qT, banks(GATE, 2)).then_inc(q_taken, 1)
                dve.wait_ge(logf_ready, layer + 1)
                link(nc.vector.tensor_tensor_scan(bT, reset, lf, 0.0, ALU.mult, ALU.add))
                exponents(0)
                exponents(1)
                keep_up(base + 7)
                level_step(layer, 0)
                level_step(layer, 1)
                keep_up(base + 8)
                dve.wait_ge(sw_squares, layer + 1)
                nc.vector.reduce_sum(head_sumsq[:, 0:20].rearrange("p (t h) -> p t h", t=TILES),
                                     sw_sq[:, :, :].rearrange("p t (h d) -> p t h d", d=HEAD_DIM), AX_X).then_inc(head_sums, 1)
                keep_up(base + 9)
                level_step(layer, 2)
                dve.wait_ge(head_rstds, 2 * layer + 1)
                for t in range(TILES):
                    v = qkv[:, t, 0:SW + KV].rearrange("p (h d) -> p h d", d=HEAD_DIM)
                    nc.vector.tensor_tensor(v, v, head_rstd[:, 10 * t:10 * t + 10].unsqueeze(2).to_broadcast([P, 10, HEAD_DIM]),
                                            ALU.mult).then_inc(qk_normed, 1)
                level_step(layer, 3)
                dve.wait_ge(qk_transposed, layer + 1)
                nc.vector.tensor_scalar(kbT, banks(0)[:, 0:SEQ], params[:, K_GAIN + layer:K_GAIN + layer + 1],
                                        None, ALU.mult).then_inc(qkT_ready, 1)
                nc.vector.tensor_scalar(qbT.rearrange("p h t -> p (h t)"), banks(2, 2),
                                        params[:, Q_GAIN + layer:Q_GAIN + layer + 1], HEAD_DIM ** -0.5,
                                        ALU.mult, ALU.mult).then_inc(qkT_ready, 1)
                keep_up(base + 10)
                level_step(layer, 4)
                keep_up(base + 11)
                level_step(layer, 5)
                keep_up(base + 12)
                softmax_max(layer, 0)
                level_step(layer, 6)
                keep_up(base + 13)
                level_step(layer, 7)
                attention_norm(layer, 0)
                keep_up(base + 14)
                level_step(layer, 8)
                softmax_max(layer, 1)
                keep_up(base + 15)
                dve.wait_ge(hgrn_squares, layer + 1)
                nc.vector.reduce_sum(head_sumsq[:, 0:TILES * HEADS], level_tile[0].rearrange("p (n d) -> p n d", d=P),
                                     AX_X).then_inc(head_sums, 1)
                dve.wait_ge(head_rstds, 2 * layer + 2)
                for t in range(TILES):
                    for h in range(HEADS):
                        cols = slice(h * P, (h + 1) * P)
                        last = nc.vector.scalar_tensor_tensor(silu_g[:, t, cols], banks(TRA + t)[:, cols],
                                                              head_rstd[:, t * HEADS + h:t * HEADS + h + 1],
                                                              silu_g[:, t, cols], ALU.mult, ALU.mult)
                last.then_inc(ya_ready, 1)
                attention_norm(layer, 1)
                softmax_max(layer, 2)
                keep_up(base + 16)
                keep_up(base + 17)
                g0 = HGRN_GAIN + layer * HEADS
                for h in range(HEADS):
                    dve.wait_ge(yaT_high, HEADS * layer + h // 2 * 2 + 2)
                    last = nc.vector.scalar_tensor_tensor(innerT[1][:, h, :], banks(GATE, 2)[:, h * SEQ:(h + 1) * SEQ],
                                                          params[:, g0 + h:g0 + h + 1], innerT[0][:, h, :].bitcast(F32),
                                                          ALU.mult, ALU.subtract)
                last.then_inc(yaT_ready, 1)
                keep_up(base + 18)
                attention_norm(layer, 2)
                keep_up(base + 19)
                for h in range(2):
                    dve.wait_ge(ybT_high, 2 * layer + h + 1)
                    last = low(hT, banks(GATE + h).rearrange("p (h t) -> p h t", h=2), (slice(None), slice(2 * h, 2 * h + 2)))
                last.then_inc(ybT_ready, 1)
                keep_up(base + PB_AT - 1)
                dve.wait_ge(branch_ready, 2 * layer + 1)
                dve.wait_ge(units_used, base + PB_AT)
                for t in range(TILES):
                    nc.vector.tensor_tensor(branch[:, t, 0:D], branch[:, t, 0:D], banks(2 * t, 2), ALU.mult)
                keep_up(base + PB_AT)
                dve.wait_ge(branch_ready, 2 * layer + 2)
                for t in range(TILES):
                    if t == 0:
                        dve.wait_ge(pb_tile0, layer + 1)
                    else:
                        dve.wait_ge(units_used, base + WO_AT)
                    link(nc.vector.tensor_tensor(branch[:, t, D:2 * D], branch[:, t, D:2 * D], banks(4 + 2 * t, 2), ALU.mult))
                    nc.vector.tensor_tensor(branch[:, t, 0:D], branch[:, t, 0:D], branch[:, t, D:2 * D],
                                            ALU.add).then_inc(merged_ready, 1)
                keep_up(base + WO_AT - 1)
                for g in range(4):
                    dve.wait_ge(mergedT_high, 4 * layer + g + 1)
                    low(hT, banks(g).rearrange("p (k t) -> p k t", k=2),
                        (slice(None), slice(2 * g, 2 * g + 2))).then_inc(mergedT_ready, 1)
                keep_up(base + WO_AT + GATE_UNITS - 1)
                add_to_x(4, 3 * layer + 1, base + WO_AT + GATE_UNITS)

            def add_to_x(bank, n, used):
                dve.wait_ge(out_tile0, n)
                nc.vector.tensor_tensor(x[:, 0, :], x[:, 0, :], banks(bank, 2), ALU.add).then_inc(x_updated, 1)
                dve.wait_ge(units_used, used)
                nc.vector.tensor_tensor(x[:, 1, :], x[:, 1, :], banks(bank + 2, 2), ALU.add).then_inc(x_updated, 1)

            def dense():
                dve.wait_ge(rstd_ready, 2)
                for s in range(STEPS):
                    keep_up(DENSE0 + item_up(s) + G_UNITS - 1)
                    dve.wait_ge(units_used, DENSE0 + item_up(s) + G_UNITS)
                    for t in range(TILES):
                        dve.wait_ge(silu_done, TILES * s + t + 1)
                        nc.vector.scalar_tensor_tensor(act[t], banks(6 + t), rstd[:, t:t + 1], act[t],
                                                       ALU.mult, ALU.mult).then_inc(act_ready, 1)
                    keep_up(DENSE0 + (item_down(s - 1) + D_UNITS if s else item_up(s) + G_UNITS) - 1)
                    for t in range(TILES):
                        dve.wait_ge(actT_high, TILES * s + t + 1)
                        low(innerT, banks(6 + t).rearrange("p (k t) -> p k t", k=4),
                            (slice(None), slice(None), slice(t * P, (t + 1) * P))).then_inc(actT_ready, 1)
                keep_up(PLE0 - 1)
                add_to_x(0, 2, PLE0)

            def route():
                e2 = [P, TILES, EXPERTS, EXPERTS]
                dve.wait_ge(logits_done, 1)
                dve.wait_ge(rstd_ready, 5)
                for t in range(TILES):
                    last = nc.vector.tensor_scalar(logits[:, t, :], banks(GATE + t)[:, 0:EXPERTS], rstd[:, t:t + 1], None, ALU.mult)
                link(last)
                for t in range(TILES):
                    last = nc.vector.scalar_tensor_tensor(logits[:, t, :], banks(GATE + t)[:, EXPERTS:2 * EXPERTS], rstd[:, t:t + 1],
                                                          logits[:, t, :], ALU.mult, ALU.add)
                link(last)
                other = logits[:, :, :].unsqueeze(2).to_broadcast(e2)
                own = logits[:, :, :].unsqueeze(3).to_broadcast(e2)
                link(nc.vector.reduce_max(top[:, :], logits[:, :, :], AX_X))
                nc.vector.tensor_tensor(gate_w[:, :, :], logits[:, :, :], top[:, :].unsqueeze(2).to_broadcast([P, TILES, EXPERTS]),
                                        ALU.subtract).then_inc(top_ready, 1)
                nc.vector.tensor_tensor(pair_a[:, :, :, :], other, own, ALU.is_gt)
                link(nc.vector.tensor_tensor(pair_b[:, :, :, :], other, own, ALU.is_equal))
                link(nc.vector.tensor_tensor(pair_b[:, :, :, :], pair_b[:, :, :, :],
                                             before[:, :, :].unsqueeze(1).to_broadcast(e2), ALU.mult))
                link(nc.vector.tensor_tensor(pair_a[:, :, :, :], pair_a[:, :, :, :], pair_b[:, :, :, :], ALU.add))
                link(nc.vector.reduce_sum(rank[:, :, :], pair_a[:, :, :, :], AX_X))
                nc.vector.tensor_scalar(chosen[:, :, :], rank[:, :, :], TOP_K - 0.5, None, ALU.is_lt).then_inc(chosen_ready, 1)
                dve.wait_ge(places_done, 1)
                place_ps = banks(TRA)[:, 0:TILES * EXPERTS].rearrange("p (t e) -> p t e", t=TILES)
                count_ps = banks(TRA)[:, TILES * EXPERTS:(TILES + 1) * EXPERTS]
                link(nc.vector.scalar_tensor_tensor(place[:, :, :], place_ps, 1.0, chosen[:, :, :], ALU.add, ALU.mult))
                link(nc.vector.tensor_scalar(item_place[:, :, 0:EXPERTS], place[:, :, :], -1.0, None, ALU.add))
                make_picks(slice(0, 1))
                dve.wait_ge(route_exps, 1)
                link(nc.vector.tensor_tensor(gate_w[:, :, :], gate_w[:, :, :], chosen[:, :, :], ALU.mult))
                link(nc.vector.reduce_sum(top[:, :], gate_w[:, :, :], AX_X))
                link(nc.vector.reciprocal(top[:, :], top[:, :]))
                link(nc.vector.tensor_tensor(gate_w[:, :, :], gate_w[:, :, :],
                                             top[:, :].unsqueeze(2).to_broadcast([P, TILES, EXPERTS]), ALU.mult))
                link(nc.vector.tensor_scalar(over[:, :], count_ps, P + 0.5, None, ALU.is_gt))
                pa1 = pair_a[:, 0, :, :]
                link(nc.vector.tensor_tensor(pa1, over[:, :].unsqueeze(1).to_broadcast([P, EXPERTS, EXPERTS]), before[:, :, :], ALU.mult))
                link(nc.vector.reduce_sum(over_before[:, :], pa1, AX_X))
                for r in range(EXTRA):
                    last = nc.vector.scalar_tensor_tensor(extra_of[:, r, :], over_before[:, :], float(r), over[:, :],
                                                          ALU.is_equal, ALU.mult)
                link(last)
                link(nc.vector.reduce_sum(n_items[:, :], over[:, :], AX_X))
                nc.vector.tensor_scalar(n_items_i[:, :], n_items[:, :], float(EXPERTS), None, ALU.add)
                pairs = [P, TILES, EXTRA, EXPERTS]
                extra = extra_of[:, :, :].unsqueeze(1).to_broadcast(pairs)
                link(nc.vector.tensor_tensor(pair_a[:, :, 0:EXTRA, :], place[:, :, :].unsqueeze(2).to_broadcast(pairs), extra, ALU.mult))
                nc.vector.memset(item_place[:, :, ITEMS - 1:ITEMS], -1.0)
                nc.vector.memset(item_gate_w[:, :, ITEMS - 1:ITEMS], 0.0)
                link(nc.vector.tensor_tensor(pair_b[:, :, 0:EXTRA, :], gate_w[:, :, :].unsqueeze(2).to_broadcast(pairs), extra, ALU.mult))
                link(nc.vector.reduce_sum(item_place[:, :, EXPERTS:ITEMS - 1], pair_a[:, :, 0:EXTRA, :], AX_X))
                nc.vector.reduce_sum(item_gate_w[:, :, EXPERTS:ITEMS - 1], pair_b[:, :, 0:EXTRA, :], AX_X)
                nc.vector.tensor_scalar(item_place[:, :, EXPERTS:ITEMS - 1], item_place[:, :, EXPERTS:ITEMS - 1],
                                        -1.0 - P, None, ALU.add)
                nc.vector.tensor_copy(item_gate_w[:, :, 0:EXPERTS], gate_w[:, :, :])
                nc.vector.memset(item_expert[:, :], 0.0).then_inc(item_added[1], 1)
                link(nc.vector.tensor_tensor(pair_a[:, 0, 0:EXTRA, :], extra_of[:, :, :],
                                             column[:, 0:EXPERTS].unsqueeze(1).to_broadcast([P, EXTRA, EXPERTS]), ALU.mult))
                nc.vector.tensor_copy(item_expert[:, 0:EXPERTS], column[:, 0:EXPERTS])
                link(nc.vector.reduce_sum(item_expert[:, EXPERTS:ITEMS - 1], pair_a[:, 0, 0:EXTRA, :], AX_X))
                nc.vector.tensor_copy(item_expert_i[:, :], item_expert[:, :]).then_inc(routed, 1)
                dve.wait_ge(routed, 1)

            def make_picks(item):
                for t in range(TILES):
                    last = nc.vector.tensor_scalar(pick[:, t, :], column[:, :], item_place[:, t, item], None, ALU.is_equal)
                last.then_inc(picks_ready, 1)

            def make_pick_gates(item):
                for t in range(TILES):
                    last = nc.vector.tensor_scalar(pick_gate[:, t, :], column[:, :], item_place[:, t, item],
                                                   item_gate_w[:, t, item], ALU.is_equal, ALU.mult)
                last.then_inc(pick_gates_ready, 1)

            def gathered_low(count):
                g0 = FFN_GAIN + KD
                for k in range(KD):
                    dve.wait_ge(gatheredT_high, (count - 1) * KD + k // 4 * 4 + 4)
                    last = nc.vector.scalar_tensor_tensor(hT[1][:, k, 0:P], banks(GATE, 2)[:, k * P:(k + 1) * P],
                                                          params[:, g0 + k:g0 + k + 1], hT[0][:, k, 0:P].bitcast(F32),
                                                          ALU.mult, ALU.subtract)
                    if k % 4 == 3:
                        last.then_inc(gatheredT_ready, 1)

            def experts():
                route()
                gathered_low(1)
                make_pick_gates(slice(0, 1))
                keep_up(MOE - 1)
                count = dve.value_load(n_items_i[0:1, 0:1], min_val=EXPERTS, max_val=EXPERTS + EXTRA)
                with dve.Fori(0, count) as t:
                    def actT_low_part(s):
                        dve.wait_ge(item_actT_high, t * STEPS + s + 1)
                        low(innerT, banks(TRA).rearrange("p (k t) -> p k t", k=4),
                            (slice(None), slice(None), slice(0, P))).then_inc(item_actT, 1)

                    for s in range(STEPS):
                        keep_up(MOE + item_gate(s) + G_UNITS, t)
                        if s == 0:
                            dve.wait_ge(pick_transposed, t + 1)
                            nc.vector.tensor_copy(spread, banks(TRB)[:, 0:SEQ]).then_inc(spread_ready, 1)
                        else:
                            actT_low_part(s - 1)
                        keep_up(MOE + item_up(s) + G_UNITS - (s > 0), t)
                        dve.wait_ge(units_used, t * PER_ITEM + MOE + item_up(s) + G_UNITS)
                        dve.wait_ge(item_silu, t * STEPS + s + 1)
                        nc.vector.tensor_tensor(act[s % 2], act[s % 2], banks(UP), ALU.mult).then_inc(item_act, 1)
                        if s == 0:
                            make_picks(bass.ds(t + 1, 1))
                            make_pick_gates(bass.ds(t + 1, 1))
                        else:
                            keep_up(MOE + item_down(s - 1) + D_UNITS - (s == STEPS - 1), t)
                    actT_low_part(STEPS - 1)
                    gathered_low(t + 2)
                    keep_up(MOE + PER_ITEM - 1, t)
                    for half in range(2):
                        dve.wait_ge(item_combined, t * 2 + half + 1)
                        for n in range(TILES):
                            xv = x[:, n, half * BANK:(half + 1) * BANK]
                            last = nc.vector.tensor_tensor(xv, xv, banks((2 if n == 0 else TRA) + half), ALU.add)
                        last.then_inc(item_added[half], 1)
                split[0] -= PER_ITEM
                return count

            def split_p(layer):
                dve.wait_ge(pT_high, layer + 1)
                low(inner, banks(P_BANK[layer]), (slice(None), slice(0, PLE * TILES))).then_inc(pT_ready, 1)

            def embedding(layer, items=0):
                base, end = (PLE0, None) if layer == 0 else (MOE, END)
                norm_low(3 * layer + 2, PLE_GAIN + layer * KD)
                keep_up(base, items, end)
                if layer == 0:
                    split_p(0)
                keep_up(base + GATE_UNITS - 1, items, end)
                for t in range(TILES):
                    if layer == 0 and t == 0:
                        dve.wait_ge(out_tile0, 3)
                    elif layer == 0:
                        dve.wait_ge(units_used, base + GATE_UNITS + 1)
                    dve.wait_ge(ple_gate_ready, TILES * layer + t + 1)
                    up = ple_up[:, t, :] if layer else banks(4 + 2 * t, 2)
                    link(nc.vector.tensor_tensor(ple_gate[:, t, :], ple_gate[:, t, :], up, ALU.mult))
                    nc.vector.tensor_tensor(x[:, t, :], x[:, t, :], ple_gate[:, t, :], ALU.add).then_inc(x_updated, 1)

            first_constants()
            keep_up(MIX0 + 1 - SLOTS)
            norm_low(0, MIX_GAIN)
            keep_up(MIX0)
            constants()
            mixer(0)
            norm_low(1, FFN_GAIN)
            keep_up(DENSE0)
            dense()
            embedding(0)
            norm_low(3, MIX_GAIN + KD)
            keep_up(MIX1)
            mixer(1)
            norm_low(4, FFN_GAIN + KD)
            split_p(1)
            keep_up(UP1)
            embedding(1, experts())

        @block.tensor
        def _(pe):
            def products(o, x_parts, x_cols, n, width, k, cols, first, last, items=0):
                parts = [a[:, n % SLOTS, :].rearrange("p (k n) -> p k n", n=width)[:, k, cols] for a in (w_hi, w_lo)]
                if k == 0:
                    pe.wait_ge(low_ready, n + 1 + items * PER_ITEM)
                nc.tensor.matmul(o, x_parts[0][x_cols], parts[0], start=first, stop=False)
                nc.tensor.matmul(o, x_parts[0][x_cols], parts[1], start=False, stop=False)
                return nc.tensor.matmul(o, x_parts[1][x_cols], parts[0], start=False, stop=last)

            def mm(o, lhsT, rhs, start, stop):
                return nc.tensor.matmul(o, lhsT, rhs, start=start, stop=stop)

            def transpose_tokens(src, bank, done, ready, ready_at, ready_step=1):
                for t in range(TILES):
                    pe.wait_ge(ready, ready_at + (t + 1) * ready_step)
                    for k in range(KD):
                        last = nc.tensor.transpose(banks(bank + k // 2)[:, k % 2 * SEQ + t * P:k % 2 * SEQ + (t + 1) * P],
                                                   src[:, t, k * P:(k + 1) * P], ident[:, :])
                        if t and k % 2:
                            last.then_inc(done, 1)

            def columns(k, t):
                return (slice(None), k, slice(t * P, (t + 1) * P))

            def flip_p(layer):
                pe.wait_ge(p_loaded, 16 * (layer + 1))
                for k in range(PLE // P):
                    for t in range(TILES):
                        last = nc.tensor.transpose(banks(P_BANK[layer])[:, k * SEQ + t * P:k * SEQ + (t + 1) * P],
                                                   p_tok[:, t, k * P:(k + 1) * P], ident[:, :])
                last.then_inc(p_transposed, 1)

            pT = [a[:, :].rearrange("p (k t) -> p k t", k=4) for a in inner]

            def wide_unit(base, u, n_units, x_parts, bank0, items=0, ready=None, ready_at=0, tile0_done=None):
                order = [(kk, t) for kk in range(2) for t in range(TILES)]
                if tile0_done is not None:
                    order = [(kk, t) for t in range(TILES) for kk in range(2)]
                if ready is not None:
                    pe.wait_ge(ready, ready_at + u + 1)
                for kk, t in order:
                    k = 2 * u + kk
                    for half in range(2):
                        last = products(banks(bank0 + 2 * t + half), x_parts, columns(k, t), base + u, D, kk,
                                        slice(half * BANK, (half + 1) * BANK), k == 0, k == 2 * n_units - 1, items)
                    if tile0_done is not None and (kk, t) == (1, 0):
                        last.then_inc(tile0_done, 1)
                last.then_inc(units_used, 1)

            def column_unit(n0, u, width, bank0, norm=None):
                per = UNIT // width
                for k in range(u * per, (u + 1) * per):
                    if norm is not None and k % 2 == 0:
                        pe.wait_ge(hT_ready, 4 * norm + k // 2 + 1)
                    for t in range(TILES):
                        last = products(banks(bank0 + t)[:, 0:width], hT, columns(k, t), n0 + u, width, k % per,
                                        slice(0, width), k == 0, k == KD - 1)
                last.then_inc(units_used, 1)

            def project(layer, c, u):
                if u == 0 and c >= 2:
                    pe.wait_ge(proj_taken, layer * OUTS + TILES * (c - 1 if c <= GATES else c))
                column_unit(MIX_AT[layer] + COLUMN_UNIT[c], u, IN_COLUMNS[c][1], COLUMN_BANK[c], 3 * layer if c == 0 else None)

            def projects(layer, c):
                for u in range(COLUMN_UNIT[c + 1] - COLUMN_UNIT[c]):
                    project(layer, c, u)

            def level_product(layer, g):
                b = GATE if g % 2 == 0 else TRA
                if g >= 2:
                    pe.wait_ge(level_taken, layer * (LEVEL_COUNT + 1) + g - 1)
                if g == 0:
                    pe.wait_ge(q_taken, layer + 1)
                    left, right = kT, qT
                else:
                    pe.wait_ge(level_ready, layer * LEVEL_COUNT + g)
                    left = right = level_tile[(g - 1) % 2]
                if g > 0 and LEVEL_HALF[g - 1] > CHUNK:
                    for h in range(HEADS):
                        last = mm(banks(b)[:, h * P:(h + 1) * P], left[:, h * SEQ:h * SEQ + P],
                                  right[:, h * SEQ + P:(h + 1) * SEQ], True, True)
                else:
                    for n in range(HEADS * TILES):
                        last = mm(banks(b, 2)[:, n * P:(n + 1) * P], left[:, n * P:(n + 1) * P],
                                  right[:, n * P:(n + 1) * P], True, True)
                last.then_inc(level_scores, 1)

            def flip_heads(src, b, done):
                for h in range(HEADS):
                    for t in range(TILES):
                        last = nc.tensor.transpose(banks(b, 2)[:, h * SEQ + t * P:h * SEQ + (t + 1) * P],
                                                   src[:, t, h * P:(h + 1) * P], ident[:, :])
                last.then_inc(done, 1)

            def attention_scores(layer, a):
                t, h0, heads = TASKS[a]
                keys = (t + 1) * P
                for h in range(h0, h0 + heads):
                    kv0 = (h // 4) * HEAD_DIM
                    last = mm(banks(2, 2)[:, (h - h0) * keys:(h - h0 + 1) * keys],
                              qbT[kv0:kv0 + HEAD_DIM, h % 4, t * P:(t + 1) * P], kbT[kv0:kv0 + HEAD_DIM, 0:keys], True, True)
                last.then_inc(sw_scores, 1)

            def flip_probs(layer, a):
                t, _, heads = TASKS[a]
                pe.wait_ge(sw_probs, len(TASKS) * layer + a + 1)
                keys = (t + 1) * P
                for kb in range(t + 1):
                    for h in range(heads):
                        last = nc.tensor.transpose(banks(2, 2)[:, (kb * heads + h) * P:(kb * heads + h + 1) * P],
                                                   sw_s[:, h * keys + kb * P:h * keys + (kb + 1) * P], ident[:, :])
                last.then_inc(sw_probs_transposed, 1)

            def attention_out(layer, a):
                t, h0, heads = TASKS[a]
                pe.wait_ge(sw_pT_ready, len(TASKS) * layer + a + 1)
                for h in range(heads):
                    v0 = SW + KV + ((h0 + h) // 4) * HEAD_DIM
                    for kb in range(t + 1):
                        last = mm(banks(OUT_BANK[a])[:, h * HEAD_DIM:(h + 1) * HEAD_DIM],
                                  sw_pT[:, (kb * heads + h) * P:(kb * heads + h + 1) * P],
                                  qkv[:, kb, v0:v0 + HEAD_DIM], kb == 0, kb == t)
                last.then_inc(sw_out, 1)

            def hgrn_output(layer):
                pe.wait_ge(level_taken, (layer + 1) * (LEVEL_COUNT + 1))
                for h in range(HEADS):
                    last = mm(banks(TRA)[:, h * P:(h + 1) * P], sc_tile[:, 2 * h, :], i_tok[:, 0, h * P:(h + 1) * P], True, True)
                last.then_inc(hgrn_out, 1)
                for h in range(HEADS):
                    mm(banks(TRB)[:, h * P:(h + 1) * P], sc_cross[:, h, :], i_tok[:, 0, h * P:(h + 1) * P], True, False)
                    last = mm(banks(TRB)[:, h * P:(h + 1) * P], sc_tile[:, 2 * h + 1, :], i_tok[:, 1, h * P:(h + 1) * P], False, True)
                last.then_inc(hgrn_out, 1)

            def mixer(layer):
                projects(layer, F)
                projects(layer, Q)
                pe.wait_ge(proj_taken, layer * OUTS + TILES * (F + 1))
                flip_heads(f_tok, TRA, f_transposed)
                projects(layer, G)
                pe.wait_ge(proj_taken, layer * OUTS + TILES * (Q + 1))
                flip_heads(q_tok, GATE, q_transposed)
                projects(layer, QA)
                level_product(layer, 0)
                projects(layer, KVA)
                level_product(layer, 1)
                project(layer, I, 0)
                level_product(layer, 2)
                project(layer, I, 1)
                level_product(layer, 3)
                pe.wait_ge(qk_normed, TILES * (layer + 1))
                pe.wait_ge(proj_taken, layer * OUTS + TILES * (I + 1))
                for t in range(TILES):
                    nc.tensor.transpose(banks(0)[:, t * P:(t + 1) * P], qkv[:, t, SW:SW + KV], ident[:, :])
                    for h in range(4):
                        last = nc.tensor.transpose(banks(2, 2)[:, h * SEQ + t * P:h * SEQ + (t + 1) * P],
                                                   qkv[:, t, h * P:(h + 1) * P], ident[:, :])
                last.then_inc(qk_transposed, 1)
                level_product(layer, 4)
                pe.wait_ge(qkT_ready, 2 * layer + 1)
                project(layer, GATES, 0)
                pe.wait_ge(qkT_ready, 2 * layer + 2)
                level_product(layer, 5)
                project(layer, GATES, 1)
                attention_scores(layer, 0)
                level_product(layer, 6)
                project(layer, GATES + 1, 0)
                level_product(layer, 7)
                flip_probs(layer, 0)
                project(layer, GATES + 1, 1)
                attention_out(layer, 0)
                level_product(layer, 8)
                pe.wait_ge(yb_ready, len(TASKS) * layer + 1)
                attention_scores(layer, 1)
                project(layer, GATES + 2, 0)
                hgrn_output(layer)
                flip_probs(layer, 1)
                project(layer, GATES + 2, 1)
                attention_out(layer, 1)
                pe.wait_ge(yb_ready, len(TASKS) * layer + 2)
                attention_scores(layer, 2)
                project(layer, GATES + 3, 0)
                pe.wait_ge(ya_ready, layer + 1)
                flip_heads(silu_g, GATE, ya_transposed)
                flip_probs(layer, 2)
                project(layer, GATES + 3, 1)
                attention_out(layer, 2)
                base = MIX_AT[layer]
                pe.wait_ge(yaT_ready, layer + 1)
                pe.wait_ge(proj_taken, (layer + 1) * OUTS)
                wide_unit(base + PA_AT, 0, 2, innerT, 0)
                pe.wait_ge(yb_ready, len(TASKS) * (layer + 1))
                for k in range(4):
                    for t in range(TILES):
                        last = nc.tensor.transpose(banks(GATE, 2)[:, k * SEQ + t * P:k * SEQ + (t + 1) * P],
                                                   qkv[:, t, k * P:(k + 1) * P], ident[:, :])
                    if k % 2:
                        last.then_inc(yb_transposed, 1)
                wide_unit(base + PA_AT, 1, 2, innerT, 0)
                pe.wait_ge(ybT_ready, layer + 1)
                for t in range(TILES):
                    for k in range(4):
                        for half in range(2):
                            last = products(banks(4 + 2 * t + half), hT, columns(k, t), base + PB_AT + k // 2, D, k % 2,
                                            slice(half * BANK, (half + 1) * BANK), k == 0, k == 3)
                    if t == 0:
                        last.then_inc(pb_tile0, 1)
                last.then_inc(units_used, 2)
                transpose_tokens(branch, 0, merged_transposed, merged_ready, TILES * layer)
                for u in range(GATE_UNITS):
                    wide_unit(base + WO_AT, u, GATE_UNITS, hT, 4, ready=mergedT_ready, ready_at=4 * layer,
                              tile0_done=out_tile0 if u == GATE_UNITS - 1 else None)

            def dense():
                def down(s):
                    for u in range(D_UNITS):
                        final = s == STEPS - 1 and u == D_UNITS - 1
                        order = [(kk, t) for kk in range(2) for t in range(TILES)]
                        if final:
                            order = [(kk, t) for t in range(TILES) for kk in range(2)]
                        for kk, t in order:
                            k = 2 * u + kk
                            for half in range(2):
                                last = products(banks(2 * t + half), innerT, columns(k, t), DENSE0 + item_down(s) + u, D,
                                                kk, slice(half * BANK, (half + 1) * BANK), s == 0 and k == 0,
                                                s == STEPS - 1 and k == 3)
                            if final and (kk, t) == (1, 0):
                                last.then_inc(out_tile0, 1)
                        last.then_inc(units_used, 1)

                for s in range(STEPS):
                    if s:
                        pe.wait_ge(silu_done, TILES * s)
                    for u in range(G_UNITS):
                        column_unit(DENSE0 + item_gate(s), u, BANK, 4, 1 if s == 0 else None)
                    if s:
                        pe.wait_ge(actT_ready, TILES * s)
                    for u in range(G_UNITS):
                        column_unit(DENSE0 + item_up(s), u, BANK, 6)
                    if s:
                        down(s - 1)
                    for t in range(TILES):
                        pe.wait_ge(act_ready, TILES * s + t + 1)
                        for k in range(4):
                            last = nc.tensor.transpose(banks(6 + t)[:, k * P:(k + 1) * P], act[t][:, k * P:(k + 1) * P], ident[:, :])
                        last.then_inc(act_transposed, 1)
                pe.wait_ge(actT_ready, TILES * STEPS)
                down(STEPS - 1)

            def ple_up_tile(t):
                for k in range(PLE // P):
                    for half in range(2):
                        last = products(banks(2 * t + half), pT, columns(k, t), UP1, D, k, slice(half * BANK, (half + 1) * BANK),
                                        k == 0, k == PLE // P - 1)
                last.then_inc(ple_up_tile0 if t == 0 else units_used, 1)

            def route():
                flip_p(1)
                for k in range(KD):
                    if k % 2 == 0:
                        pe.wait_ge(hT_ready, 16 + k // 2 + 1)
                    for t in range(TILES):
                        mm(banks(GATE + t)[:, 0:2 * EXPERTS], hT[0][columns(k, t)], router_parts[:, k, :, :], k == 0, False)
                        last = mm(banks(GATE + t)[:, 0:EXPERTS], hT[1][columns(k, t)], router_parts[:, k, 0, :], False, k == KD - 1)
                last.then_inc(logits_done, 1)
                pe.wait_ge(pT_ready, 2)
                ple_up_tile(0)
                pe.wait_ge(chosen_ready, 1)
                b = banks(TRA)
                mm(b[:, 0:EXPERTS], later[:, :], chosen[:, 0, :], True, True)
                mm(b[:, EXPERTS:2 * EXPERTS], ones[:, :], chosen[:, 0, :], True, False)
                mm(b[:, EXPERTS:2 * EXPERTS], later[:, :], chosen[:, 1, :], False, True)
                mm(b[:, 2 * EXPERTS:3 * EXPERTS], ones[:, :], chosen[:, 0, :], True, False)
                mm(b[:, 2 * EXPERTS:3 * EXPERTS], ones[:, :], chosen[:, 1, :], False, True).then_inc(places_done, 1)

            def gather(count):
                pe.wait_ge(picks_ready, count)
                for k in range(KD):
                    for t in range(TILES):
                        last = mm(banks(GATE, 2)[:, k * P:(k + 1) * P], normed[:, t, k * P:(k + 1) * P], pick[:, t, :],
                                  t == 0, t == TILES - 1)
                    if k % 4 == 3:
                        last.then_inc(gathered, 1)

            def experts():
                route()
                ple_up_tile(1)
                pe.wait_ge(normed_ready, TILES)
                gather(1)
                pe.wait_ge(ple_up_taken, TILES)
                pe.wait_ge(routed, 1)
                count = pe.value_load(n_items_i[0:1, 0:1], min_val=EXPERTS, max_val=EXPERTS + EXTRA)
                with pe.Fori(0, count) as t:
                    def step_product(first_unit, bank, first=False):
                        for k in range(KD):
                            if first and k % 4 == 0:
                                pe.wait_ge(gatheredT_ready, t * 2 + k // 4 + 1)
                            last = products(banks(bank), hT, columns(k, 0), MOE + first_unit + k // 4, BANK, k % 4,
                                            slice(0, BANK), k == 0, k == KD - 1, t)
                            if k % 4 == 3:
                                last.then_inc(units_used, 1)

                    def flip(s):
                        pe.wait_ge(item_act, t * STEPS + s + 1)
                        for k in range(4):
                            last = nc.tensor.transpose(banks(TRA)[:, k * P:(k + 1) * P], act[s % 2][:, k * P:(k + 1) * P],
                                                       ident[:, :])
                        last.then_inc(item_act_transposed, 1)

                    def down_tile(s, k, half):
                        return products(banks(half), innerT, columns(k, 0), MOE + item_down(s) + k // 2, D, k % 2,
                                        slice(half * BANK, (half + 1) * BANK), s == 0 and k == 0, s == STEPS - 1 and k == 3, t)

                    for s in range(STEPS):
                        if s:
                            pe.wait_ge(item_silu, t * STEPS + s)
                        step_product(item_gate(s), GATE, s == 0)
                        if s:
                            flip(s - 1)
                        else:
                            pe.wait_ge(item_added[1], t + 1)
                            pe.wait_ge(pick_gates_ready, t + 1)
                            for n in range(TILES):
                                last = nc.tensor.transpose(banks(TRB)[:, n * P:(n + 1) * P], pick_gate[:, n, :], ident[:, :])
                            last.then_inc(pick_transposed, 1)
                        step_product(item_up(s), UP)
                        if s:
                            pe.wait_ge(item_actT, t * STEPS + s)
                            for k in range(4):
                                for half in range(2):
                                    last = down_tile(s - 1, k, half)
                                if k % 2:
                                    last.then_inc(units_used, 1)
                    flip(STEPS - 1)
                    gather(t + 2)
                    pe.wait_ge(item_actT, t * STEPS + STEPS)
                    for k in range(2):
                        for half in range(2):
                            last = down_tile(STEPS - 1, k, half)
                    last.then_inc(units_used, 1)
                    for half in range(2):
                        for k in range(2, 4):
                            last = down_tile(STEPS - 1, k, half)
                        if half == 0:
                            last.then_inc(item_y_done, 1)
                        else:
                            last.then_inc(units_used, 1)
                    pe.wait_ge(spread_ready, t + 1)
                    for half in range(2):
                        pe.wait_ge(item_y_taken, t * 2 + half + 1)
                        for n in range(TILES):
                            last = mm(banks((2 if n == 0 else TRA) + half), spread[:, n * P:(n + 1) * P],
                                      y_item[:, half * BANK:(half + 1) * BANK], True, True)
                        last.then_inc(item_combined, 1)
                return count

            def embedding(layer, count=0):
                n = 3 * layer + 2
                base = PLE0 if layer == 0 else MOE
                for u in range(GATE_UNITS):
                    wide_unit(base, u, GATE_UNITS, hT, 0, count, ready=hT_ready, ready_at=4 * n,
                              tile0_done=out_tile0 if layer and u == GATE_UNITS - 1 else None)
                    if layer == 0 and u == 0:
                        pe.wait_ge(hT_ready, 4 * n + 4)
                        flip_p(layer)
                if layer == 0:
                    pe.wait_ge(pT_ready, 1)
                    wide_unit(base + GATE_UNITS, 0, 1, pT, 4, tile0_done=out_tile0)

            pe.wait_ge(vector_constants, 1)
            pe.wait_ge(params_loaded, 16 * PARAM_DMAS)
            nc.tensor.transpose(banks(TRB)[:, 0:PARAM_ROWS], param_rows[0:PARAM_ROWS, :],
                                ident[0:PARAM_ROWS, 0:PARAM_ROWS]).then_inc(params_transposed, 1)
            transpose_tokens(x, 0, x_transposed, x_loaded, 0, 16)
            mixer(0)
            transpose_tokens(x, 0, x_transposed, x_updated, 0)
            dense()
            transpose_tokens(x, 4, x_transposed, x_updated, 2)
            embedding(0)
            pe.wait_ge(ple_gate_ready, TILES)
            transpose_tokens(x, 0, x_transposed, x_updated, 4)
            mixer(1)
            transpose_tokens(x, 0, x_transposed, x_updated, 6)
            count = experts()
            for k in range(KD):
                if k % 4 == 0:
                    pe.wait_ge(item_added[k // 4], count + k // 4)
                if k == 0:
                    pe.wait_ge(gatheredT_ready, count * 2 + 2)
                for t in range(TILES):
                    last = nc.tensor.transpose(banks(4 + k // 2)[:, k % 2 * SEQ + t * P:k % 2 * SEQ + (t + 1) * P],
                                               x[:, t, k * P:(k + 1) * P], ident[:, :])
                if k % 2:
                    last.then_inc(x_transposed, 1)
            embedding(1, count)


_INS = ["x", "p", "lb_logits", "g_mix", "w_in", "q_norm", "k_norm", "sinks", "hgrn_norm", "w_pa", "w_pb", "w_o",
        "g_ffn", "w_dense_gate", "w_dense_up", "w_dense_down", "w_router", "w_moe_gate", "w_moe_up", "w_moe_down",
        "g_ple", "w_ple_gate", "w_ple_up"]


def kernel(**inputs):
    import numpy as _np
    import concourse.bacc as _bacc
    from concourse import mybir as _mybir
    from concourse.bass_utils import run_bass_kernel_spmd as _run

    nc = _bacc.Bacc("TRN2", target_bir_lowering=False, num_devices=1)
    arrays, args = {}, []
    for name in _INS:
        a = _np.ascontiguousarray(inputs[name])
        arrays[f"in_{name}"] = a
        args.append(nc.dram_tensor(f"in_{name}", a.shape, _mybir.dt.from_np(a.dtype), kind="ExternalInput").ap())
    shape = inputs["x"].shape
    args.append(nc.dram_tensor("trunk_out", shape, _mybir.dt.float32, kind="ExternalOutput").ap())
    build_trunk(nc, *args)
    r = _run(nc, [arrays], core_ids=[0])
    return r.results[0]["trunk_out"]
```
